# Optimizing a Trainium2 kernel written in Bass

```python
import jax, jax.numpy as jnp
from jax import lax
import numpy as np

D_MODEL = 2048
BATCH = 1
SEQ = 1024
DEPTH = 1
DEC_BATCH = 8
DEC_SEQ = 8
PAST_LEN = 8192
PAGE_SIZE = 128

HEAD = 64
D_R = D_MODEL // 2
H_R = D_R // HEAD
R_W = 64
R_A = 64
D_SHIFT = 3 * D_R + R_W + R_A
CHUNK = 128
D_G = D_MODEL // 2
N_GROUPS = 8
GW = D_G // N_GROUPS
N_IN = D_SHIFT + D_R + 3 * D_G + 2 * D_MODEL
RMS_EPS = 1e-6
LN_EPS = 1e-5
GN_EPS = 64e-5

kernel_name = "rwkv7_chunk_sgu_gated_hybrid_step"

def rms_norm(x, g):
    xf = x.astype(jnp.float32)
    y = xf * lax.rsqrt(jnp.mean(xf * xf, axis=-1, keepdims=True) + RMS_EPS)
    return (y * g).astype(x.dtype)

def layer_norm(x, g, b):
    xf = x.astype(jnp.float32)
    mu = jnp.mean(xf, axis=-1, keepdims=True)
    var = jnp.mean(jnp.square(xf - mu), axis=-1, keepdims=True)
    return ((xf - mu) * lax.rsqrt(var + LN_EPS) * g + b).astype(x.dtype)

def wkv7_scan(S0, r, w, k, v, a, b):
    def step(S, inp):
        r_t, w_t, k_t, v_t, a_t, b_t = inp
        Sa = jnp.einsum('bhvk,bhk->bhv', S, a_t)
        S = S * w_t[:, :, None, :] + Sa[..., None] * b_t[:, :, None, :] + v_t[..., None] * k_t[:, :, None, :]
        y = jnp.einsum('bhvk,bhk->bhv', S, r_t)
        return S, y
    xs = tuple(jnp.swapaxes(t, 0, 1) for t in (r, w, k, v, a, b))
    S, ys = lax.scan(step, S0, xs)
    return S, jnp.swapaxes(ys, 0, 1)

def chunk_spatial_mix(vn, sgu_w, sgu_b):
    Bn, T, _ = vn.shape
    L = CHUNK if T % CHUNK == 0 else T
    C = T // L
    vr = vn.reshape(Bn, C, L, N_GROUPS, GW)
    mask = jnp.tril(jnp.ones((L, L), vn.dtype))
    Wm = sgu_w[:, :L, :L] * mask
    s = jnp.einsum('gts,bcsgd->bctgd', Wm, vr) + jnp.transpose(sgu_b[:, :L])[None, None, :, :, None]
    return s.reshape(Bn, T, D_G)

def mixer_layer(h, shift_prev, S0, norm_g, w_in, shift_mu, w0, w2, a0, a2, k_k, k_a, r_k,
                lnx_g, lnx_b, sgu_ln_g, sgu_ln_b, sgu_w, sgu_b, w_proj_a, w_proj_b, w_out):
    Bn, T, _ = h.shape
    xn = rms_norm(h, norm_g)
    z = xn @ w_in
    zs = z[..., :D_SHIFT]
    zs_prev = jnp.concatenate([shift_prev.astype(z.dtype), zs[:, :-1]], axis=1)
    zs_mix = zs + (zs_prev - zs) * shift_mu
    new_shift = zs[:, -1:]
    r, k, v, wd, ad = jnp.split(zs_mix, [D_R, 2 * D_R, 3 * D_R, 3 * D_R + R_W], axis=-1)
    g_r, u, vg, g_g, gate_a, gate_b = jnp.split(
        z[..., D_SHIFT:], [D_R, D_R + D_G, D_R + 2 * D_G, D_R + 3 * D_G, D_R + 3 * D_G + D_MODEL], axis=-1)

    f32 = jnp.float32
    r, k, v, wd, ad = (t.astype(f32) for t in (r, k, v, wd, ad))
    w_log = -jax.nn.softplus(-(w0 + jnp.tanh(wd) @ w2)) - 0.5
    decay = jnp.exp(-jnp.exp(w_log))
    a_gate = jax.nn.sigmoid(a0 + ad @ a2)
    kk = (k * k_k).reshape(Bn, T, H_R, HEAD)
    kk = kk / jnp.maximum(jnp.linalg.norm(kk, axis=-1, keepdims=True), 1e-12)
    k = k * (1.0 + (a_gate - 1.0) * k_a)
    hs = lambda t: t.reshape(Bn, T, H_R, HEAD)
    rh, kh, vh, ah = hs(r), hs(k), hs(v), hs(a_gate)
    S, y = wkv7_scan(S0.astype(f32), rh, hs(decay), kh, vh, -kk, kk * ah)
    mu = jnp.mean(y, axis=-1, keepdims=True)
    var = jnp.mean(jnp.square(y - mu), axis=-1, keepdims=True)
    y = (y - mu) * lax.rsqrt(var + GN_EPS) * lnx_g.reshape(H_R, HEAD) + lnx_b.reshape(H_R, HEAD)
    y = y + jnp.sum(rh * kh * r_k, axis=-1, keepdims=True) * vh
    y = y.reshape(Bn, T, D_R).astype(h.dtype)
    ya = (y * jax.nn.silu(g_r)) @ w_proj_a

    vn = layer_norm(vg, sgu_ln_g, sgu_ln_b)
    s = chunk_spatial_mix(vn, sgu_w, sgu_b)
    yb = (u * s * jax.nn.silu(g_g)) @ w_proj_b

    m = jax.nn.sigmoid(gate_a) * ya + jax.nn.sigmoid(gate_b) * yb
    return h + m @ w_out, new_shift, S, vn

def setup_inputs(seed: int = 0) -> dict:
    key = jax.random.key(seed)
    ks = jax.random.split(key, 32)
    nrm = lambda k, shape, s: jax.random.normal(k, shape, jnp.float32) * s
    return {
        "x_prompt": nrm(ks[0], (BATCH, SEQ, D_MODEL), 1.0),
        "x_sample": nrm(ks[1], (DEC_BATCH, DEC_SEQ, D_MODEL), 1.0),
        "state_wkv": nrm(ks[2], (DEPTH, DEC_BATCH, H_R, HEAD, HEAD), 0.3),
        "state_shift": nrm(ks[3], (DEPTH, DEC_BATCH, 1, D_SHIFT), 1.0),
        "norm_g": 1.0 + nrm(ks[4], (DEPTH, D_MODEL), 0.05),
        "w_in": nrm(ks[5], (DEPTH, D_MODEL, N_IN), D_MODEL ** -0.5),
        "shift_mu": jax.random.uniform(ks[6], (DEPTH, D_SHIFT), jnp.float32, 0.1, 0.9),
        "w0": nrm(ks[7], (DEPTH, D_R), 0.5),
        "w2": nrm(ks[8], (DEPTH, R_W, D_R), 0.5 * R_W ** -0.5),
        "a0": nrm(ks[9], (DEPTH, D_R), 0.1),
        "a2": nrm(ks[10], (DEPTH, R_A, D_R), R_A ** -0.5),
        "k_k": 0.85 + nrm(ks[11], (DEPTH, D_R), 0.05),
        "k_a": 1.0 + nrm(ks[12], (DEPTH, D_R), 0.05),
        "r_k": nrm(ks[13], (DEPTH, H_R, HEAD), 0.1),
        "lnx_g": 1.0 + nrm(ks[14], (DEPTH, D_R), 0.05),
        "lnx_b": nrm(ks[15], (DEPTH, D_R), 0.02),
        "sgu_ln_g": 1.0 + nrm(ks[16], (DEPTH, D_G), 0.05),
        "sgu_ln_b": nrm(ks[17], (DEPTH, D_G), 0.02),
        "sgu_w": nrm(ks[18], (DEPTH, N_GROUPS, CHUNK, CHUNK), CHUNK ** -0.5),
        "sgu_b": 1.0 + nrm(ks[19], (DEPTH, N_GROUPS, CHUNK), 0.1),
        "w_proj_a": nrm(ks[20], (DEPTH, D_R, D_MODEL), D_R ** -0.5),
        "w_proj_b": nrm(ks[21], (DEPTH, D_G, D_MODEL), D_G ** -0.5),
        "w_out": nrm(ks[22], (DEPTH, D_MODEL, D_MODEL), D_MODEL ** -0.5),
        "final_norm_g": 1.0 + nrm(ks[23], (D_MODEL,), 0.05),
    }

def reference(x_prompt, x_sample, state_wkv, state_shift, norm_g, w_in, shift_mu, w0, w2, a0, a2,
              k_k, k_a, r_k, lnx_g, lnx_b, sgu_ln_g, sgu_ln_b, sgu_w, sgu_b, w_proj_a, w_proj_b,
              w_out, final_norm_g):
    hp, hs = x_prompt, x_sample
    wkv_p, shift_p, wkv_s, shift_s, chunk_v_s = [], [], [], [], []
    shift0 = jnp.zeros((BATCH, 1, D_SHIFT), x_prompt.dtype)
    S0 = jnp.zeros((BATCH, H_R, HEAD, HEAD), jnp.float32)
    for l in range(DEPTH):
        lp = (norm_g[l], w_in[l], shift_mu[l], w0[l], w2[l], a0[l], a2[l], k_k[l], k_a[l], r_k[l],
              lnx_g[l], lnx_b[l], sgu_ln_g[l], sgu_ln_b[l], sgu_w[l], sgu_b[l],
              w_proj_a[l], w_proj_b[l], w_out[l])
        hp, sh_p, S_p, _ = mixer_layer(hp, shift0, S0, *lp)
        hs, sh_s, S_s, vn_s = mixer_layer(hs, state_shift[l], state_wkv[l], *lp)
        wkv_p.append(S_p)
        shift_p.append(sh_p)
        wkv_s.append(S_s.astype(state_wkv.dtype))
        shift_s.append(sh_s.astype(state_shift.dtype))
        chunk_v_s.append(vn_s)
    y_prompt = rms_norm(hp, final_norm_g)
    y_sample = rms_norm(hs, final_norm_g)
    return (y_prompt, y_sample, jnp.stack(wkv_p), jnp.stack(shift_p), jnp.stack(wkv_s),
            jnp.stack(shift_s), jnp.stack(chunk_v_s))


_drawn_inputs = setup_inputs


def setup_inputs(seed=0):
    import zlib

    import numpy as np

    out = dict(_drawn_inputs(seed))
    spreads = {}
    factors = {'k_k': 4.522, 'lnx_g': 3.905, 'lnx_b': 8.0, 'sgu_ln_b': 2.882}
    for name, (base, spread) in spreads.items():
        noise = np.random.default_rng([zlib.crc32(name.encode()), seed]).standard_normal(out[name].shape)
        drawn = base * np.exp(spread * noise) if base else spread * noise
        out[name] = __import__('jax').numpy.asarray(drawn.astype(out[name].dtype))
    for name, factor in factors.items():
        out[name] = (out[name] * factor).astype(out[name].dtype)
    return out
```

```python
from contextlib import ExitStack

import concourse.bass as bass
from concourse import mybir

P = 128
D_MODEL, D_R, D_G = 2048, 1024, 1024
KT = D_MODEL // P
KH = D_R // P
HEAD = 64
PAIRS = D_R // P
PROMPT, BATCH, STEPS = 1024, 8, 8
SAMPLE = BATCH * STEPS
TOK = PROMPT + SAMPLE
NCH = 364
TP = 3 * NCH
ZO = 4
ZW = ZO + TP
PAD = TP - TOK
CH = 64
NCHUNK = PROMPT // CH
Q = 128
T_R, T_K, T_V, T_LR, T_GR = 0, 8, 16, 24, 25
T_U, T_VG, T_GG, T_GA, T_GB, NTILE = 33, 41, 49, 57, 73, 89
N_SHIFT = 25
LEVELS = (2, 4, 8, 16, 32)
RMS_EPS, LN_EPS, GN_EPS = 1e-6, 1e-5, 64e-5
DECAY = 0.6065306597126334

F32, F32R = mybir.dt.float32, mybir.dt.float32r
ALU, ACT = mybir.AluOpType, mybir.ActivationFunctionType
MUL, ADD, SUB = ALU.mult, ALU.add, ALU.subtract


def tile_of(dram, i):
    if isinstance(i, int):
        return dram[i]
    return dram[bass.ds(i, 1)].rearrange("o p c -> (o p) c")


class Scope:

    def __init__(self, nc, stack):
        self.nc, self.stack, self.sems = nc, stack, []
        stack.callback(self.clear)

    def sb(self, name, shape, dt=F32):
        return self.stack.enter_context(self.nc.sbuf_tensor(name, shape, dt))

    def ps(self, name, shape):
        return self.stack.enter_context(self.nc.psum_tensor(name, shape, F32))

    def sem(self, name):
        self.sems.append(self.nc.alloc_semaphore(name))
        return self.sems[-1]

    def clear(self):
        self.nc.clear_and_free_semaphores(self.sems)
        self.nc.all_engine_barrier()


def pieces(ap):
    return ap.rearrange("p (c n) -> p c n", c=3)


class Gemm:

    def __init__(self, nc, sc, tag, wt, kts, xh, xl, koff):
        self.nc, self.wt, self.kts, self.xh, self.xl, self.koff = nc, wt, kts, xh, xl, koff
        self.raw = [sc.sb(f"{tag}_raw{s}", [P, kts * P]) for s in range(2)]
        self.wh = [sc.sb(f"{tag}_wh{s}", [P, kts * P], F32R) for s in range(2)]
        self.wl = [sc.sb(f"{tag}_wl{s}", [P, kts * P], F32R) for s in range(2)]
        self.acc = [sc.ps(f"{tag}_acc{s}", [P, 3, 512]) for s in range(2)]
        self.w_loaded = [sc.sem(f"{tag}_w_loaded{s}") for s in range(2)]
        self.hi_ready = [sc.sem(f"{tag}_hi_ready{s}") for s in range(2)]
        self.lo_ready = [sc.sem(f"{tag}_lo_ready{s}") for s in range(2)]
        self.group_done = [sc.sem(f"{tag}_group_done{s}") for s in range(2)]
        self.evacuated = [sc.sem(f"{tag}_evacuated{s}") for s in range(2)]
        self.x_ready = sc.sem(f"{tag}_x_ready")

    def load(self, sp, g, i, s):
        sp.wait_ge(self.lo_ready[s], i)
        sp.dma_start(self.raw[s][:, :], tile_of(self.wt, g)).then_inc(self.w_loaded[s], 16)

    def split(self, dve, i, s):
        dve.wait_ge(self.w_loaded[s], i * 16 + 16)
        dve.wait_ge(self.group_done[s], i)
        dve.tensor_copy(self.wh[s][:, :], self.raw[s][:, :]).then_inc(self.hi_ready[s], 1)
        dve.wait_ge(self.hi_ready[s], i + 1)
        dve.tensor_tensor(self.wl[s][:, :], self.raw[s][:, :], self.wh[s][:, :].bitcast(F32),
                          SUB).then_inc(self.lo_ready[s], 1)

    def products(self, pe, i, s):
        pe.wait_ge(self.lo_ready[s], i + 1)
        pe.wait_ge(self.evacuated[s], i)
        for k in range(self.kts):
            kx = k + self.koff[s]
            pe.wait_ge(self.x_ready, kx + 1)
            for w, x in ((self.wh, self.xh), (self.wh, self.xl), (self.wl, self.xh)):
                for c in range(3):
                    mm = pe.matmul(self.acc[s][:, c, 0:NCH], w[s][:, k * P:(k + 1) * P],
                                   x[:, kx, c * NCH:(c + 1) * NCH],
                                   start=(k == 0 and w is self.wh and x is self.xh),
                                   stop=(k == self.kts - 1 and w is self.wl))
        mm.then_inc(self.group_done[s], 1)

    def sums(self, s):
        return self.acc[s][:, :, 0:NCH]


def in_slots(engine, groups, body):
    for s in range(2):
        body(s, 0, s)
    with engine.Fori(1, groups // 2) as i:
        for s in range(2):
            body(i * 2 + s, i, s)
    if groups % 2:
        body(groups - 1, groups // 2, 0)


def phase_in(nc, xT, norm_g, wt, z):
    with ExitStack() as stack:
        sc = Scope(nc, stack)
        xh = sc.sb("in_xh", [P, KT, TP], F32R)
        xl = sc.sb("in_xl", [P, KT, TP], F32R)
        gm = Gemm(nc, sc, "in", wt, KT, xh, xl, (0, 0))
        stage = [sc.sb(f"in_stage{s}", [P, ZW]) for s in range(2)]
        xs = sc.sb("in_xs", [P, TP])
        g_sb = sc.sb("in_g", [P, KT])
        eps = sc.sb("in_eps", [P, 1])
        ones = sc.sb("in_ones", [P, P])
        sem_x = [sc.sem(f"in_x_loaded{n}") for n in range(2)]
        sem_g, const_ready = sc.sem("in_g_loaded"), sc.sem("in_const_ready")
        sq_ready, sq_summed = sc.sem("in_sq_ready"), sc.sem("in_sq_summed")
        ms_ready, rt_ready, rstd_ready = sc.sem("in_ms_ready"), sc.sem("in_rt_ready"), sc.sem("in_rstd_ready")
        xn_ready, xh_ready = sc.sem("in_xn_ready"), sc.sem("in_xh_ready")
        stored = [sc.sem(f"in_stored{s}") for s in range(2)]
        xbuf = [xs[:, :], stage[0][:, ZO:ZW]]
        sqb = stage[1][:, ZO:ZW]
        rstd = sc.sb("in_rstd", [P, TP])

        with nc.Block() as block:
            @block.sync
            def _(sp):
                sp.dma_start(g_sb[:, :], norm_g).then_inc(sem_g, 16)
                in_slots(sp, NTILE, lambda g, i, s: gm.load(sp, g, i, s))

            @block.gpsimd
            def _(pool):
                pool.memset(ones[:, :], 1.0 / D_MODEL).then_inc(const_ready, 1)
                pool.memset(eps[:, :], RMS_EPS).then_inc(const_ready, 1)
                pool.memset(stage[0][:, 0:ZO], 0.0).then_inc(const_ready, 1)
                pool.memset(stage[1][:, 0:ZO], 0.0).then_inc(const_ready, 1)
                for b in xbuf:
                    pool.memset(b[:, TOK:TP], 0.0).then_inc(const_ready, 1)
                for n in range(2 * KT):
                    if 2 <= n < KT:
                        pool.wait_ge(sq_ready, n - 1)
                    if n >= KT:
                        pool.wait_ge(sq_ready, min(n - 1, KT))
                    if n >= KT + 2:
                        pool.wait_ge(gm.x_ready, n - 1 - KT)
                    pool.dma_start(xbuf[n % 2][:, 0:TOK], xT[n % KT]).then_inc(sem_x[n % 2], 16)

            @block.scalar
            def _(act):
                act.wait_ge(const_ready, 6)
                for n in range(KT):
                    act.wait_ge(sem_x[n % 2], 16 * (n // 2 + 1))
                    act.wait_ge(sq_summed, n)
                    nc.scalar.activation(sqb, xbuf[n % 2], ACT.Square).then_inc(sq_ready, 1)
                act.wait_ge(sq_summed, KT)
                nc.scalar.activation(pieces(rstd[:, :]), gm.acc[0][:, :, 0:NCH], ACT.Sqrt,
                                     bias=eps[:, 0:1]).then_inc(rt_ready, 1)
                for n in range(KT):
                    act.wait_ge(xn_ready, n + 1)
                    nc.scalar.activation(xh[:, n, :], xbuf[n % 2], ACT.Copy).then_inc(xh_ready, 1)
                act.wait_ge(gm.x_ready, KT)

                def store(g, i, s):
                    act.wait_ge(gm.group_done[s], i + 1)
                    act.wait_ge(stored[s], i * 16)
                    nc.scalar.activation(pieces(stage[s][:, ZO:ZW]), gm.sums(s), ACT.Copy).then_inc(gm.evacuated[s], 1)
                    act.wait_ge(gm.evacuated[s], i + 1)
                    act.dma_start(tile_of(z, g), stage[s][:, :]).then_inc(stored[s], 16)

                in_slots(act, NTILE, store)
                act.wait_ge(stored[0], 16 * (NTILE - NTILE // 2))
                act.wait_ge(stored[1], 16 * (NTILE // 2))

            @block.vector
            def _(dve):
                dve.wait_ge(rt_ready, 1)
                dve.reciprocal(rstd[:, :], rstd[:, :]).then_inc(rstd_ready, 1)
                dve.wait_ge(rstd_ready, 1)
                dve.wait_ge(sem_g, 16)
                for n in range(KT):
                    x = xbuf[n % 2]
                    dve.wait_ge(sem_x[n % 2], 16 * (KT // 2 + n // 2 + 1))
                    if n >= 1:
                        dve.wait_ge(gm.x_ready, n)
                    dve.scalar_tensor_tensor(x[:, :], x[:, :], g_sb[:, n:n + 1], rstd[:, :], MUL, MUL).then_inc(xn_ready, 1)
                    dve.wait_ge(xn_ready, n + 1)
                    dve.wait_ge(xh_ready, n + 1)
                    dve.tensor_tensor(xl[:, n, :], x[:, :], xh[:, n, :].bitcast(F32), SUB).then_inc(gm.x_ready, 1)
                in_slots(dve, NTILE, lambda g, i, s: gm.split(dve, i, s))

            @block.tensor
            def _(pe):
                pe.wait_ge(const_ready, 1)
                for n in range(KT):
                    pe.wait_ge(sq_ready, n + 1)
                    for c in range(3):
                        mm = pe.matmul(gm.acc[0][:, c, 0:NCH], ones[:, :], sqb[:, c * NCH:(c + 1) * NCH],
                                       start=(n == 0), stop=(n == KT - 1))
                    mm.then_inc(sq_summed, 1)
                pe.wait_ge(rt_ready, 1)
                in_slots(pe, NTILE, lambda g, i, s: gm.products(pe, i, s))


def phase_rwkv(nc, z, lowrank, mu, par, shiftT, stateT, yT, shift_out, swkv_out, pwkv_out):
    with ExitStack() as stack:
        sc = Scope(nc, stack)
        sb, sem = sc.sb, sc.sem
        H2 = slice(0, HEAD), slice(HEAD, P)
        FOUR = slice(0, 4), slice(4, 8)

        zin = sb("zin", [P, N_SHIFT, CH + 1])
        gin = sb("gin", [P, PAIRS, CH])
        mix = sb("mix", [P, N_SHIFT, CH])
        r, k = mix[:, T_R:T_K, :], mix[:, T_K:T_V, :]
        v_pad = sb("v_pad", [P, PAIRS, 2 * CH])
        v = v_pad[:, :, CH:2 * CH]
        lr_w, lr_a = sb("lr_w", [P, CH]), sb("lr_a", [P, CH])
        big = lambda name: sb(name, [P, PAIRS, CH])
        sw, sa, cum, cum1 = big("sw"), big("sa"), big("cum"), big("cum1")
        ep, en, em = big("ep"), big("en"), big("em")
        kkr, sq, nrm, rn, kk = big("kkr"), big("sq"), big("nrm"), big("rn"), big("kk")
        t1, k2, rk, rkp, bsa, bonus = big("t1"), big("k2"), big("rk"), big("rkp"), big("bsa"), big("bonus")
        bk = sb("bk", [P, PAIRS, 2, CH])
        bkw = sb("bkw", [P, PAIRS, 2, CH])
        ar = sb("ar", [P, PAIRS, 2, 2, CH])
        m = sb("m", [P, PAIRS, 2, 2, CH])
        at = sb("at", [P, PAIRS, P])
        t, tt = sb("t", [P, PAIRS, P]), sb("tt", [P, PAIRS, P])
        pl = [sb(f"p{b}", [P, PAIRS, P]) for b in LEVELS]
        bkt = sb("bkt", [P, PAIRS, P])
        zz = sb("zz", [P, PAIRS, P])
        xst = sb("xst", [P, PAIRS, HEAD])
        st, stw = sb("st", [P, PAIRS, HEAD]), sb("stw", [P, PAIRS, HEAD])
        y, yc, ysq, sd, gate, yo = big("y"), big("yc"), big("ysq"), big("sd"), big("gate"), big("yo")
        ident, avg, ones = sb("ident", [P, P]), sb("avg", [P, P]), sb("ones", [P, P])
        mask = sb("mask", [P, 2, CH])
        lmask = [sb(f"lmask{b}", [P, 4 * CH]) for b in LEVELS]
        sub1 = sb("sub1", [P, P])
        reset = sb("reset", [P, PAIRS * CH])
        eps = sb("gn_eps", [P, 1])
        lrw = sb("lrw", [P, 2, D_R])
        mu_sb, par_sb = sb("mu_sb", [P, N_SHIFT]), sb("par_sb", [P, 5, PAIRS])
        k_k, k_a, r_k, lnx_g, lnx_b = (
            par_sb[:, n, :].unsqueeze(2).broadcast_to([P, PAIRS, CH]) for n in range(5))
        zprev = sb("zprev", [P, N_SHIFT, BATCH])
        sts = sb("sts", [P, BATCH, PAIRS, HEAD])
        amask = [sb(f"amask{n}", [P, 2, BATCH, CH]) for n in range(2)]
        zmask = [sb(f"zmask{n}", [P, PAIRS, P]) for n in range(2)]
        cmask, rmask = sb("cmask", [P, BATCH, CH]), sb("rmask", [P, BATCH])
        sh_out = sb("sh_out", [P, N_SHIFT, 1 + BATCH])

        bank = [sc.ps(f"bank{n}", [P, 512]) for n in range(8)]
        by = lambda n, j: bank[n][:, :].rearrange("p (j c) -> p j c", j=j)

        zin_loaded, gin_loaded, par_loaded = sem("zin_loaded"), sem("gin_loaded"), sem("par_loaded")
        smp_loaded, const_ready, masks_ready = sem("smp_loaded"), sem("const_ready"), sem("masks_ready")
        ident0 = sem("ident0")
        diff_ready, scaled_ready, mix_ready = sem("diff_ready"), sem("scaled_ready"), sem("mix_ready")
        lr_ready, wa_done, sig_ready = sem("lr_ready"), sem("wa_done"), sem("sig_ready")
        cum_ready, exp_ready = sem("cum_ready"), sem("exp_ready")
        kkr_ready, sq_ready, ss_done, nrm_ready = sem("kkr_ready"), sem("sq_ready"), sem("ss_done"), sem("nrm_ready")
        clamp_ready, rn_ready, kk_ready = sem("clamp_ready"), sem("rn_ready"), sem("kk_ready")
        t1_ready, k2_ready, rk_ready, rkp_ready = sem("t1_ready"), sem("k2_ready"), sem("rk_ready"), sem("rkp_ready")
        bonus_done, bonus_ready = sem("bonus_done"), sem("bonus_ready")
        bsa_ready, bk_ready, ar_ready = sem("bsa_ready"), sem("bk_ready"), sem("ar_ready")
        vt_done, zv_ready = sem("vt_done"), sem("zv_ready")
        m_done, m_ready, at_ready = sem("m_done"), sem("m_ready"), sem("at_ready")
        bkw_ready, bkt_done, bkt_ready = sem("bkw_ready"), sem("bkt_done"), sem("bkt_ready")
        tt0_ready, tt_ready, t_done, t_ready = sem("tt0_ready"), sem("tt_ready"), sem("t_done"), sem("t_ready")
        lp_done, lp_ready, lt_done, ltt_done = sem("lp_done"), sem("lp_ready"), sem("lt_done"), sem("ltt_done")
        lt_ready, ltt_ready = sem("lt_ready"), sem("ltt_ready")
        x_done, x_ready, u_done, u_ready = sem("x_done"), sem("x_ready"), sem("u_done"), sem("u_ready")
        s_done, stw_ready, st_ready, y_done = sem("s_done"), sem("stw_ready"), sem("st_ready"), sem("y_done")
        y_ready, mean_done, yc_ready, ysq_ready = sem("y_ready"), sem("mean_done"), sem("yc_ready"), sem("ysq_ready")
        var_done, sd_ready, rs_ready = sem("var_done"), sem("sd_ready"), sem("rs_ready")
        yn_ready, yg_ready, yb_ready, yv_ready = sem("yn_ready"), sem("yg_ready"), sem("yb_ready"), sem("yv_ready")
        gsig_ready, gate_ready, yo_ready, y_stored = sem("gsig_ready"), sem("gate_ready"), sem("yo_ready"), sem("y_stored")
        state_stored = sem("state_stored")
        amask_ready, xs_pair, zmask_ready = sem("amask_ready"), sem("xs_pair"), sem("zmask_ready")
        shift_ready, lv_masks = sem("shift_ready"), sem("lv_masks")

        NL = len(LEVELS)

        def levels(sample):
            return [b for b in LEVELS if not sample or b < STEPS]

        def halves_of(ap, b):
            w = ap.rearrange("p u (n h b) -> p (u n) h b", h=2, b=b)
            return w[:, :, 0, :], w[:, :, 1, :]

        def sync_chunk(sp, it, sample):
            if not sample:
                z_at, g_at = it * CH + (ZO - 1), it * CH + ZO
                if not isinstance(it, int):
                    z_at, g_at = sp.snap(z_at), sp.snap(g_at)
            sp.wait_ge(mix_ready, it * 3)
            if sample:
                sp.dma_start(zin[:, :, :], z[0:N_SHIFT, :, ZO + PROMPT - 1:ZO + TOK].rearrange("n p c -> p n c")
                             ).then_inc(zin_loaded, 16)
            else:
                sp.dma_start(zin[:, :, :], z[0:N_SHIFT, :, bass.ds(z_at, CH + 1)].rearrange(
                    "n p c -> p n c")).then_inc(zin_loaded, 16)
            sp.wait_ge(gate_ready, it)
            src = z[T_GR:T_GR + PAIRS, :, ZO + PROMPT:ZO + TOK] if sample else \
                z[T_GR:T_GR + PAIRS, :, bass.ds(g_at, CH)]
            sp.dma_start(gin[:, :, :], src.rearrange("n p c -> p n c")).then_inc(gin_loaded, 16)
            if sample:
                sp.dma_start(zprev[:, :, :], shiftT).then_inc(smp_loaded, 16)
                sp.dma_start(sts[:, :, :, :], stateT).then_inc(smp_loaded, 16)
                sp.wait_ge(shift_ready, 2)
                sp.dma_start(shift_out, sh_out[:, :, :]).then_inc(state_stored, 16)

        def vector_chunk(dve, it, sample):
            dve.wait_ge(zin_loaded, it * 16 + 16)
            dve.wait_ge(lr_ready, it * 2)
            dve.wait_ge(yo_ready, it)
            cur = zin[:, :, 1:CH + 1]
            if sample:
                dve.wait_ge(smp_loaded, 32)
                c4 = cur.rearrange("p n (b t) -> p n b t", b=BATCH)
                m4 = mix[:, :, :].rearrange("p n (b t) -> p n b t", b=BATCH)
                dve.tensor_tensor(m4[:, :, :, 1:STEPS], c4[:, :, :, 0:STEPS - 1], c4[:, :, :, 1:STEPS],
                                  SUB).then_inc(diff_ready, 1)
                dve.tensor_tensor(m4[:, :, :, 0], zprev[:, :, :], c4[:, :, :, 0], SUB).then_inc(diff_ready, 1)
                dve.tensor_copy(sh_out[:, :, 0:1], zin[:, :, 0:1]).then_inc(shift_ready, 1)
                dve.tensor_copy(sh_out[:, :, 1:1 + BATCH], c4[:, :, :, STEPS - 1]).then_inc(shift_ready, 1)
                dve.wait_ge(diff_ready, it + 2)
            else:
                dve.tensor_tensor(mix[:, :, :], zin[:, :, 0:CH], cur, SUB).then_inc(diff_ready, 1)
                dve.wait_ge(diff_ready, it + 1)
            dve.tensor_tensor(mix[:, :, :], mix[:, :, :], mu_sb[:, :].unsqueeze(2).broadcast_to([P, N_SHIFT, CH]),
                              MUL).then_inc(scaled_ready, 1)
            dve.wait_ge(scaled_ready, it + 1)
            dve.tensor_tensor(mix[:, T_LR, :], mix[:, T_LR, :], cur[:, T_LR, :], ADD).then_inc(mix_ready, 1)
            dve.tensor_tensor(mix[:, T_R:T_V, :], mix[:, T_R:T_V, :], cur[:, T_R:T_V, :], ADD).then_inc(mix_ready, 1)
            dve.tensor_tensor(v, mix[:, T_V:T_LR, :], cur[:, T_V:T_LR, :], ADD).then_inc(mix_ready, 1)
            dve.wait_ge(sig_ready, it * 2 + 1)
            flat = lambda ap: ap[:, :, :].rearrange("p u c -> p (u c)")
            dve.tensor_tensor_scan(flat(cum), reset[:, :], flat(sw), 0.0, MUL, ADD).then_inc(cum_ready, 1)
            dve.wait_ge(cum_ready, it * 2 + 1)
            dve.tensor_tensor(cum1[:, :, :], cum[:, :, :], sw[:, :, :], SUB).then_inc(cum_ready, 1)
            dve.wait_ge(sig_ready, it * 2 + 2)
            dve.scalar_tensor_tensor(t1[:, :, :], sa[:, :, :], -1.0, k_a, ADD, MUL).then_inc(t1_ready, 1)
            dve.wait_ge(t1_ready, it + 1)
            dve.scalar_tensor_tensor(k2[:, :, :], t1[:, :, :], 1.0, k, ADD, MUL).then_inc(k2_ready, 1)
            dve.wait_ge(nrm_ready, it + 1)
            dve.tensor_scalar(nrm[:, :, :], nrm[:, :, :], 1e-12, None, ALU.max).then_inc(clamp_ready, 1)
            dve.wait_ge(clamp_ready, it + 1)
            dve.reciprocal(rn[:, :, :], nrm[:, :, :]).then_inc(rn_ready, 1)
            dve.wait_ge(rn_ready, it + 1)
            dve.tensor_tensor(kk[:, :, :], kkr[:, :, :], rn[:, :, :], MUL).then_inc(kk_ready, 1)
            dve.wait_ge(kk_ready, it + 1)
            dve.tensor_tensor(bsa[:, :, :], kk[:, :, :], sa[:, :, :], MUL).then_inc(bsa_ready, 1)
            dve.wait_ge(exp_ready, it * 3 + 3)
            for h in range(2):
                dve.scalar_tensor_tensor(ar[H2[h], :, h, 0, :], kk[H2[h], :, :], -1.0, em[H2[h], :, :],
                                         MUL, MUL).then_inc(ar_ready, 1)
                dve.tensor_tensor(ar[H2[h], :, h, 1, :], r[H2[h], :, :], ep[H2[h], :, :], MUL).then_inc(ar_ready, 1)
            dve.wait_ge(bsa_ready, it + 1)
            dve.tensor_tensor(bk[:, :, 0, :], bsa[:, :, :], en[:, :, :], MUL).then_inc(bk_ready, 1)
            dve.wait_ge(bonus_done, it + 1)
            dve.tensor_tensor(bonus[:, :, :], by(3, PAIRS), v, MUL).then_inc(bonus_ready, 1)
            msk = mask[:, :, :].rearrange("p j c -> p (j c)").unsqueeze(1).broadcast_to([P, 4, P])
            for q in range(4):
                dve.wait_ge(m_done, it * 4 + q + 1)
                dve.tensor_tensor(m[:, 2 * q:2 * q + 2, :, :, :].rearrange("p u h j c -> p (u h) (j c)"), by(q, 4),
                                  msk, MUL).then_inc(m_ready, 1)
            dve.wait_ge(at_ready, it * 2 + 2)
            dve.tensor_tensor(tt[:, :, :], at[:, :, :], sub1[:, :].unsqueeze(1).broadcast_to([P, PAIRS, P]),
                              MUL).then_inc(tt0_ready, 1)
            dve.wait_ge(tt0_ready, it + 1)
            dve.tensor_tensor(tt[:, :, :], tt[:, :, :], ident[:, :].unsqueeze(1).broadcast_to([P, PAIRS, P]),
                              ADD).then_inc(tt_ready, 1)
            n_t, n_tt = it * (2 * NL - 2), it * 2 * NL
            for n, b in enumerate(levels(sample)):
                last = b == levels(sample)[-1]
                for f in range(2):
                    dve.wait_ge(lp_done, it * 2 * NL + 2 * n + f + 1)
                    dst = halves_of(pl[n][:, FOUR[f], :], b)[0]
                    dve.tensor_tensor(dst, bank[f][:, 0:4 * CH].rearrange("p (n b) -> p n b", b=b),
                                      lmask[n][:, :].rearrange("p (n b) -> p n b", b=b), MUL).then_inc(lp_ready, 1)
                for f in range(2):
                    if not last:
                        dst = halves_of(t[:, FOUR[f], :], b)[0]
                        dve.wait_ge(lt_done, n_t + 2 * n + f + 1)
                        dve.tensor_tensor(dst, dst, bank[2 + f][:, 0:4 * CH].rearrange("p (n b) -> p n b", b=b),
                                          ADD).then_inc(lt_ready, 1)
                    dst = halves_of(tt[:, FOUR[f], :], b)[1]
                    dve.wait_ge(ltt_done, n_tt + 2 * n + f + 1)
                    dve.tensor_tensor(dst, dst, bank[4 + f][:, 0:4 * CH].rearrange("p (n b) -> p n b", b=b),
                                      ADD).then_inc(ltt_ready, 1)
            if not sample:
                wc = ep[:, :, CH - 1:CH].broadcast_to([P, PAIRS, HEAD])
                dve.wait_ge(st_ready, it * 4)
                dve.wait_ge(const_ready, 1)
                dve.tensor_tensor(stw[:, :, :], st[:, :, :], wc, MUL).then_inc(stw_ready, 1)
                dve.wait_ge(stw_ready, it + 1)
                dve.wait_ge(y_done, it + 1)
                for f in range(2):
                    dve.wait_ge(s_done, it * 2 + f + 1)
                    for h in range(2):
                        dve.tensor_tensor(st[H2[h], FOUR[f], :], stw[H2[h], FOUR[f], :],
                                          by(2 + f, 4)[H2[h], :, H2[h]], ADD).then_inc(st_ready, 1)
            else:
                dve.wait_ge(y_done, it + 1)
                for b in range(BATCH):
                    wc = ep[:, :, STEPS * b + STEPS - 1:STEPS * (b + 1)].broadcast_to([P, PAIRS, HEAD])
                    dve.wait_ge(st_ready, (it + b) * 4)
                    dve.tensor_tensor(stw[:, :, :], sts[:, b, :, :], wc, MUL).then_inc(stw_ready, 1)
                    dve.wait_ge(stw_ready, it + b + 1)
                    for f in range(2):
                        dve.wait_ge(s_done, (it + b) * 2 + f + 1)
                        for h in range(2):
                            dve.tensor_tensor(sts[H2[h], b, FOUR[f], :], stw[H2[h], FOUR[f], :],
                                              by(2 + f, 4)[H2[h], :, H2[h]], ADD).then_inc(st_ready, 1)
            dve.wait_ge(mean_done, it + 1)
            dve.tensor_tensor(yc[:, :, :], y[:, :, :], by(6, PAIRS), SUB).then_inc(yc_ready, 1)
            dve.wait_ge(sd_ready, it + 1)
            dve.reciprocal(sd[:, :, :], sd[:, :, :]).then_inc(rs_ready, 1)
            dve.wait_ge(rs_ready, it + 1)
            dve.tensor_tensor(y[:, :, :], yc[:, :, :], sd[:, :, :], MUL).then_inc(yn_ready, 1)
            dve.wait_ge(yv_ready, it + 1)
            dve.wait_ge(gate_ready, it + 1)
            dve.wait_ge(y_stored, it * 16)
            dve.tensor_tensor(yo[:, :, :], y[:, :, :], gate[:, :, :], MUL).then_inc(yo_ready, 1)

        def scalar_chunk(act, it, sample):
            act.wait_ge(mix_ready, it * 3 + 1)
            act.wait_ge(par_loaded, 48)
            act.wait_ge(const_ready, 1)
            act.wait_ge(yo_ready, it)
            nc.scalar.activation(lr_w[0:HEAD, :], mix[0:HEAD, T_LR, :], ACT.Tanh).then_inc(lr_ready, 1)
            nc.scalar.activation(lr_a[HEAD:P, :], mix[HEAD:P, T_LR, :], ACT.Copy).then_inc(lr_ready, 1)
            act.wait_ge(wa_done, it * 2 + 1)
            nc.scalar.activation(sw[:, :, :], by(0, PAIRS), ACT.Sigmoid).then_inc(sig_ready, 1)
            act.wait_ge(wa_done, it * 2 + 2)
            nc.scalar.activation(sa[:, :, :], by(1, PAIRS), ACT.Sigmoid).then_inc(sig_ready, 1)
            act.wait_ge(gin_loaded, it * 16 + 16)
            nc.scalar.activation(gate[:, :, :], gin[:, :, :], ACT.Sigmoid).then_inc(gsig_ready, 1)
            act.wait_ge(cum_ready, it * 2 + 1)
            nc.scalar.activation(ep[:, :, :], cum[:, :, :], ACT.Exp, scale=-DECAY).then_inc(exp_ready, 1)
            nc.scalar.activation(en[:, :, :], cum[:, :, :], ACT.Exp, scale=DECAY).then_inc(exp_ready, 1)
            act.wait_ge(cum_ready, it * 2 + 2)
            nc.scalar.activation(em[:, :, :], cum1[:, :, :], ACT.Exp, scale=-DECAY).then_inc(exp_ready, 1)
            act.wait_ge(kkr_ready, it + 1)
            nc.scalar.activation(sq[:, :, :], kkr[:, :, :], ACT.Square).then_inc(sq_ready, 1)
            act.wait_ge(ss_done, it + 1)
            nc.scalar.activation(nrm[:, :, :], by(2, PAIRS), ACT.Sqrt).then_inc(nrm_ready, 1)
            for f in range(2):
                act.wait_ge(vt_done, it * 2 + f + 1)
                nc.scalar.activation(zz[:, FOUR[f], :], by(6 + f, 4), ACT.Copy).then_inc(zv_ready, 1)
            for h in range(2):
                act.wait_ge(m_ready, it * 4 + 4)
                nc.scalar.activation(at[H2[h], :, H2[h]], m[H2[0], :, h, 0, :], ACT.Copy).then_inc(at_ready, 1)
            for f in range(2):
                act.wait_ge(bkt_done, it * 2 + f + 1)
                nc.scalar.activation(bkt[:, FOUR[f], :], by(4 + f, 4), ACT.Copy).then_inc(bkt_ready, 1)
            for f in range(2):
                act.wait_ge(t_done, it * 2 + f + 1)
                nc.scalar.activation(t[:, FOUR[f], :], by(6 + f, 4), ACT.Copy).then_inc(t_ready, 1)
            for f in range(2):
                act.wait_ge(x_done, it * 2 + f + 1)
                for h in range(2):
                    nc.scalar.activation(xst[H2[h], FOUR[f], :], by(6 + f, 4)[H2[0], :, H2[h]],
                                         ACT.Copy).then_inc(x_ready, 1)
            for f in range(2):
                act.wait_ge(u_done, it * 2 + f + 1)
                nc.scalar.activation(zz[H2[0], FOUR[f], :], by(f, 4)[H2[0], :, :], ACT.Copy).then_inc(u_ready, 1)
            if sample:
                for b in range(BATCH):
                    act.wait_ge(u_ready, it * 2 + 2)
                    if b >= 2:
                        act.wait_ge(s_done, (it + b - 2) * 2 + 2)
                    nc.scalar.activation(zmask[b % 2][:, :, :], zz[:, :, :], ACT.Copy,
                                         scale=rmask[:, b:b + 1]).then_inc(zmask_ready, 1)
            act.wait_ge(y_done, it + 1)
            for f in range(2):
                nc.scalar.activation(y[:, FOUR[f], :], by(4 + f, 8)[:, 0:4, :], ACT.Copy).then_inc(y_ready, 1)
            act.wait_ge(yc_ready, it + 1)
            nc.scalar.activation(ysq[:, :, :], yc[:, :, :], ACT.Square).then_inc(ysq_ready, 1)
            act.wait_ge(var_done, it + 1)
            nc.scalar.activation(sd[:, :, :], by(7, PAIRS), ACT.Sqrt, bias=eps[:, 0:1]).then_inc(sd_ready, 1)
            dst = yT[:, :, PROMPT:TOK] if sample else yT[:, :, bass.ds(it * CH, CH)]
            act.wait_ge(yo_ready, it + 1)
            act.dma_start(dst.rearrange("n p c -> p n c"), yo[:, :, :]).then_inc(y_stored, 16)

        def pool_chunk(pool, it, sample):
            TTo = pool.tensor_tensor
            pool.wait_ge(mix_ready, it * 3 + 2)
            pool.wait_ge(yo_ready, it)
            TTo(kkr[:, :, :], k, k_k, MUL).then_inc(kkr_ready, 1)
            pool.wait_ge(k2_ready, it + 1)
            TTo(rk[:, :, :], r, k2[:, :, :], MUL).then_inc(rk_ready, 1)
            pool.wait_ge(rk_ready, it + 1)
            TTo(rkp[:, :, :], rk[:, :, :], r_k, MUL).then_inc(rkp_ready, 1)
            pool.wait_ge(exp_ready, it * 3 + 2)
            TTo(bk[:, :, 1, :], k2[:, :, :], en[:, :, :], MUL).then_inc(bk_ready, 1)
            pool.wait_ge(bk_ready, it * 2 + 2)
            for j in range(2):
                if sample:
                    w4 = ep[:, :, :].rearrange("p u (b t) -> p u b t", t=STEPS)[:, :, :, STEPS - 1:STEPS].broadcast_to(
                        [P, PAIRS, BATCH, STEPS])
                    split = lambda ap: ap[:, :, j, :].rearrange("p u (b t) -> p u b t", t=STEPS)
                    TTo(split(bkw), split(bk), w4, MUL).then_inc(bkw_ready, 1)
                else:
                    TTo(bkw[:, :, j, :], bk[:, :, j, :], ep[:, :, CH - 1:CH].broadcast_to([P, PAIRS, CH]),
                        MUL).then_inc(bkw_ready, 1)
            if sample:
                pool.wait_ge(ar_ready, it * 4 + 4)
                for p in range(PAIRS):
                    if p >= 2:
                        pool.wait_ge(xs_pair, p - 1)
                    for h in range(2):
                        TTo(amask[p % 2][:, h, :, :], ar[:, p, h, 0, :].unsqueeze(1).broadcast_to([P, BATCH, CH]),
                            cmask[:, :, :], MUL).then_inc(amask_ready, 1)
            pool.wait_ge(gsig_ready, it + 1)
            TTo(gate[:, :, :], gate[:, :, :], gin[:, :, :], MUL).then_inc(gate_ready, 1)
            pool.wait_ge(yn_ready, it + 1)
            TTo(y[:, :, :], y[:, :, :], lnx_g, MUL).then_inc(yg_ready, 1)
            pool.wait_ge(yg_ready, it + 1)
            TTo(y[:, :, :], y[:, :, :], lnx_b, ADD).then_inc(yb_ready, 1)
            pool.wait_ge(yb_ready, it + 1)
            pool.wait_ge(bonus_ready, it + 1)
            TTo(y[:, :, :], y[:, :, :], bonus[:, :, :], ADD).then_inc(yv_ready, 1)

        def tensor_chunk(pe, it, sample):
            pe.wait_ge(lr_ready, it * 2 + 2)
            pe.wait_ge(yo_ready, it)
            for j, lr in enumerate((lr_w, lr_a)):
                for p in range(PAIRS):
                    mm = pe.matmul(by(j, PAIRS)[:, p, :], lrw[:, j, p * P:(p + 1) * P], lr[:, :], start=True, stop=True)
                mm.then_inc(wa_done, 1)
            for f in range(2):
                pe.wait_ge(mix_ready, it * 3 + 3)
                for p in range(4 * f, 4 * f + 4):
                    mm = pe.transpose(by(6 + f, 4)[:, p % 4, :], v_pad[:, p, :], ident[:, :])
                mm.then_inc(vt_done, 1)
            pe.wait_ge(sq_ready, it + 1)
            pe.matmul(bank[2][:, :], ones[:, :], sq[:, :, :].rearrange("p u c -> p (u c)"), start=True,
                      stop=True).then_inc(ss_done, 1)
            pe.wait_ge(rkp_ready, it + 1)
            pe.matmul(bank[3][:, :], ones[:, :], rkp[:, :, :].rearrange("p u c -> p (u c)"), start=True,
                      stop=True).then_inc(bonus_done, 1)
            pe.wait_ge(bk_ready, it * 2 + 2)
            pe.wait_ge(ar_ready, it * 4 + 4)
            for q in range(4):
                if q == 0:
                    pe.wait_ge(sig_ready, it * 2 + 2)
                if q == 2:
                    pe.wait_ge(nrm_ready, it + 1)
                if q == 3:
                    pe.wait_ge(bonus_ready, it + 1)
                for p in (2 * q, 2 * q + 1):
                    mm = pe.matmul(bank[q][:, (p % 2) * 256:(p % 2) * 256 + 256],
                                   bk[:, p, :, :].rearrange("p j c -> p (j c)"),
                                   ar[:, p, :, :, :].rearrange("p h j c -> p (h j c)"), start=True, stop=True)
                mm.then_inc(m_done, 1)
            pe.wait_ge(bkw_ready, it * 2 + 2)
            for f in range(2):
                for p in range(4 * f, 4 * f + 4):
                    mm = pe.transpose(by(4 + f, 4)[:, p % 4, :], bkw[:, p, :, :].rearrange("p j c -> p (j c)"),
                                      ident[:, :])
                mm.then_inc(bkt_done, 1)
            pe.wait_ge(tt_ready, it + 1)
            for f in range(2):
                pe.wait_ge(zv_ready, it * 2 + f + 1)
                for p in range(4 * f, 4 * f + 4):
                    mm = pe.transpose(by(6 + f, 4)[:, p % 4, :], tt[:, p, :], ident[:, :])
                mm.then_inc(t_done, 1)
            for n, b in enumerate(levels(sample)):
                last = b == levels(sample)[-1]
                for f in range(2):
                    if n == 0:
                        pe.wait_ge(t_ready, it * 2 + f + 1)
                        pe.wait_ge(bkt_ready, it * 2 + 2)
                    else:
                        pe.wait_ge(lt_ready, it * (2 * NL - 2) + 2 * n - 1 + f)
                    for p in range(4 * f, 4 * f + 4):
                        mm = pe.matmul(by(f, 8)[:, p % 4, :], at[:, p, :], halves_of(t[:, p:p + 1, :], b)[0],
                                       start=True, stop=True)
                    mm.then_inc(lp_done, 1)
                for f in range(2):
                    pe.wait_ge(lp_ready, it * 2 * NL + 2 * n + f + 1)
                    if n > 0:
                        pe.wait_ge(ltt_ready, it * 2 * NL + 2 * n - 1 + f)
                    if not last:
                        for p in range(4 * f, 4 * f + 4):
                            mm = pe.matmul(by(2 + f, 8)[:, p % 4, :], tt[:, p, :], halves_of(pl[n][:, p:p + 1, :], b)[0],
                                           start=True, stop=True)
                        mm.then_inc(lt_done, 1)
                    for p in range(4 * f, 4 * f + 4):
                        mm = pe.matmul(by(4 + f, 8)[:, p % 4, :], pl[n][:, p, :], halves_of(tt[:, p:p + 1, :], b)[1],
                                       start=True, stop=True)
                    mm.then_inc(ltt_done, 1)
            pe.wait_ge(const_ready, 1)
            pe.wait_ge(st_ready, it * 4)
            pe.wait_ge(zv_ready, it * 2 + 2)
            if sample:
                pe.wait_ge(smp_loaded, 32)
            for f in range(2):
                for p in range(4 * f, 4 * f + 4):
                    if sample:
                        pe.wait_ge(amask_ready, 2 * p + 2)
                    for h in range(2):
                        out = by(6 + f, 4)[H2[0], p % 4, H2[h]]
                        if sample:
                            for b in range(BATCH):
                                mm = pe.matmul(out, amask[p % 2][:, h, b, :], sts[:, b, p, :], start=(b == 0), stop=False)
                            if h == 1:
                                mm.then_inc(xs_pair, 1)
                        else:
                            pe.matmul(out, ar[:, p, h, 0, :], st[:, p, :], start=True, stop=False)
                        mm = pe.matmul(out, m[:, p, h, 0, :], zz[:, p, H2[h]], start=False, stop=True)
                mm.then_inc(x_done, 1)
            pe.wait_ge(ltt_ready, it * 2 * NL + 2 * len(levels(sample)))
            for f in range(2):
                pe.wait_ge(x_ready, it * 4 + 2 * f + 2)
                for p in range(4 * f, 4 * f + 4):
                    for h in range(2):
                        mm = pe.matmul(by(f, 4)[H2[0], p % 4, H2[h]], tt[:, p, H2[h]], xst[:, p, :], start=True, stop=True)
                mm.then_inc(u_done, 1)
            for f in range(2):
                pe.wait_ge(u_ready, it * 2 + f + 1)
                for p in range(4 * f, 4 * f + 4):
                    for h in range(2):
                        out = by(4 + f, 8)[H2[h], p % 4, :]
                        if sample:
                            for b in range(BATCH):
                                c = slice(b * STEPS, (b + 1) * STEPS)
                                pe.matmul(out[:, c], sts[:, b, p, :], ar[:, p, h, 1, c], start=True, stop=False)
                                mm = pe.matmul(out[:, c], zz[:, p, H2[h]], m[:, p, h, 1, c], start=False, stop=True)
                        else:
                            pe.matmul(out, st[:, p, :], ar[:, p, h, 1, :], start=True, stop=False)
                            mm = pe.matmul(out, zz[:, p, H2[h]], m[:, p, h, 1, :], start=False, stop=True)
            mm.then_inc(y_done, 1)
            for b in range(BATCH if sample else 1):
                if sample:
                    pe.wait_ge(zmask_ready, b + 1)
                for f in range(2):
                    if sample and b > 0:
                        pe.wait_ge(st_ready, (it + b) * 4 - 2 + 2 * f)
                    for p in range(4 * f, 4 * f + 4):
                        mm = pe.matmul(by(2 + f, 4)[:, p % 4, :], bkt[:, p, :],
                                       zmask[b % 2][:, p, :] if sample else zz[:, p, :], start=True, stop=True)
                    mm.then_inc(s_done, 1)
            pe.wait_ge(y_ready, it * 2 + 2)
            pe.matmul(bank[6][:, :], avg[:, :], y[:, :, :].rearrange("p u c -> p (u c)"), start=True,
                      stop=True).then_inc(mean_done, 1)
            pe.wait_ge(ysq_ready, it + 1)
            pe.matmul(bank[7][:, :], avg[:, :], ysq[:, :, :].rearrange("p u c -> p (u c)"), start=True,
                      stop=True).then_inc(var_done, 1)

        def full(b):
            return b[tuple(slice(None) for _ in b.shape)]

        fills = ((ident, 0.0), (ones, 0.0), (avg, 0.0), (sub1, 0.0), (reset, 1.0), (eps, GN_EPS),
                 (mask, 1.0), (lr_w, 0.0), (lr_a, 0.0), (cmask, 0.0), (rmask, 1.0),
                 (v_pad, 0.0), (ar, 0.0), (at, 0.0), *((x, 0.0) for x in pl), *((x, 1.0) for x in lmask))

        def constants(pool):
            for b, val in fills:
                pool.memset(full(b), val).then_inc(ident0, 1)
            pool.wait_ge(ident0, len(fills))
            steps = [0]

            def select(ap, pattern, op, fill, base, cm):
                pool.affine_select(out=ap, in_=ap, pattern=pattern, compare_op=op, fill=fill, base=base,
                                   channel_multiplier=cm).then_inc(masks_ready, 1)
                steps[0] += 1
                pool.wait_ge(masks_ready, steps[0])

            def fill(ap, val):
                pool.memset(ap, val).then_inc(masks_ready, 1)
                steps[0] += 1
                pool.wait_ge(masks_ready, steps[0])

            select(ident[:, :], [[-1, P]], ALU.not_equal, 1.0, 0, 1)
            for h in range(2):
                fill(ones[H2[h], H2[h]], 1.0)
                fill(avg[H2[h], H2[h]], 1.0 / HEAD)
            select(sub1[:, :], [[-1, P]], ALU.not_equal, 1.0, 1, 1)
            fill(sub1[:, :].rearrange("p (n b) -> p n b", b=2)[:, :, 0], 0.0)
            fill(reset[:, :].rearrange("p (n c) -> p n c", c=CH)[:, :, 0], 0.0)
            fill(lr_w[HEAD:HEAD + 1, :], 1.0)
            fill(lr_a[0:1, :], 1.0)
            for rows in H2:
                select(mask[rows, 0, :], [[1, CH]], ALU.is_ge, 0.0, -1, -1)
                select(mask[rows, 1, :], [[1, CH]], ALU.is_ge, 0.0, 0, -1)
            for n, b in enumerate(LEVELS):
                select(lmask[n][:, :], [[0, 4], [-2 * b, CH // b], [0, b]], ALU.is_ge, 0.0, -b, 1)
                select(lmask[n][:, :], [[0, 4], [2 * b, CH // b], [0, b]], ALU.is_ge, 0.0, 2 * b - 1, -1)
            for b in range(BATCH):
                fill(cmask[:, b, b * STEPS:(b + 1) * STEPS], 1.0)
            for rows in H2:
                select(rmask[rows, :], [[-STEPS, BATCH]], ALU.is_ge, 0.0, 0, 1)
                select(rmask[rows, :], [[STEPS, BATCH]], ALU.is_ge, 0.0, STEPS - 1, -1)
            pool.memset(st[:, :, :], 0.0).then_inc(const_ready, 1)

        def sample_masks(pool):
            pool.wait_ge(yo_ready, NCHUNK)
            n = 0
            for rows in H2:
                for j in range(2):
                    pool.affine_select(out=mask[rows, j, :], in_=mask[rows, j, :], pattern=[[-STEPS, BATCH], [0, STEPS]],
                                       compare_op=ALU.is_ge, fill=0.0, base=0, channel_multiplier=1).then_inc(lv_masks, 1)
                    n += 1
                    pool.wait_ge(lv_masks, n)
            pool.memset(reset[:, :].rearrange("p (n c) -> p n c", c=STEPS)[:, :, 0], 0.0).then_inc(lv_masks, 1)

        with nc.Block() as block:
            @block.sync
            def _(sp):
                sp.dma_start(lrw[:, :, :], lowrank).then_inc(par_loaded, 16)
                sp.dma_start(mu_sb[:, :], mu).then_inc(par_loaded, 16)
                sp.dma_start(par_sb[:, :, :], par).then_inc(par_loaded, 16)
                sync_chunk(sp, 0, False)
                with sp.Fori(1, NCHUNK) as it:
                    sync_chunk(sp, it, False)
                sp.wait_ge(st_ready, NCHUNK * 4)
                sp.dma_start(pwkv_out, st[:, :, :]).then_inc(state_stored, 16)
                sync_chunk(sp, NCHUNK, True)
                sp.wait_ge(st_ready, (NCHUNK + BATCH) * 4)
                sp.dma_start(swkv_out, sts[:, :, :, :]).then_inc(state_stored, 16)
                sp.wait_ge(state_stored, 48)
                sp.wait_ge(y_stored, (NCHUNK + 1) * 16)

            @block.gpsimd
            def _(pool):
                constants(pool)
                pool.wait_ge(const_ready, 1)
                pool.wait_ge(par_loaded, 48)
                pool_chunk(pool, 0, False)
                with pool.Fori(1, NCHUNK) as it:
                    pool_chunk(pool, it, False)
                sample_masks(pool)
                pool_chunk(pool, NCHUNK, True)

            @block.scalar
            def _(act):
                scalar_chunk(act, 0, False)
                with act.Fori(1, NCHUNK) as it:
                    scalar_chunk(act, it, False)
                scalar_chunk(act, NCHUNK, True)

            @block.vector
            def _(dve):
                dve.wait_ge(par_loaded, 48)
                dve.wait_ge(const_ready, 1)
                vector_chunk(dve, 0, False)
                with dve.Fori(1, NCHUNK) as it:
                    vector_chunk(dve, it, False)
                dve.wait_ge(lv_masks, 5)
                vector_chunk(dve, NCHUNK, True)

            @block.tensor
            def _(pe):
                pe.wait_ge(par_loaded, 48)
                pe.wait_ge(const_ready, 1)
                tensor_chunk(pe, 0, False)
                with pe.Fori(1, NCHUNK) as it:
                    tensor_chunk(pe, it, False)
                tensor_chunk(pe, NCHUNK, True)


def phase_sgu(nc, z, wT, bias, ln_par, sT, vn_out):
    with ExitStack() as stack:
        sc = Scope(nc, stack)
        sb, sem = sc.sb, sc.sem
        G = PAIRS
        vn = sb("vn", [P, G, TP])
        sqb = [sb(f"sgu_sq{n}", [P, TP]) for n in range(2)]
        rs = sb("sgu_rs", [P, TP])
        u, gg, sg = ([sb(f"sgu_{n}{j}", [P, TP]) for j in range(2)] for n in ("u", "g", "sg"))
        so = [sb(f"sgu_out{j}", [P, TP]) for j in range(2)]
        vt = [sb(f"sgu_vt{j}", [P, 4, Q]) for j in range(2)]
        wm, w8 = sb("sgu_wm", [P, G, Q]), sb("sgu_w8", [SAMPLE, G, SAMPLE])
        bb = sb("sgu_bb", [P, G, Q])
        lnp = sb("sgu_ln", [P, 2, G])
        ones, ident, eps = sb("sgu_ones", [P, P]), sb("sgu_ident", [P, P]), sb("sgu_eps", [P, 1])
        mean, var = sc.ps("sgu_mean", [P, 3, 512]), sc.ps("sgu_var", [P, 3, 512])
        mixed = [sc.ps(f"sgu_mixed{j}", [P, 512]) for j in range(2)]
        turned = [mean[:, j, :] for j in range(2)]

        vg_loaded = [sem(f"vg_loaded{n}") for n in range(G)]
        w_loaded, w8_loaded, w8_zero = sem("sgu_w_loaded"), sem("sgu_w8_loaded"), sem("sgu_w8_zero")
        const0, const_ready, w_ready = sem("sgu_const0"), sem("sgu_const_ready"), sem("sgu_w_ready")
        mean_done, vc_ready, sq_ready, sq_summed = sem("sgu_mean_done"), sem("vc_ready"), sem("sgu_sq_ready"), sem("sgu_sq_summed")
        rt_ready, rs_ready, vs_ready, vn_ready = sem("sgu_rt_ready"), sem("sgu_rs_ready"), sem("vs_ready"), sem("vn_ready")
        turn_done, vt_ready, mix_done, mix_read = sem("turn_done"), sem("vt_ready"), sem("sgu_mix_done"), sem("sgu_mix_read")
        ug_loaded = [sem(f"ug_loaded{j}") for j in range(2)]
        sig_ready, su_ready, gate_ready, out_ready = sem("sgu_sig_ready"), sem("su_ready"), sem("sgu_gate_ready"), sem("sgu_out_ready")
        stored, vn_stored = [sem(f"sgu_stored{j}") for j in range(2)], sem("vn_stored")
        cols = lambda j: slice(j * 512, (j + 1) * 512) if j < 2 else slice(PROMPT, TOK)

        with nc.Block() as block:
            @block.sync
            def _(sp):
                for n in range(G):
                    sp.dma_start(vn[:, n, :], z[T_VG + n, :, ZO:ZW]).then_inc(vg_loaded[n], 16)
                for n in range(G):
                    j = n % 2
                    if n >= 2:
                        sp.wait_ge(out_ready, n - 1)
                    sp.dma_start(u[j][:, :], z[T_U + n, :, ZO:ZW]).then_inc(ug_loaded[j], 16)
                    sp.dma_start(gg[j][:, :], z[T_GG + n, :, ZO:ZW]).then_inc(ug_loaded[j], 16)
                    if n >= 1:
                        sp.wait_ge(out_ready, n)
                        sp.dma_start(sT[n - 1, :, 0:TOK], so[1 - j][:, 0:TOK]).then_inc(stored[1 - j], 16)
                    if n == 1:
                        sp.wait_ge(vn_ready, G)
                        sp.dma_start(vn_out, vn[:, :, PROMPT:TOK]).then_inc(vn_stored, 16)
                sp.wait_ge(out_ready, G)
                sp.dma_start(sT[G - 1, :, 0:TOK], so[(G - 1) % 2][:, 0:TOK]).then_inc(stored[(G - 1) % 2], 16)
                for j in range(2):
                    sp.wait_ge(stored[j], G // 2 * 16)
                sp.wait_ge(vn_stored, 16)

            @block.gpsimd
            def _(pool):
                pool.dma_start(wm[:, :, :], wT.rearrange("g s t -> s g t")).then_inc(w_loaded, 16)
                pool.dma_start(bb[:, :, :], bias.unsqueeze(0).broadcast_to([P, G, Q])).then_inc(w_loaded, 16)
                pool.dma_start(lnp[:, :, :], ln_par).then_inc(w_loaded, 16)
                pool.memset(w8[:, :, :], 0.0).then_inc(w8_zero, 1)
                pool.memset(ones[:, :], 1.0 / D_G).then_inc(const_ready, 1)
                pool.memset(eps[:, :], LN_EPS).then_inc(const_ready, 1)
                pool.memset(ident[:, :], 0.0).then_inc(const0, 1)
                pool.wait_ge(const0, 1)
                pool.affine_select(out=ident[:, :], in_=ident[:, :], pattern=[[-1, P]], compare_op=ALU.not_equal,
                                   fill=1.0, base=0, channel_multiplier=1).then_inc(const_ready, 1)
                pool.wait_ge(w8_zero, 1)
                for b in range(BATCH):
                    e = slice(b * STEPS, (b + 1) * STEPS)
                    pool.dma_start(w8[e, :, e], wT[:, 0:STEPS, 0:STEPS].rearrange("g s t -> s g t")).then_inc(w8_loaded, 16)
                pool.wait_ge(w_loaded, 48)
                pool.wait_ge(const_ready, 3)
                pool.affine_select(out=wm[:, :, :], in_=wm[:, :, :], pattern=[[0, G], [1, Q]], compare_op=ALU.is_ge,
                                   fill=0.0, base=0, channel_multiplier=-1).then_inc(w_ready, 1)
                pool.wait_ge(w8_loaded, 16 * BATCH)
                pool.wait_ge(w_ready, 1)
                pool.affine_select(out=w8[:, :, :], in_=w8[:, :, :], pattern=[[0, G], [1, SAMPLE]], compare_op=ALU.is_ge,
                                   fill=0.0, base=0, channel_multiplier=-1).then_inc(w_ready, 1)
                for n in range(G):
                    j = n % 2
                    pool.wait_ge(sig_ready, n + 1)
                    pool.tensor_tensor(sg[j][:, 0:TOK], sg[j][:, 0:TOK], gg[j][:, 0:TOK], MUL).then_inc(gate_ready, 1)
                    pool.wait_ge(gate_ready, n + 1)
                    pool.wait_ge(su_ready, 3 * n + 3)
                    pool.tensor_tensor(so[j][:, 0:TOK], so[j][:, 0:TOK], sg[j][:, 0:TOK], MUL).then_inc(out_ready, 1)

            @block.scalar
            def _(act):
                for n in range(G):
                    act.wait_ge(vc_ready, n + 1)
                    if n >= 2:
                        act.wait_ge(sq_summed, n - 1)
                    nc.scalar.activation(sqb[n % 2][:, :], vn[:, n, :], ACT.Square).then_inc(sq_ready, 1)
                act.wait_ge(sq_summed, G)
                act.wait_ge(const_ready, 3)
                nc.scalar.activation(pieces(rs[:, :]), var[:, :, 0:NCH], ACT.Sqrt, bias=eps[:, 0:1]).then_inc(rt_ready, 1)
                act.wait_ge(w_loaded, 48)
                for n in range(G):
                    act.wait_ge(vs_ready, n + 1)
                    nc.scalar.activation(vn[:, n, :], vn[:, n, :], ACT.Identity, scale=lnp[:, 0, n:n + 1],
                                         bias=lnp[:, 1, n:n + 1]).then_inc(vn_ready, 1)
                for n in range(G):
                    act.wait_ge(ug_loaded[n % 2], 32 * (n // 2 + 1))
                    if n >= 2:
                        act.wait_ge(out_ready, n - 1)
                    nc.scalar.activation(sg[n % 2][:, 0:TOK], gg[n % 2][:, 0:TOK], ACT.Sigmoid).then_inc(sig_ready, 1)
                    for j in range(3):
                        e = 3 * n + j
                        act.wait_ge(turn_done, e + 1)
                        if e >= 2:
                            act.wait_ge(mix_done, e - 1)
                        if j < 2:
                            nc.scalar.activation(vt[e % 2][:, :, :].rearrange("p c t -> p (c t)"), turned[e % 2],
                                                 ACT.Copy).then_inc(vt_ready, 1)
                        else:
                            nc.scalar.activation(vt[e % 2][0:SAMPLE, 0, :], turned[e % 2][0:SAMPLE, 0:P],
                                                 ACT.Copy).then_inc(vt_ready, 1)

            @block.vector
            def _(dve):
                dve.wait_ge(mean_done, 1)
                for n in range(G):
                    dve.tensor_tensor(pieces(vn[:, n, :]), pieces(vn[:, n, :]), mean[:, :, 0:NCH], SUB).then_inc(vc_ready, 1)
                dve.wait_ge(rt_ready, 1)
                dve.reciprocal(rs[:, :], rs[:, :]).then_inc(rs_ready, 1)
                dve.wait_ge(rs_ready, 1)
                for n in range(G):
                    dve.tensor_tensor(vn[:, n, :], vn[:, n, :], rs[:, :], MUL).then_inc(vs_ready, 1)
                for n in range(G):
                    dve.wait_ge(ug_loaded[n % 2], 32 * (n // 2 + 1))
                    if n >= 2:
                        dve.wait_ge(stored[n % 2], n // 2 * 16)
                    for j in range(3):
                        e = 3 * n + j
                        dst, src = so[n % 2][:, cols(j)], mixed[e % 2][:, :]
                        dve.wait_ge(mix_done, e + 1)
                        if j < 2:
                            dst4 = dst.rearrange("p (c t) -> p c t", t=Q)
                            dve.tensor_tensor(dst4, src.rearrange("p (c t) -> p c t", t=Q),
                                              bb[:, n, :].unsqueeze(1).broadcast_to([P, 4, Q]), ADD).then_inc(mix_read, 1)
                        else:
                            dst4 = dst.rearrange("p (c t) -> p c t", t=STEPS)
                            dve.tensor_tensor(dst4, src[:, 0:SAMPLE].rearrange("p (c t) -> p c t", t=STEPS),
                                              bb[:, n, 0:STEPS].unsqueeze(1).broadcast_to([P, BATCH, STEPS]),
                                              ADD).then_inc(mix_read, 1)
                        dve.wait_ge(mix_read, e + 1)
                        dve.tensor_tensor(dst, dst, u[n % 2][:, cols(j)], MUL).then_inc(su_ready, 1)

            @block.tensor
            def _(pe):
                pe.wait_ge(const_ready, 3)
                for n in range(G):
                    pe.wait_ge(vg_loaded[n], 16)
                    for c in range(3):
                        mm = pe.matmul(mean[:, c, 0:NCH], ones[:, :], vn[:, n, c * NCH:(c + 1) * NCH],
                                       start=(n == 0), stop=(n == G - 1))
                mm.then_inc(mean_done, 1)
                for n in range(G):
                    pe.wait_ge(sq_ready, n + 1)
                    for c in range(3):
                        mm = pe.matmul(var[:, c, 0:NCH], ones[:, :], sqb[n % 2][:, c * NCH:(c + 1) * NCH],
                                       start=(n == 0), stop=(n == G - 1))
                    mm.then_inc(sq_summed, 1)
                pe.wait_ge(w_ready, 2)

                def turn(e):
                    n, j = e // 3, e % 3
                    pe.wait_ge(vn_ready, n + 1)
                    if e >= 2:
                        pe.wait_ge(vt_ready, e - 1)
                    if j < 2:
                        for c in range(4):
                            o = j * 512 + c * Q
                            mm = pe.transpose(turned[e % 2][:, c * Q:(c + 1) * Q], vn[:, n, o:o + Q], ident[:, :])
                    else:
                        mm = pe.transpose(turned[e % 2][0:SAMPLE, 0:P], vn[:, n, PROMPT:TOK], ident[:, :])
                    mm.then_inc(turn_done, 1)

                turn(0)
                for e in range(3 * G):
                    n, j = e // 3, e % 3
                    if e + 1 < 3 * G:
                        turn(e + 1)
                    pe.wait_ge(vt_ready, e + 1)
                    if e >= 2:
                        pe.wait_ge(mix_read, e - 1)
                    if j < 2:
                        for c in range(4):
                            mm = pe.matmul(mixed[e % 2][:, c * Q:(c + 1) * Q], vt[e % 2][:, c, :], wm[:, n, :],
                                           start=True, stop=True)
                    else:
                        mm = pe.matmul(mixed[e % 2][:, 0:SAMPLE], vt[e % 2][0:SAMPLE, 0, :], w8[:, n, :],
                                       start=True, stop=True)
                    mm.then_inc(mix_done, 1)


class Operand:

    RING = 4

    def __init__(self, sc, tag, tiles, xh, xl, gm, ring):
        self.tiles, self.xh, self.xl, self.gm = tiles, xh, xl, gm
        self.ring = [sc.sb(f"{tag}_xs{n}", [P, TP]) for n in range(ring)]
        self.loaded = [sc.sem(f"{tag}_x_loaded{n}") for n in range(ring)]
        self.xh_ready, self.pad_ready = sc.sem(f"{tag}_xh_ready"), sc.sem(f"{tag}_pad_ready")

    def load(self, engine):
        r = len(self.ring)
        for n, tile in enumerate(self.tiles):
            if n >= r:
                engine.wait_ge(self.gm.x_ready, n - r + 1)
            engine.dma_start(self.ring[n % r][:, 0:TOK], tile).then_inc(self.loaded[n % r], 16)

    def pad(self, engine):
        for b in self.ring:
            engine.memset(b[:, TOK:TP], 0.0).then_inc(self.pad_ready, 1)

    def split(self, dve):
        r = len(self.ring)
        dve.wait_ge(self.pad_ready, r)
        for n in range(len(self.tiles)):
            x = self.ring[n % r]
            dve.wait_ge(self.loaded[n % r], 16 * (n // r + 1))
            dve.tensor_copy(self.xh[:, n, :], x[:, :]).then_inc(self.xh_ready, 1)
            dve.wait_ge(self.xh_ready, n + 1)
            dve.tensor_tensor(self.xl[:, n, :], x[:, :], self.xh[:, n, :].bitcast(F32), SUB).then_inc(self.gm.x_ready, 1)


def phase_merge(nc, z, yT, sT, wt, mT):
    with ExitStack() as stack:
        sc = Scope(nc, stack)
        xh, xl = sc.sb("mg_xh", [P, KT, TP], F32R), sc.sb("mg_xl", [P, KT, TP], F32R)
        gm = Gemm(nc, sc, "mg", wt, KH, xh, xl, (0, KH))
        op = Operand(sc, "mg", [d[n, :, 0:TOK] for d in (yT, sT) for n in range(KH)], xh, xl, gm, 4)
        gate = [sc.sb(f"mg_gate{s}", [P, TP]) for s in range(2)]
        part = [sc.sb(f"mg_part{s}", [P, TP]) for s in range(2)]
        mo = sc.sb("mg_out", [P, TP])
        gate_loaded = [sc.sem(f"mg_gate_loaded{s}") for s in range(2)]
        sig_ready, part_ready = sc.sem("mg_sig_ready"), sc.sem("mg_part_ready")
        m_ready, stored = sc.sem("mg_m_ready"), sc.sem("mg_m_stored")

        with nc.Block() as block:
            @block.sync
            def _(sp):
                def load(g, i, s):
                    gm.load(sp, g, i, s)
                    sp.wait_ge(part_ready, i * 2)
                    sp.dma_start(gate[s][:, :], tile_of(z, i + (T_GA, T_GB)[s])[:, ZO:ZW]).then_inc(gate_loaded[s], 16)

                in_slots(sp, 2 * KT, load)

            @block.scalar
            def _(act):
                op.load(act)

                def step(g, i, s):
                    act.wait_ge(gate_loaded[s], i * 16 + 16)
                    nc.scalar.activation(gate[s][:, :], gate[s][:, :], ACT.Sigmoid).then_inc(sig_ready, 1)
                    act.wait_ge(gm.group_done[s], i + 1)
                    act.wait_ge(m_ready, i)
                    nc.scalar.activation(pieces(part[s][:, :]), gm.sums(s), ACT.Copy).then_inc(gm.evacuated[s], 1)
                    if s == 1:
                        act.wait_ge(m_ready, i + 1)
                        act.dma_start(tile_of(mT, i), mo[:, :]).then_inc(stored, 16)

                in_slots(act, 2 * KT, step)
                act.wait_ge(stored, KT * 16)

            @block.gpsimd
            def _(pool):
                op.pad(pool)

                def step(g, i, s):
                    pool.wait_ge(sig_ready, i * 2 + s + 1)
                    pool.wait_ge(gm.evacuated[s], i + 1)
                    pool.tensor_tensor(part[s][:, :], part[s][:, :], gate[s][:, :], MUL).then_inc(part_ready, 1)
                    if s == 1:
                        pool.wait_ge(part_ready, i * 2 + 2)
                        pool.wait_ge(stored, i * 16)
                        pool.tensor_tensor(mo[:, :], part[0][:, :], part[1][:, :], ADD).then_inc(m_ready, 1)

                in_slots(pool, 2 * KT, step)

            @block.vector
            def _(dve):
                for s in range(2):
                    gm.split(dve, 0, s)
                op.split(dve)
                with dve.Fori(1, KT) as i:
                    for s in range(2):
                        gm.split(dve, i, s)

            @block.tensor
            def _(pe):
                in_slots(pe, 2 * KT, lambda g, i, s: gm.products(pe, i, s))


def phase_out(nc, xT, mT, wt, hT, ssq_dram):
    with ExitStack() as stack:
        sc = Scope(nc, stack)
        xh, xl = sc.sb("out_xh", [P, KT, TP], F32R), sc.sb("out_xl", [P, KT, TP], F32R)
        gm = Gemm(nc, sc, "out", wt, KT, xh, xl, (0, 0))
        op = Operand(sc, "out", [mT[n, :, 0:TOK] for n in range(KT)], xh, xl, gm, 2)
        xr, h = op.ring
        sq, ssq = sc.sb("out_sq", [P, TP]), sc.sb("out_ssq", [P, TP])
        x_loaded, h_ready, sq_ready = sc.sem("out_xr_loaded"), sc.sem("h_ready"), sc.sem("out_sq_ready")
        ssq_ready, stored, ssq_stored = sc.sem("ssq_ready"), sc.sem("h_stored"), sc.sem("ssq_stored")

        with nc.Block() as block:
            @block.sync
            def _(sp):
                in_slots(sp, KT, lambda g, i, s: gm.load(sp, g, i, s))

            @block.scalar
            def _(act):
                op.load(act)
                act.wait_ge(gm.x_ready, KT)

                def step(g, i, s):
                    act.wait_ge(h_ready, g)
                    act.dma_start(xr[:, 0:TOK], tile_of(xT, g)).then_inc(x_loaded, 16)
                    act.wait_ge(gm.group_done[s], i + 1)
                    act.wait_ge(stored, g * 16)
                    act.wait_ge(sq_ready, g)
                    nc.scalar.activation(pieces(h[:, :]), gm.sums(s), ACT.Copy).then_inc(gm.evacuated[s], 1)
                    act.wait_ge(h_ready, g + 1)
                    act.dma_start(tile_of(hT, g), h[:, :]).then_inc(stored, 16)

                in_slots(act, KT, step)
                act.wait_ge(ssq_ready, KT + 1)
                act.dma_start(ssq_dram, ssq[:, :]).then_inc(ssq_stored, 16)
                act.wait_ge(stored, KT * 16)
                act.wait_ge(ssq_stored, 16)

            @block.gpsimd
            def _(pool):
                op.pad(pool)
                pool.memset(ssq[:, :], 0.0).then_inc(ssq_ready, 1)

                def step(g, i, s):
                    pool.wait_ge(x_loaded, g * 16 + 16)
                    pool.wait_ge(gm.evacuated[s], i + 1)
                    pool.tensor_tensor(h[:, :], h[:, :], xr[:, :], ADD).then_inc(h_ready, 1)
                    pool.wait_ge(h_ready, g + 1)
                    pool.wait_ge(ssq_ready, g + 1)
                    pool.tensor_tensor(sq[:, :], h[:, :], h[:, :], MUL).then_inc(sq_ready, 1)
                    pool.wait_ge(sq_ready, g + 1)
                    pool.tensor_tensor(ssq[:, :], ssq[:, :], sq[:, :], ADD).then_inc(ssq_ready, 1)

                in_slots(pool, KT, step)

            @block.vector
            def _(dve):
                for s in range(2):
                    gm.split(dve, 0, s)
                op.split(dve)
                with dve.Fori(1, KT // 2) as i:
                    for s in range(2):
                        gm.split(dve, i, s)

            @block.tensor
            def _(pe):
                in_slots(pe, KT, lambda g, i, s: gm.products(pe, i, s))


def phase_final(nc, hT, ssq_dram, final_g, outT):
    with ExitStack() as stack:
        sc = Scope(nc, stack)
        h = sc.sb("fin_h", [P, KT, TP])
        o = [sc.sb(f"fin_o{n}", [P, TP]) for n in range(4)]
        ssq, rs = sc.sb("fin_ssq", [P, TP]), sc.sb("fin_rs", [P, TP])
        g_sb, eps, ones = sc.sb("fin_g", [P, KT]), sc.sb("fin_eps", [P, 1]), sc.sb("fin_ones", [P, P])
        ms = sc.ps("fin_ms", [P, 3, 512])
        h_loaded = [sc.sem(f"fin_h_loaded{n}") for n in range(KT)]
        ssq_loaded, const_ready, ms_done = sc.sem("fin_ssq_loaded"), sc.sem("fin_const_ready"), sc.sem("fin_ms_done")
        rt_ready, rs_ready, o_ready = sc.sem("fin_rt_ready"), sc.sem("fin_rs_ready"), sc.sem("fin_o_ready")
        stored = [sc.sem(f"fin_stored{n}") for n in range(4)]

        with nc.Block() as block:
            @block.sync
            def _(sp):
                sp.dma_start(ssq[:, :], ssq_dram).then_inc(ssq_loaded, 16)
                sp.dma_start(g_sb[:, :], final_g).then_inc(ssq_loaded, 16)
                for n in range(KT):
                    sp.dma_start(h[:, n, :], hT[n]).then_inc(h_loaded[n], 16)

            @block.gpsimd
            def _(pool):
                pool.memset(ones[:, :], 1.0 / D_MODEL).then_inc(const_ready, 1)
                pool.memset(eps[:, :], RMS_EPS).then_inc(const_ready, 1)

            @block.tensor
            def _(pe):
                pe.wait_ge(const_ready, 2)
                pe.wait_ge(ssq_loaded, 32)
                for c in range(3):
                    mm = pe.matmul(ms[:, c, 0:NCH], ones[:, :], ssq[:, c * NCH:(c + 1) * NCH], start=True, stop=True)
                mm.then_inc(ms_done, 1)

            @block.scalar
            def _(act):
                act.wait_ge(const_ready, 2)
                act.wait_ge(ms_done, 1)
                nc.scalar.activation(pieces(rs[:, :]), ms[:, :, 0:NCH], ACT.Sqrt, bias=eps[:, 0:1]).then_inc(rt_ready, 1)
                for n in range(KT):
                    act.wait_ge(o_ready, n + 1)
                    act.dma_start(outT[n], o[n % 4][:, 0:TOK]).then_inc(stored[n % 4], 16)
                for s in stored:
                    act.wait_ge(s, KT // 4 * 16)

            @block.vector
            def _(dve):
                dve.wait_ge(rt_ready, 1)
                dve.reciprocal(rs[:, :], rs[:, :]).then_inc(rs_ready, 1)
                dve.wait_ge(rs_ready, 1)
                dve.wait_ge(ssq_loaded, 32)
                for n in range(KT):
                    dve.wait_ge(h_loaded[n], 16)
                    if n >= 4:
                        dve.wait_ge(stored[n % 4], n // 4 * 16)
                    dve.scalar_tensor_tensor(o[n % 4][:, :], h[:, n, :], g_sb[:, n:n + 1], rs[:, :], MUL,
                                             MUL).then_inc(o_ready, 1)


OUTPUTS = {
    "outT": (KT, P, TOK), "shift_out": (P, N_SHIFT, 1 + BATCH), "pwkv_out": (P, PAIRS, HEAD),
    "swkv_out": (P, BATCH, PAIRS, HEAD), "vn_out": (P, PAIRS, SAMPLE),
}


def program(nc, a):
    scratch = lambda name, shape: nc.dram_tensor(name, shape, F32, kind="Internal").ap()
    z = scratch("z", (NTILE, P, ZW))
    yT, sT = scratch("yT", (PAIRS, P, TP)), scratch("sT", (PAIRS, P, TP))
    mT, hT, ssq = scratch("mT", (KT, P, TP)), scratch("hT", (KT, P, TP)), scratch("ssq", (P, TP))
    phase_in(nc, a["xT"], a["norm_g"], a["w_in"], z)
    phase_rwkv(nc, z, a["lowrank"], a["mu"], a["par"], a["shiftT"], a["stateT"], yT, a["shift_out"], a["swkv_out"],
               a["pwkv_out"])
    phase_sgu(nc, z, a["sgu_wT"], a["sgu_b"], a["ln_par"], sT, a["vn_out"])
    phase_merge(nc, z, yT, sT, a["w_proj"], mT)
    phase_out(nc, a["xT"], mT, a["w_out"], hT, ssq)
    phase_final(nc, hT, ssq, a["final_g"], a["outT"])


def layouts(inputs):
    import numpy as np
    x = {n: np.asarray(a) for n, a in inputs.items()}
    rows = lambda a: np.ascontiguousarray(a.reshape(-1, P).T)
    tok = np.concatenate([x["x_prompt"].reshape(PROMPT, D_MODEL), x["x_sample"].reshape(SAMPLE, D_MODEL)])
    tiles = lambda w: w.reshape(w.shape[0] // P, P, -1, P).transpose(2, 1, 0, 3).reshape(w.shape[1] // P, P, -1)
    low = np.zeros((P, 2, D_R), np.float32)
    low[0:HEAD, 0], low[HEAD, 0] = x["w2"][0], x["w0"][0]
    low[HEAD:P, 1], low[0, 1] = x["a2"][0], x["a0"][0]
    out = {
        "xT": tok.T.reshape(KT, P, TOK),
        "norm_g": rows(x["norm_g"][0]),
        "w_in": tiles(x["w_in"][0]),
        "lowrank": low,
        "mu": rows(x["shift_mu"][0]),
        "par": np.stack([rows(x[n].reshape(-1)) for n in ("k_k", "k_a", "r_k", "lnx_g", "lnx_b")], 1),
        "shiftT": x["state_shift"].reshape(BATCH, N_SHIFT, P).transpose(2, 1, 0),
        "stateT": x["state_wkv"].reshape(BATCH, PAIRS, 2, HEAD, HEAD).transpose(2, 4, 0, 1, 3).reshape(
            P, BATCH, PAIRS, HEAD),
        "sgu_wT": x["sgu_w"][0].transpose(0, 2, 1),
        "sgu_b": x["sgu_b"][0],
        "ln_par": np.stack([rows(x[n][0]) for n in ("sgu_ln_g", "sgu_ln_b")], 1),
        "w_proj": np.stack([tiles(x["w_proj_a"][0]), tiles(x["w_proj_b"][0])], 1).reshape(2 * KT, P, KH * P),
        "w_out": tiles(x["w_out"][0]),
        "final_g": rows(x["final_norm_g"]),
    }
    return {n: np.ascontiguousarray(a) for n, a in out.items()}


def kernel(**inputs):
    import numpy as np
    import concourse.bacc as bacc
    from concourse.bass_utils import run_bass_kernel_spmd

    nc = bacc.Bacc("TRN2", target_bir_lowering=False, num_devices=1)
    arrays = {f"in_{n}": a for n, a in layouts(inputs).items()}
    aps = {n[3:]: nc.dram_tensor(n, a.shape, mybir.dt.from_np(a.dtype), kind="ExternalInput").ap()
           for n, a in arrays.items()}
    for n, shape in OUTPUTS.items():
        aps[n] = nc.dram_tensor(n, shape, F32, kind="ExternalOutput").ap()
    program(nc, aps)
    got = run_bass_kernel_spmd(nc, [arrays], core_ids=[0]).results[0]

    tok = got["outT"].reshape(D_MODEL, TOK).T
    shift = got["shift_out"].transpose(2, 1, 0).reshape(1 + BATCH, N_SHIFT * P)
    pwkv = got["pwkv_out"].reshape(2, HEAD, PAIRS, HEAD).transpose(2, 0, 3, 1).reshape(1, 1, 2 * PAIRS, HEAD, HEAD)
    swkv = got["swkv_out"].reshape(2, HEAD, BATCH, PAIRS, HEAD).transpose(2, 3, 0, 4, 1).reshape(
        1, BATCH, 2 * PAIRS, HEAD, HEAD)
    vn = got["vn_out"].transpose(2, 1, 0).reshape(1, BATCH, STEPS, D_G)
    back = np.ascontiguousarray
    return (back(tok[:PROMPT]).reshape(1, PROMPT, D_MODEL), back(tok[PROMPT:]).reshape(BATCH, STEPS, D_MODEL),
            back(pwkv), back(shift[0:1]).reshape(1, 1, 1, -1), back(swkv), back(shift[1:]).reshape(1, BATCH, 1, -1),
            back(vn))
```

```python
from contextlib import ExitStack

import concourse.bass as bass
from concourse import mybir

P = 128
D_MODEL, D_R, D_G = 2048, 1024, 1024
KT = D_MODEL // P
KH = D_R // P
HEAD = 64
PAIRS = D_R // P
PROMPT, BATCH, STEPS = 1024, 8, 8
SAMPLE = BATCH * STEPS
TOK = PROMPT + SAMPLE
NCH = 364
TP = 3 * NCH
ZO = 4
ZW = ZO + TP
PAD = TP - TOK
CH = 64
NCHUNK = PROMPT // CH
Q = 128
T_R, T_K, T_V, T_LR, T_GR = 0, 8, 16, 24, 25
T_U, T_VG, T_GG, T_GA, T_GB, NTILE = 33, 41, 49, 57, 73, 89
N_SHIFT = 25
LEVELS = (2, 4, 8, 16, 32)
RMS_EPS, LN_EPS, GN_EPS = 1e-6, 1e-5, 64e-5
DECAY = 0.6065306597126334

F32, F32R = mybir.dt.float32, mybir.dt.float32r
ALU, ACT = mybir.AluOpType, mybir.ActivationFunctionType
MUL, ADD, SUB = ALU.mult, ALU.add, ALU.subtract


def tile_of(dram, i):
    if isinstance(i, int):
        return dram[i]
    return dram[bass.ds(i, 1)].rearrange("o p c -> (o p) c")


def after(engine, sem, n):
    if not isinstance(n, int) or n > 0:
        engine.wait_ge(sem, n)


class Scope:

    def __init__(self, nc, stack):
        self.nc, self.stack, self.sems = nc, stack, []
        stack.callback(self.clear)

    def sb(self, name, shape, dt=F32):
        return self.stack.enter_context(self.nc.sbuf_tensor(name, shape, dt))

    def ps(self, name, shape):
        return self.stack.enter_context(self.nc.psum_tensor(name, shape, F32))

    def sem(self, name):
        self.sems.append(self.nc.alloc_semaphore(name))
        return self.sems[-1]

    def clear(self):
        self.nc.clear_and_free_semaphores(self.sems)
        self.nc.all_engine_barrier()


def pieces(ap):
    return ap.rearrange("p (c n) -> p c n", c=3)


class Gemm:

    def __init__(self, nc, sc, tag, wt, kts, xh, xl, koff):
        self.nc, self.wt, self.kts, self.xh, self.xl, self.koff = nc, wt, kts, xh, xl, koff
        self.raw = [sc.sb(f"{tag}_raw{s}", [P, kts * P]) for s in range(2)]
        self.wh = [sc.sb(f"{tag}_wh{s}", [P, kts * P], F32R) for s in range(2)]
        self.wl = [sc.sb(f"{tag}_wl{s}", [P, kts * P], F32R) for s in range(2)]
        self.acc = [sc.ps(f"{tag}_acc{s}", [P, 3, 512]) for s in range(2)]
        self.w_loaded = [sc.sem(f"{tag}_w_loaded{s}") for s in range(2)]
        self.hi_ready = [sc.sem(f"{tag}_hi_ready{s}") for s in range(2)]
        self.lo_ready = [sc.sem(f"{tag}_lo_ready{s}") for s in range(2)]
        self.group_done = [sc.sem(f"{tag}_group_done{s}") for s in range(2)]
        self.evacuated = [sc.sem(f"{tag}_evacuated{s}") for s in range(2)]
        self.x_ready = sc.sem(f"{tag}_x_ready")

    def load(self, sp, g, i, s):
        sp.wait_ge(self.lo_ready[s], i)
        sp.dma_start(self.raw[s][:, :], tile_of(self.wt, g)).then_inc(self.w_loaded[s], 16)

    def split(self, dve, i, s):
        dve.wait_ge(self.w_loaded[s], i * 16 + 16)
        dve.wait_ge(self.group_done[s], i)
        dve.tensor_copy(self.wh[s][:, :], self.raw[s][:, :]).then_inc(self.hi_ready[s], 1)
        dve.wait_ge(self.hi_ready[s], i + 1)
        dve.tensor_tensor(self.wl[s][:, :], self.raw[s][:, :], self.wh[s][:, :].bitcast(F32),
                          SUB).then_inc(self.lo_ready[s], 1)

    def products(self, pe, i, s, before=lambda k: None):
        pe.wait_ge(self.lo_ready[s], i + 1)
        pe.wait_ge(self.evacuated[s], i)
        for k in range(self.kts):
            before(k)
            kx = k + self.koff[s]
            pe.wait_ge(self.x_ready, kx + 1)
            for w, x in ((self.wh, self.xh), (self.wh, self.xl), (self.wl, self.xh)):
                for c in range(3):
                    mm = pe.matmul(self.acc[s][:, c, 0:NCH], w[s][:, k * P:(k + 1) * P],
                                   x[:, kx, c * NCH:(c + 1) * NCH],
                                   start=(k == 0 and w is self.wh and x is self.xh),
                                   stop=(k == self.kts - 1 and w is self.wl))
        mm.then_inc(self.group_done[s], 1)

    def sums(self, s):
        return self.acc[s][:, :, 0:NCH]


def in_slots(engine, groups, body):
    for s in range(2):
        body(s, 0, s)
    with engine.Fori(1, groups // 2) as i:
        for s in range(2):
            body(i * 2 + s, i, s)
    if groups % 2:
        body(groups - 1, groups // 2, 0)


def phase_in(nc, xT, norm_g, wt, z):
    with ExitStack() as stack:
        sc = Scope(nc, stack)
        xh = sc.sb("in_xh", [P, KT, TP], F32R)
        xl = sc.sb("in_xl", [P, KT, TP], F32R)
        gm = Gemm(nc, sc, "in", wt, KT, xh, xl, (0, 0))
        stage = [sc.sb(f"in_stage{s}", [P, ZW]) for s in range(2)]
        sqb = [b[:, ZO:ZW] for b in stage]
        g_sb = sc.sb("in_g", [P, KT])
        eps = sc.sb("in_eps", [P, 1])
        ones = sc.sb("in_ones", [P, P])
        rstd = sc.sb("in_rstd", [P, TP])
        xr = [sc.sb(f"in_x{n}", [P, TP]) for n in range(2)]
        ring = [xr[0][:, :], xr[1][:, :], rstd[:, :], gm.raw[1][:, 0:TP]]
        x_loaded = [sc.sem(f"in_x_loaded{n}") for n in range(4)]
        g_loaded, const_ready = sc.sem("in_g_loaded"), sc.sem("in_const_ready")
        sq_ready, sq_summed = sc.sem("in_sq_ready"), sc.sem("in_sq_summed")
        rt_ready, rstd_ready, xh_ready = sc.sem("in_rt_ready"), sc.sem("in_rstd_ready"), sc.sem("in_xh_ready")
        stored = [sc.sem(f"in_stored{s}") for s in range(2)]
        turns = NTILE // 2
        x = lambda n: ring[n % 4]

        with nc.Block() as block:
            @block.sync
            def _(sp):
                sp.dma_start(g_sb[:, :], norm_g).then_inc(g_loaded, 16)
                gm.load(sp, 0, 0, 0)
                for n in range(KT):
                    if n >= 4:
                        sp.wait_ge(gm.x_ready, n - 3)
                        sp.wait_ge(sq_ready, n - 3)
                    sp.dma_start(x(n)[:, 0:TOK], xT[n]).then_inc(x_loaded[n % 4], 16)
                sp.wait_ge(gm.x_ready, KT)
                sp.wait_ge(sq_ready, KT)
                gm.load(sp, 1, 0, 1)
                with sp.Fori(1, turns) as i:
                    for s in range(2):
                        gm.load(sp, i * 2 + s, i, s)
                if NTILE % 2:
                    gm.load(sp, NTILE - 1, turns, 0)

            @block.gpsimd
            def _(pool):
                pool.memset(ones[:, :], 1.0 / D_MODEL).then_inc(const_ready, 1)
                pool.memset(eps[:, :], RMS_EPS).then_inc(const_ready, 1)
                pool.memset(stage[0][:, 0:ZO], 0.0).then_inc(const_ready, 1)
                pool.memset(stage[1][:, 0:ZO], 0.0).then_inc(const_ready, 1)
                for b in ring:
                    pool.memset(b[:, TOK:TP], 0.0).then_inc(const_ready, 1)

            @block.scalar
            def _(act):
                act.wait_ge(const_ready, 8)
                for n in range(KT):
                    act.wait_ge(x_loaded[n % 4], 16 * (n // 4 + 1))
                    if n >= 2:
                        act.wait_ge(sq_summed, n - 1)
                    nc.scalar.activation(sqb[n % 2], x(n), ACT.Square).then_inc(sq_ready, 1)
                act.wait_ge(sq_summed, KT)
                act.wait_ge(gm.x_ready, KT)
                nc.scalar.activation(pieces(rstd[:, :]), gm.sums(1), ACT.Sqrt, bias=eps[:, 0:1]).then_inc(rt_ready, 1)

                def store(g, i, s):
                    act.wait_ge(gm.evacuated[s], i + 1)
                    act.dma_start(tile_of(z, g), stage[s][:, :]).then_inc(stored[s], 16)

                in_slots(act, NTILE, store)
                act.wait_ge(stored[0], 16 * (NTILE - turns))
                act.wait_ge(stored[1], 16 * turns)

            @block.vector
            def _(dve):
                gm.split(dve, 0, 0)
                dve.wait_ge(const_ready, 8)
                dve.wait_ge(g_loaded, 16)
                for n in range(KT):
                    dve.wait_ge(x_loaded[n % 4], 16 * (n // 4 + 1))
                    dve.tensor_scalar(xh[:, n, :], x(n), g_sb[:, n:n + 1], None, MUL).then_inc(xh_ready, 1)
                    dve.wait_ge(xh_ready, n + 1)
                    dve.scalar_tensor_tensor(xl[:, n, :], x(n), g_sb[:, n:n + 1], xh[:, n, :].bitcast(F32), MUL,
                                             SUB).then_inc(gm.x_ready, 1)
                gm.split(dve, 0, 1)
                dve.wait_ge(rt_ready, 1)
                dve.reciprocal(rstd[:, :], rstd[:, :]).then_inc(rstd_ready, 1)
                dve.wait_ge(rstd_ready, 1)

                def evacuate(i, s):
                    dve.wait_ge(gm.group_done[s], i + 1)
                    dve.wait_ge(stored[s], i * 16)
                    dve.tensor_tensor(pieces(stage[s][:, ZO:ZW]), gm.sums(s), pieces(rstd[:, :]),
                                      MUL).then_inc(gm.evacuated[s], 1)

                def turn(i):
                    for s in range(2):
                        evacuate(i, s)
                        gm.split(dve, i + 1, s)

                turn(0)
                with dve.Fori(1, turns - 1) as i:
                    turn(i)
                evacuate(turns - 1, 0)
                if NTILE % 2:
                    gm.split(dve, turns, 0)
                evacuate(turns - 1, 1)
                if NTILE % 2:
                    evacuate(turns, 0)

            @block.tensor
            def _(pe):
                pe.wait_ge(const_ready, 1)

                def sum_squares(n):
                    pe.wait_ge(sq_ready, n + 1)
                    for c in range(3):
                        mm = pe.matmul(gm.acc[1][:, c, 0:NCH], ones[:, :], sqb[n % 2][:, c * NCH:(c + 1) * NCH],
                                       start=(n == 0), stop=(n == KT - 1))
                    mm.then_inc(sq_summed, 1)

                gm.products(pe, 0, 0, sum_squares)
                pe.wait_ge(rt_ready, 1)
                gm.products(pe, 0, 1)
                with pe.Fori(1, turns) as i:
                    for s in range(2):
                        gm.products(pe, i, s)
                if NTILE % 2:
                    gm.products(pe, turns, 0)


def phase_rwkv(nc, z, lowrank, lr_bias, mu, par, shiftT, stateT, yT, shift_out, swkv_out, pwkv_out):
    with ExitStack() as stack:
        sc = Scope(nc, stack)
        sb, sem = sc.sb, sc.sem
        H2 = slice(0, HEAD), slice(HEAD, P)
        FOUR = slice(0, 4), slice(4, 8)
        NH = 2 * PAIRS
        two = lambda name, shape: [sb(f"{name}{n}", shape) for n in range(2)]
        big = lambda name: sb(name, [P, PAIRS, CH])

        zin = sb("zin", [P, N_SHIFT, CH + 1])
        gin = sb("gin", [P, PAIRS, CH])
        mix = sb("mix", [P, N_SHIFT, CH])
        r, k = mix[:, T_R:T_K, :], mix[:, T_K:T_V, :]
        v_pad = sb("v_pad", [P, PAIRS, 2 * CH])
        v = v_pad[:, :, CH:2 * CH]
        lr = sb("lr", [P, 2, CH])
        swa, cum, cum1 = sb("swa", [P, 2, PAIRS, CH]), big("cum"), big("cum1")
        sw, sa = swa[:, 0, :, :], swa[:, 1, :, :]
        ep, en, em = big("ep"), big("en"), big("em")
        kk, sq = big("kk"), big("sq")
        nrm, rn, rnx = sb("nrm", [NH, CH]), sb("rn", [NH, CH]), sb("rnx", [NH, PAIRS, CH])
        k2, rk, bsa, bv, gs = big("k2"), big("rk"), big("bsa"), big("bv"), big("gs")
        bk = sb("bk", [P, PAIRS, 2, CH])
        bkw = sb("bkw", [P, PAIRS, 2, CH])
        ar = two("ar", [P, PAIRS, 2, 2, CH])
        m = two("m", [P, PAIRS, 2, 2, CH])
        at, t = sb("at", [P, PAIRS, P]), sb("t", [P, PAIRS, P])
        tt = two("tt", [P, PAIRS, P])
        pl = [sb(f"p{b}", [P, PAIRS, P]) for b in LEVELS]
        bkt = two("bkt", [P, PAIRS, P])
        zz = two("zz", [P, PAIRS, P])
        xst = sb("xst", [P, PAIRS, HEAD])
        st, stw = sb("st", [P, PAIRS, HEAD]), sb("stw", [P, PAIRS, HEAD])
        bonus, gate, wc = two("bonus", [P, PAIRS, CH]), two("gate", [P, PAIRS, CH]), two("wc", [P, PAIRS, BATCH])
        y, ysq, yo = big("y"), big("ysq"), big("yo")
        sd, rs, rsx = sb("sd", [NH, CH]), sb("rs", [NH, CH]), sb("rsx", [NH, PAIRS, CH])
        ident, avg = sb("ident", [P, P]), sb("avg", [P, P])
        ones = sb("ones", [P, P])
        hsum = sb("hsum", [P, PAIRS, NH])
        of_pair, to_head = sb("of_pair", [NH, PAIRS]), sb("to_head", [NH, P])
        mask = sb("mask", [P, 2, CH])
        lmask = [sb(f"lmask{b}", [P, 4 * CH]) for b in LEVELS]
        diag2 = sb("diag2", [P, P])
        reset = sb("reset", [P, PAIRS * CH])
        eps = sb("gn_eps", [P, 1])
        lrw, lrb, lr_one = sb("lrw", [P, D_R]), sb("lrb", [2, D_R]), sb("lr_one", [2, 2, CH])
        mu_sb, par_sb = sb("mu_sb", [P, N_SHIFT]), sb("par_sb", [P, 5, PAIRS])
        k_k, k_a, r_k, lnx_g, lnx_b = (
            par_sb[:, n, :].unsqueeze(2).broadcast_to([P, PAIRS, CH]) for n in range(5))
        sts = sb("sts", [P, BATCH, PAIRS, HEAD])
        zprev = sb("zprev", [P, N_SHIFT, BATCH])
        amask = [pl[2 + n][:, :, :].rearrange("p u (h c) -> p h u c", h=2) for n in range(2)]
        zmask = [pl[4], t]
        cmask, rmask = sb("cmask", [P, BATCH, CH]), sb("rmask", [P, BATCH])
        sh_out = sb("sh_out", [P, N_SHIFT, 1 + BATCH])

        bank = [sc.ps(f"bank{n}", [P, 512]) for n in range(8)]
        L0, L1, L2, L3, E0, E1, B0, B1 = range(8)
        by = lambda n, j: bank[n][:, :].rearrange("p (j c) -> p j c", j=j)
        MM, LL, LT, EE, BB = (L0, L1, L2, L3), (L0, L2), (L1, L3), (E0, E1), (B0, B1)

        zin_loaded, gin_loaded, par_loaded = sem("zin_loaded"), sem("gin_loaded"), sem("par_loaded")
        zprev_loaded, sts_loaded = sem("zprev_loaded"), sem("sts_loaded")
        filled, masks_ready, const_ready = sem("filled"), sem("masks_ready"), sem("const_ready")
        smasks_ready, rnx_ready = sem("smasks_ready"), sem("rnx_ready")
        diff_ready, lrs_ready, scaled_ready, mix_ready = sem("diff_ready"), sem("lrs_ready"), sem("scaled_ready"), sem("mix_ready")
        lrmix_ready, lr_ready, wa_done, sig_ready = sem("lrmix_ready"), sem("lr_ready"), sem("wa_done"), sem("sig_ready")
        cum_ready, cum1_ready, exp_ready = sem("cum_ready"), sem("cum1_ready"), sem("exp_ready")
        kkr_ready, sq_ready, ss_done, nrm_ready = sem("kkr_ready"), sem("sq_ready"), sem("ss_done"), sem("nrm_ready")
        clamp_ready, rn_ready, rnb_done, kk_ready = sem("clamp_ready"), sem("rn_ready"), sem("rnb_done"), sem("kk_ready")
        t1_ready, k2_ready, rk_ready, bsa_ready = sem("t1_ready"), sem("k2_ready"), sem("rk_ready"), sem("bsa_ready")
        rkp_ready, rsx_ready, yg_ready = sem("rkp_ready"), sem("rsx_ready"), sem("yg_ready")
        b_ready, k_ready, ar_ready = sem("b_ready"), sem("k_ready"), sem("ar_ready")
        vt_done, zv_ready, bonus_done, bv_ready, bonus_ready = (
            sem("vt_done"), sem("zv_ready"), sem("bonus_done"), sem("bv_ready"), sem("bonus_ready"))
        gs_ready, gate_ready, wc_ready = sem("gs_ready"), sem("gate_ready"), sem("wc_ready")
        m_done, m_ready, at_ready = sem("m_done"), sem("m_ready"), sem("at_ready")
        bkw_ready, bkt_done, bkt_ready = sem("bkw_ready"), sem("bkt_done"), sem("bkt_ready")
        tt_ready, t_done, t_ready = sem("tt_ready"), sem("t_done"), sem("t_ready")
        lp_done, lp_ready, lt_done, ltt_done = sem("lp_done"), sem("lp_ready"), sem("lt_done"), sem("ltt_done")
        lt_ready, ltt_ready = sem("lt_ready"), sem("ltt_ready")
        x_done, x_ready, u_done, u_ready = sem("x_done"), sem("x_ready"), sem("u_done"), sem("u_ready")
        s_done, stw_ready, st_ready, y_done = sem("s_done"), sem("stw_ready"), sem("st_ready"), sem("y_done")
        y_ready, mean_done, yc_ready, ysq_ready = sem("y_ready"), sem("mean_done"), sem("yc_ready"), sem("ysq_ready")
        var_done, sd_ready, rs_ready, rsb_done = sem("var_done"), sem("sd_ready"), sem("rs_ready"), sem("rsb_done")
        yn_ready, yv_ready, yo_ready, y_stored = sem("yn_ready"), sem("yv_ready"), sem("yo_ready"), sem("y_stored")
        amask_ready, xs_pair, zmask_ready = sem("amask_ready"), sem("xs_pair"), sem("zmask_ready")
        shift_ready, state_stored = sem("shift_ready"), sem("state_stored")

        NL = len(LEVELS)
        SMP = NCHUNK
        flat = lambda ap: ap.rearrange("p u c -> p (u c)")

        def last_level(c):
            return LEVELS.index(STEPS // 2) if is_sample(c) else NL - 1

        def is_sample(c):
            return isinstance(c, int) and c == SMP

        def halves_of(ap, b):
            w = ap.rearrange("p u (n h b) -> p (u n) h b", h=2, b=b)
            return w[:, :, 0, :], w[:, :, 1, :]

        def pb(buffers, c):
            return buffers[parity(c)]

        def parity(c):
            return c % 2 if isinstance(c, int) else par_of[id(c)]

        par_of = {}

        def sync_load(sp, c):
            if is_sample(c):
                z_at, g_at = ZO + PROMPT - 1, ZO + PROMPT
            elif isinstance(c, int):
                z_at, g_at = c * CH + (ZO - 1), c * CH + ZO
            else:
                z_at, g_at = sp.snap(c * CH + (ZO - 1)), sp.snap(c * CH + ZO)
            cols = (lambda at, n: slice(at, at + n)) if isinstance(c, int) else bass.ds
            after(sp, mix_ready, c * 2)
            sp.dma_start(zin[:, :, :], z[0:N_SHIFT, :, cols(z_at, CH + 1)].rearrange("n p c -> p n c")
                         ).then_inc(zin_loaded, 16)
            if is_sample(c):
                sp.dma_start(zprev[:, :, :], shiftT).then_inc(zprev_loaded, 16)
            after(sp, gate_ready, c)
            sp.dma_start(gin[:, :, :], z[T_GR:T_GR + PAIRS, :, cols(g_at, CH)].rearrange("n p c -> p n c")
                         ).then_inc(gin_loaded, 16)

        def v_diff(dve, c):
            cur = zin[:, :, 1:CH + 1]
            dve.wait_ge(zin_loaded, c * 16 + 16)
            if is_sample(c):
                c4 = cur.rearrange("p n (b t) -> p n b t", b=BATCH)
                m4 = mix[:, :, :].rearrange("p n (b t) -> p n b t", b=BATCH)
                dve.wait_ge(zprev_loaded, 16)
                dve.tensor_copy(sh_out[:, :, 0:1], zin[:, :, 0:1]).then_inc(shift_ready, 1)
                dve.tensor_copy(sh_out[:, :, 1:1 + BATCH], c4[:, :, :, STEPS - 1]).then_inc(shift_ready, 1)
                dve.tensor_tensor(m4[:, :, :, 0], zprev[:, :, :], c4[:, :, :, 0], SUB).then_inc(shift_ready, 1)
                dve.wait_ge(shift_ready, 3)
                dve.tensor_tensor(m4[:, :, :, 1:STEPS], c4[:, :, :, 0:STEPS - 1], c4[:, :, :, 1:STEPS],
                                  SUB).then_inc(diff_ready, 1)
            else:
                dve.tensor_tensor(mix[:, :, :], zin[:, :, 0:CH], cur, SUB).then_inc(diff_ready, 1)
            dve.wait_ge(diff_ready, c + 1)
            dve.tensor_scalar(mix[:, T_LR, :], mix[:, T_LR, :], mu_sb[:, T_LR:T_LR + 1], None, MUL).then_inc(lrs_ready, 1)
            dve.wait_ge(lrs_ready, c + 1)
            dve.tensor_tensor(mix[:, T_LR, :], mix[:, T_LR, :], cur[:, T_LR, :], ADD).then_inc(lrmix_ready, 1)

        def p_scale(pool, c):
            pool.wait_ge(diff_ready, c + 1)
            pool.tensor_tensor(mix[:, 0:T_LR, :], mix[:, 0:T_LR, :],
                               mu_sb[:, 0:T_LR].unsqueeze(2).broadcast_to([P, T_LR, CH]), MUL).then_inc(scaled_ready, 1)

        def v_mix(dve, c):
            cur = zin[:, :, 1:CH + 1]
            dve.wait_ge(scaled_ready, c + 1)
            dve.tensor_tensor(mix[:, T_R:T_V, :], mix[:, T_R:T_V, :], cur[:, T_R:T_V, :], ADD).then_inc(mix_ready, 1)
            dve.tensor_tensor(v, mix[:, T_V:T_LR, :], cur[:, T_V:T_LR, :], ADD).then_inc(mix_ready, 1)

        def a_lowrank(act, c):
            act.wait_ge(lrmix_ready, c + 1)
            nc.scalar.activation(lr[0:HEAD, 0, :], mix[0:HEAD, T_LR, :], ACT.Tanh).then_inc(lr_ready, 1)
            nc.scalar.activation(lr[HEAD:P, 1, :], mix[HEAD:P, T_LR, :], ACT.Copy).then_inc(lr_ready, 1)

        def t_lowrank(pe, c):
            pe.wait_ge(lr_ready, c * 2 + 2)
            after(pe, bkt_ready, c * 2)
            for f in range(2):
                for p in range(4 * f, 4 * f + 4):
                    out, cols = by(EE[f], 4)[:, p % 4, :], slice(p * P, (p + 1) * P)
                    pe.matmul(out, lrw[:, cols], lr[:, :, :].rearrange("p j c -> p (j c)"), start=True, stop=False)
                    mm = pe.matmul(out, lrb[:, cols], lr_one[:, :, :].rearrange("p j c -> p (j c)"), start=False, stop=True)
                mm.then_inc(wa_done, 1)

        def a_sigmoids(act, c):
            for f in range(2):
                act.wait_ge(wa_done, c * 2 + f + 1)
                nc.scalar.activation(swa[:, :, FOUR[f], :].rearrange("p j u c -> p u j c"),
                                     bank[EE[f]][:, :].rearrange("p (u j c) -> p u j c", u=4, j=2),
                                     ACT.Sigmoid).then_inc(sig_ready, 1)

        def a_gate(act, c):
            act.wait_ge(gin_loaded, c * 16 + 16)
            nc.scalar.activation(gs[:, :, :], gin[:, :, :], ACT.Sigmoid).then_inc(gs_ready, 1)

        def v_scan(dve, c):
            if is_sample(c):
                dve.wait_ge(smasks_ready, 1)
            dve.wait_ge(sig_ready, c * 2 + 2)
            dve.tensor_tensor_scan(flat(cum[:, :, :]), reset[:, :], flat(sw), 0.0, MUL, ADD).then_inc(cum_ready, 1)

        def v_k(dve, c):
            dve.scalar_tensor_tensor(k2[:, :, :], sa, -1.0, k_a, ADD, MUL).then_inc(t1_ready, 1)
            dve.wait_ge(t1_ready, c + 1)
            dve.scalar_tensor_tensor(k2[:, :, :], k2[:, :, :], 1.0, k, ADD, MUL).then_inc(k2_ready, 1)

        def p_early(pool, c):
            pool.wait_ge(mix_ready, c * 2 + 1)
            pool.tensor_tensor(kk[:, :, :], k, k_k, MUL).then_inc(kkr_ready, 1)
            pool.wait_ge(cum_ready, c + 1)
            pool.tensor_tensor(cum1[:, :, :], cum[:, :, :], sw, SUB).then_inc(cum1_ready, 1)
            pool.wait_ge(k2_ready, c + 1)
            pool.tensor_tensor(rk[:, :, :], r, k2[:, :, :], MUL).then_inc(rk_ready, 1)
            pool.wait_ge(rk_ready, c + 1)
            pool.tensor_tensor(rk[:, :, :], rk[:, :, :], r_k, MUL).then_inc(rkp_ready, 1)
            pool.wait_ge(exp_ready, c * 3 + 2)
            pool.tensor_tensor(bk[:, :, 1, :], k2[:, :, :], en[:, :, :], MUL).then_inc(k_ready, 1)

        def a_exps(act, c):
            act.wait_ge(cum_ready, c + 1)
            nc.scalar.activation(ep[:, :, :], cum[:, :, :], ACT.Exp, scale=-DECAY).then_inc(exp_ready, 1)
            nc.scalar.activation(en[:, :, :], cum[:, :, :], ACT.Exp, scale=DECAY).then_inc(exp_ready, 1)
            act.wait_ge(cum1_ready, c + 1)
            nc.scalar.activation(em[:, :, :], cum1[:, :, :], ACT.Exp, scale=-DECAY).then_inc(exp_ready, 1)

        def a_square(act, c):
            act.wait_ge(kkr_ready, c + 1)
            nc.scalar.activation(sq[:, :, :], kk[:, :, :], ACT.Square).then_inc(sq_ready, 1)

        def t_sumsq(pe, c):
            pe.wait_ge(sq_ready, c + 1)
            pe.wait_ge(sig_ready, c * 2 + 1)
            for p in range(PAIRS):
                mm = pe.matmul(bank[E0][0:NH, 0:CH], hsum[:, p, :], sq[:, p, :], start=(p == 0), stop=(p == PAIRS - 1))
            mm.then_inc(ss_done, 1)

        def a_norm(act, c):
            act.wait_ge(ss_done, c + 1)
            nc.scalar.activation(nrm[:, :], bank[E0][0:NH, 0:CH], ACT.Sqrt).then_inc(nrm_ready, 1)

        def v_norm(dve, c):
            dve.wait_ge(nrm_ready, c + 1)
            dve.tensor_scalar(nrm[:, :], nrm[:, :], 1e-12, None, ALU.max).then_inc(clamp_ready, 1)
            dve.wait_ge(clamp_ready, c + 1)
            dve.reciprocal(rn[:, :], nrm[:, :]).then_inc(rn_ready, 1)
            dve.wait_ge(rn_ready, c + 1)
            dve.tensor_tensor(rnx[:, :, :], rn[:, :].unsqueeze(1).broadcast_to([NH, PAIRS, CH]),
                              of_pair[:, :].unsqueeze(2).broadcast_to([NH, PAIRS, CH]), MUL).then_inc(rnx_ready, 1)

        def t_spread_norm(pe, c):
            pe.wait_ge(rnx_ready, c + 1)
            pe.wait_ge(sig_ready, c * 2 + 2)
            pe.matmul(bank[E1][:, :], to_head[:, :], flat(rnx[:, :, :]), start=True, stop=True).then_inc(rnb_done, 1)

        def t_bonus(pe, c):
            pe.wait_ge(rkp_ready, c + 1)
            pe.wait_ge(nrm_ready, c + 1)
            pe.matmul(bank[E0][:, :], ones[:, :], flat(rk[:, :, :]), start=True, stop=True).then_inc(bonus_done, 1)

        def v_kk(dve, c):
            dve.wait_ge(rnb_done, c + 1)
            dve.tensor_tensor(kk[:, :, :], kk[:, :, :], by(E1, PAIRS), MUL).then_inc(kk_ready, 1)
            dve.wait_ge(kk_ready, c + 1)
            dve.tensor_tensor(bsa[:, :, :], kk[:, :, :], sa, MUL).then_inc(bsa_ready, 1)

        def v_ar(dve, c, h):
            a = pb(ar, c)
            dve.wait_ge(exp_ready, c * 3 + 3)
            after(dve, y_done, c - 1)
            dve.scalar_tensor_tensor(a[H2[h], :, h, 0, :], kk[H2[h], :, :], -1.0, em[H2[h], :, :],
                                     MUL, MUL).then_inc(ar_ready, 1)
            dve.tensor_tensor(a[H2[h], :, h, 1, :], r[H2[h], :, :], ep[H2[h], :, :], MUL).then_inc(ar_ready, 1)

        def v_b(dve, c):
            dve.wait_ge(bonus_done, c + 1)
            after(dve, bonus_ready, c)
            dve.tensor_tensor(bv[:, :, :], by(E0, PAIRS), v, MUL).then_inc(bv_ready, 1)
            dve.wait_ge(bsa_ready, c + 1)
            after(dve, bkw_ready, c * 2)
            dve.tensor_tensor(bk[:, :, 0, :], bsa[:, :, :], en[:, :, :], MUL).then_inc(b_ready, 1)

        def t_values(pe, c):
            pe.wait_ge(mix_ready, c * 2 + 2)
            pe.wait_ge(bv_ready, c + 1)
            for f in range(2):
                for p in range(4 * f, 4 * f + 4):
                    mm = pe.transpose(by(EE[f], 4)[:, p % 4, :], v_pad[:, p, :], ident[:, :])
                mm.then_inc(vt_done, 1)

        def t_m(pe, c):
            a = pb(ar, c)
            pe.wait_ge(b_ready, c + 1)
            pe.wait_ge(k_ready, c + 1)
            pe.wait_ge(ar_ready, c * 4 + 4)
            after(pe, ltt_ready, c * 2 * NL)
            for q in range(4):
                for p in (2 * q, 2 * q + 1):
                    mm = pe.matmul(bank[MM[q]][:, (p % 2) * 256:(p % 2) * 256 + 256],
                                   bk[:, p, :, :].rearrange("p j c -> p (j c)"),
                                   a[:, p, :, :, :].rearrange("p h j c -> p (h j c)"), start=True, stop=True)
                mm.then_inc(m_done, 1)

        def a_values(act, c):
            for f in range(2):
                act.wait_ge(vt_done, c * 2 + f + 1)
                after(act, s_done, c * 2 - 2)
                nc.scalar.activation(pb(zz, c)[:, FOUR[f], :], by(EE[f], 4), ACT.Copy).then_inc(zv_ready, 1)

        def v_mask(dve, c):
            msk = mask[:, :, :].rearrange("p j c -> p (j c)").unsqueeze(1).broadcast_to([P, 4, P])
            if is_sample(c):
                dve.wait_ge(smasks_ready, 5)
            after(dve, u_done, c * 2 - 2)
            for q in range(4):
                dve.wait_ge(m_done, c * 4 + q + 1)
                dve.tensor_tensor(pb(m, c)[:, 2 * q:2 * q + 2, :, :, :].rearrange("p u h j c -> p (u h) (j c)"),
                                  by(MM[q], 4), msk, MUL).then_inc(m_ready, 1)

        def v_at(dve, c):
            eye = ident[H2[0], H2[0]].unsqueeze(1).broadcast_to([HEAD, PAIRS, HEAD])
            dve.wait_ge(m_ready, c * 4 + 4)
            for h in range(2):
                dve.tensor_tensor(at[H2[h], :, H2[h]], pb(m, c)[H2[0], :, h, 0, :], eye, ADD).then_inc(at_ready, 1)

        def p_mid(pool, c):
            pool.wait_ge(b_ready, c + 1)
            pool.wait_ge(k_ready, c + 1)
            after(pool, bkt_done, c * 2)
            for j in range(2):
                if is_sample(c):
                    split = lambda ap: ap.rearrange("p u (b t) -> p u b t", t=STEPS)
                    pool.tensor_tensor(split(bkw[:, :, j, :]), split(bk[:, :, j, :]),
                                       split(ep[:, :, :])[:, :, :, STEPS - 1:STEPS].broadcast_to(
                                           [P, PAIRS, BATCH, STEPS]), MUL).then_inc(bkw_ready, 1)
                else:
                    pool.tensor_tensor(bkw[:, :, j, :], bk[:, :, j, :], ep[:, :, CH - 1:CH].broadcast_to([P, PAIRS, CH]),
                                       MUL).then_inc(bkw_ready, 1)
            pool.wait_ge(gs_ready, c + 1)
            after(pool, yo_ready, c - 1)
            pool.tensor_tensor(pb(gate, c)[:, :, :], gs[:, :, :], gin[:, :, :], MUL).then_inc(gate_ready, 1)
            pool.wait_ge(bv_ready, c + 1)
            after(pool, yv_ready, c - 1)
            pool.tensor_tensor(pb(bonus, c)[:, :, :], bv[:, :, :], lnx_b, ADD).then_inc(bonus_ready, 1)

        def v_wc(dve, c):
            after(dve, stw_ready, c - 1)
            src = ep[:, :, :].rearrange("p u (b t) -> p u b t", t=STEPS)[:, :, :, STEPS - 1]
            dve.tensor_copy(pb(wc, c)[:, :, :], src).then_inc(wc_ready, 1)

        def t_bkt(pe, c):
            pe.wait_ge(bkw_ready, c * 2 + 2)
            for f in range(2):
                pe.wait_ge(zv_ready, c * 2 + f + 1)
                for p in range(4 * f, 4 * f + 4):
                    mm = pe.transpose(by(EE[f], 4)[:, p % 4, :], bkw[:, p, :, :].rearrange("p j c -> p (j c)"), ident[:, :])
                mm.then_inc(bkt_done, 1)

        def a_bkt(act, c):
            for f in range(2):
                act.wait_ge(bkt_done, c * 2 + f + 1)
                nc.scalar.activation(pb(bkt, c)[:, FOUR[f], :], by(EE[f], 4), ACT.Copy).then_inc(bkt_ready, 1)

        def v_tt(dve, c):
            dve.wait_ge(at_ready, c * 2 + 2)
            dve.tensor_tensor(pb(tt, c)[:, :, :], at[:, :, :], diag2[:, :].unsqueeze(1).broadcast_to([P, PAIRS, P]),
                              MUL).then_inc(tt_ready, 1)

        def t_turn(pe, c):
            pe.wait_ge(tt_ready, c + 1)
            for f in range(2):
                for p in range(4 * f, 4 * f + 4):
                    mm = pe.transpose(by(LT[f], 4)[:, p % 4, :], pb(tt, c)[:, p, :], ident[:, :])
                mm.then_inc(t_done, 1)

        def a_turn(act, c):
            for f in range(2):
                act.wait_ge(t_done, c * 2 + f + 1)
                nc.scalar.activation(t[:, FOUR[f], :], by(LT[f], 4), ACT.Copy).then_inc(t_ready, 1)

        def t_level(pe, c, n):
            last = n == last_level(c)
            if n > last_level(c):
                return
            for f in range(2):
                if n == 0:
                    pe.wait_ge(t_ready, c * 2 + f + 1)
                else:
                    pe.wait_ge(lt_ready, (c * (NL - 1) + n) * 2 - 1 + f)
                for p in range(4 * f, 4 * f + 4):
                    mm = pe.matmul(by(LL[f], 4)[:, p % 4, :], at[:, p, :], t[:, p, :], start=True, stop=True)
                mm.then_inc(lp_done, 1)
            for f in range(2):
                pe.wait_ge(lp_ready, (c * NL + n) * 2 + f + 1)
                if n:
                    pe.wait_ge(ltt_ready, (c * NL + n) * 2 - 1 + f)
                if not last:
                    for p in range(4 * f, 4 * f + 4):
                        mm = pe.matmul(by(LL[f], 4)[:, p % 4, :], pb(tt, c)[:, p, :], pl[n][:, p, :], start=True, stop=True)
                    mm.then_inc(lt_done, 1)
                for p in range(4 * f, 4 * f + 4):
                    mm = pe.matmul(by(LT[f], 4)[:, p % 4, :], pl[n][:, p, :], pb(tt, c)[:, p, :], start=True, stop=True)
                mm.then_inc(ltt_done, 1)

        def v_level(dve, c, n):
            b, last = LEVELS[n], n == last_level(c)
            if n > last_level(c):
                return
            for f in range(2):
                dve.wait_ge(lp_done, (c * NL + n) * 2 + f + 1)
                dve.tensor_tensor(halves_of(pl[n][:, FOUR[f], :], b)[0], halves_of(by(LL[f], 4), b)[0],
                                  lmask[n][:, :].rearrange("p (n b) -> p n b", b=b), MUL).then_inc(lp_ready, 1)
            for f in range(2):
                if not last:
                    dst = halves_of(t[:, FOUR[f], :], b)[0]
                    dve.wait_ge(lt_done, (c * (NL - 1) + n) * 2 + f + 1)
                    dve.tensor_tensor(dst, dst, halves_of(by(LL[f], 4), b)[0], ADD).then_inc(lt_ready, 1)
                dst = halves_of(pb(tt, c)[:, FOUR[f], :], b)[1]
                dve.wait_ge(ltt_done, (c * NL + n) * 2 + f + 1)
                dve.tensor_tensor(dst, dst, halves_of(by(LT[f], 4), b)[1], ADD).then_inc(ltt_ready, 1)

        def t_rhs(pe, c):
            sample, a, mc, zc = is_sample(c), pb(ar, c), pb(m, c), pb(zz, c)
            after(pe, st_ready, c * 4)
            after(pe, yn_ready, c)
            if sample:
                pe.wait_ge(sts_loaded, 16)
            for f in range(2):
                for p in range(4 * f, 4 * f + 4):
                    if sample:
                        pe.wait_ge(amask_ready, 2 * p + 2)
                    for h in range(2):
                        out = by(BB[f], 4)[H2[0], p % 4, H2[h]]
                        if sample:
                            for b in range(BATCH):
                                mm = pe.matmul(out, amask[p % 2][:, h, b, :], sts[:, b, p, :], start=(b == 0), stop=False)
                            if h == 1:
                                mm.then_inc(xs_pair, 1)
                        else:
                            pe.matmul(out, a[:, p, h, 0, :], st[:, p, :], start=True, stop=False)
                        mm = pe.matmul(out, mc[:, p, h, 0, :], zc[:, p, H2[h]], start=False, stop=True)
                mm.then_inc(x_done, 1)

        def a_rhs(act, c):
            for f in range(2):
                act.wait_ge(x_done, c * 2 + f + 1)
                for h in range(2):
                    nc.scalar.activation(xst[H2[h], FOUR[f], :], by(BB[f], 4)[H2[0], :, H2[h]],
                                         ACT.Copy).then_inc(x_ready, 1)

        def t_u(pe, c):
            for f in range(2):
                pe.wait_ge(x_ready, c * 4 + 2 * f + 2)
                for p in range(4 * f, 4 * f + 4):
                    for h in range(2):
                        mm = pe.matmul(by(BB[f], 4)[H2[0], p % 4, H2[h]], pb(tt, c)[:, p, H2[h]], xst[:, p, :],
                                       start=True, stop=True)
                mm.then_inc(u_done, 1)

        def a_u(act, c):
            for f in range(2):
                act.wait_ge(u_done, c * 2 + f + 1)
                nc.scalar.activation(pb(zz, c)[H2[0], FOUR[f], :], by(BB[f], 4)[H2[0], :, :],
                                     ACT.Copy).then_inc(u_ready, 1)

        def t_y(pe, c):
            a, mc, zc = pb(ar, c), pb(m, c), pb(zz, c)
            pe.wait_ge(u_ready, c * 2 + 2)
            for h in range(2):
                for p in range(PAIRS):
                    out = by(B1, PAIRS)[H2[h], p, :]
                    if is_sample(c):
                        for b in range(BATCH):
                            e = slice(b * STEPS, (b + 1) * STEPS)
                            pe.matmul(out[:, e], sts[:, b, p, :], a[:, p, h, 1, e], start=True, stop=False)
                            mm = pe.matmul(out[:, e], zc[:, p, H2[h]], mc[:, p, h, 1, e], start=False, stop=True)
                    else:
                        pe.matmul(out, st[:, p, :], a[:, p, h, 1, :], start=True, stop=False)
                        mm = pe.matmul(out, zc[:, p, H2[h]], mc[:, p, h, 1, :], start=False, stop=True)
            mm.then_inc(y_done, 1)

        def t_state(pe, c):
            sample = is_sample(c)
            for b in range(BATCH if sample else 1):
                if sample:
                    pe.wait_ge(zmask_ready, b + 1)
                for f in range(2):
                    if f == 1 and b == 0:
                        pe.wait_ge(y_ready, c + 1)
                    if sample and b > 0:
                        pe.wait_ge(st_ready, (c + b) * 4 - 2 + 2 * f)
                    for p in range(4 * f, 4 * f + 4):
                        mm = pe.matmul(by(BB[f], 4)[:, p % 4, :], pb(bkt, c)[:, p, :],
                                       (zmask[b % 2] if sample else pb(zz, c))[:, p, :], start=True, stop=True)
                    mm.then_inc(s_done, 1)

        def v_decay(dve, c, b=0):
            src = sts[:, b, :, :] if is_sample(c) else st[:, :, :]
            after(dve, st_ready, (c + b) * 4)
            dve.wait_ge(wc_ready, c + 1)
            at_b = b if is_sample(c) else BATCH - 1
            dve.tensor_tensor(stw[:, :, :], src, pb(wc, c)[:, :, at_b:at_b + 1].broadcast_to([P, PAIRS, HEAD]),
                              MUL).then_inc(stw_ready, 1)

        def v_state(dve, c):
            for b in range(BATCH if is_sample(c) else 1):
                dst = sts[:, b, :, :] if is_sample(c) else st[:, :, :]
                if b > 0:
                    v_decay(dve, c, b)
                dve.wait_ge(stw_ready, c + b + 1)
                dve.wait_ge(y_done, c + 1)
                for f in range(2):
                    dve.wait_ge(s_done, (c + b) * 2 + f + 1)
                    for h in range(2):
                        dve.tensor_tensor(dst[H2[h], FOUR[f], :], stw[H2[h], FOUR[f], :],
                                          by(BB[f], 4)[H2[h], :, H2[h]], ADD).then_inc(st_ready, 1)

        def a_y(act, c):
            act.wait_ge(y_done, c + 1)
            after(act, yv_ready, c)
            nc.scalar.activation(y[:, :, :], by(B1, PAIRS), ACT.Copy).then_inc(y_ready, 1)

        def t_mean(pe, c):
            pe.wait_ge(y_ready, c + 1)
            if is_sample(c):
                pe.wait_ge(st_ready, (c + BATCH) * 4)
            else:
                pe.wait_ge(st_ready, c * 4 + 4)
            pe.matmul(bank[B0][:, :], avg[:, :], flat(y[:, :, :]), start=True, stop=True).then_inc(mean_done, 1)

        def v_center(dve, c):
            dve.wait_ge(mean_done, c + 1)
            dve.tensor_tensor(y[:, :, :], y[:, :, :], by(B0, PAIRS), SUB).then_inc(yc_ready, 1)

        def a_ysq(act, c):
            act.wait_ge(yc_ready, c + 1)
            nc.scalar.activation(ysq[:, :, :], y[:, :, :], ACT.Square).then_inc(ysq_ready, 1)

        def t_var(pe, c):
            pe.wait_ge(ysq_ready, c + 1)
            for p in range(PAIRS):
                mm = pe.matmul(bank[B0][0:NH, 0:CH], hsum[:, p, :], ysq[:, p, :], start=(p == 0), stop=(p == PAIRS - 1))
            mm.then_inc(var_done, 1)

        def a_sd(act, c):
            act.wait_ge(var_done, c + 1)
            nc.scalar.activation(sd[:, :], bank[B0][0:NH, 0:CH], ACT.Sqrt, scale=1.0 / HEAD,
                                 bias=eps[0:NH, 0:1]).then_inc(sd_ready, 1)

        def v_rs(dve, c):
            dve.wait_ge(sd_ready, c + 1)
            dve.reciprocal(rs[:, :], sd[:, :]).then_inc(rs_ready, 1)
            dve.wait_ge(rs_ready, c + 1)
            dve.tensor_tensor(rsx[:, :, :], rs[:, :].unsqueeze(1).broadcast_to([NH, PAIRS, CH]),
                              of_pair[:, :].unsqueeze(2).broadcast_to([NH, PAIRS, CH]), MUL).then_inc(rsx_ready, 1)

        def t_spread_sd(pe, c):
            pe.wait_ge(rsx_ready, c + 1)
            pe.matmul(bank[B0][:, :], to_head[:, :], flat(rsx[:, :, :]), start=True, stop=True).then_inc(rsb_done, 1)

        def v_scale(dve, c):
            dve.wait_ge(rsb_done, c + 1)
            dve.tensor_tensor(y[:, :, :], y[:, :, :], by(B0, PAIRS), MUL).then_inc(yn_ready, 1)

        def p_out(pool, c):
            pool.wait_ge(yn_ready, c + 1)
            pool.tensor_tensor(y[:, :, :], y[:, :, :], lnx_g, MUL).then_inc(yg_ready, 1)
            pool.wait_ge(yg_ready, c + 1)
            pool.wait_ge(bonus_ready, c + 1)
            pool.tensor_tensor(y[:, :, :], y[:, :, :], pb(bonus, c)[:, :, :], ADD).then_inc(yv_ready, 1)
            pool.wait_ge(yv_ready, c + 1)
            after(pool, y_stored, c * 16)
            pool.tensor_tensor(yo[:, :, :], y[:, :, :], pb(gate, c)[:, :, :], MUL).then_inc(yo_ready, 1)

        def a_store(act, c):
            dst = yT[:, :, PROMPT:TOK] if is_sample(c) else yT[:, :, c * CH:(c + 1) * CH] if isinstance(c, int) \
                else yT[:, :, bass.ds(c * CH, CH)]
            act.wait_ge(yo_ready, c + 1)
            act.dma_start(dst.rearrange("n p c -> p n c"), yo[:, :, :]).then_inc(y_stored, 16)

        def p_sample(pool):
            pool.wait_ge(ar_ready, (SMP + 1) * 4)
            for p in range(PAIRS):
                if p >= 2:
                    pool.wait_ge(xs_pair, p - 1)
                for h in range(2):
                    pool.tensor_tensor(amask[p % 2][:, h, :, :], pb(ar, SMP)[:, p, h, 0, :].unsqueeze(1).broadcast_to(
                        [P, BATCH, CH]), cmask[:, :, :], MUL).then_inc(amask_ready, 1)

        def a_sample(act):
            for b in range(BATCH):
                act.wait_ge(u_ready, (SMP + 1) * 2)
                if b >= 2:
                    act.wait_ge(s_done, (SMP + b - 1) * 2)
                nc.scalar.activation(zmask[b % 2][:, :, :], pb(zz, SMP)[:, :, :], ACT.Copy,
                                     scale=rmask[:, b:b + 1]).then_inc(zmask_ready, 1)

        def scalar_step(act, c, e, d):
            a_values(act, c)
            if d is not None:
                a_rhs(act, d)
                a_u(act, d)
            a_bkt(act, c)
            if d is not None:
                a_y(act, d)
            a_turn(act, c)
            if e is not None:
                scalar_early(act, e)
            if d is not None:
                a_ysq(act, d)
                a_sd(act, d)
                a_store(act, d)

        def scalar_early(act, e):
            a_lowrank(act, e)
            a_sigmoids(act, e)
            a_square(act, e)
            a_gate(act, e)
            a_norm(act, e)
            a_exps(act, e)

        def vector_step(dve, c, e, d):
            v_mask(dve, c)
            v_at(dve, c)
            v_tt(dve, c)
            v_wc(dve, c)
            if d is not None:
                v_decay(dve, d)
            if e is not None:
                v_diff(dve, e)
            v_level(dve, c, 0)
            if e is not None:
                v_mix(dve, e)
                v_scan(dve, e)
            if d is not None:
                v_state(dve, d)
            if e is not None:
                v_k(dve, e)
            v_level(dve, c, 1)
            if e is not None:
                v_norm(dve, e)
            if d is not None:
                v_center(dve, d)
            v_level(dve, c, 2)
            if e is not None:
                v_kk(dve, e)
                v_ar(dve, e, 0)
            v_level(dve, c, 3)
            if d is not None:
                v_rs(dve, d)
            if e is not None:
                v_ar(dve, e, 1)
            v_level(dve, c, 4)
            if e is not None:
                v_b(dve, e)
            if d is not None:
                v_scale(dve, d)

        def tensor_step(pe, c, e, d):
            t_values(pe, c)
            if d is not None:
                t_rhs(pe, d)
            t_m(pe, c)
            if d is not None:
                t_u(pe, d)
            t_bkt(pe, c)
            if d is not None:
                t_y(pe, d)
            t_turn(pe, c)
            t_level(pe, c, 0)
            if e is not None:
                t_lowrank(pe, e)
            if d is not None:
                t_state(pe, d)
            if e is not None:
                t_sumsq(pe, e)
            t_level(pe, c, 1)
            if d is not None:
                t_mean(pe, d)
            t_level(pe, c, 2)
            if d is not None:
                t_var(pe, d)
            if e is not None:
                t_spread_norm(pe, e)
                t_bonus(pe, e)
            t_level(pe, c, 3)
            t_level(pe, c, 4)
            if d is not None:
                t_spread_sd(pe, d)

        def pool_step(pool, c, e, d):
            p_mid(pool, c)
            if e is not None:
                p_scale(pool, e)
                if is_sample(e):
                    sample_reset(pool)
                p_early(pool, e)
                if is_sample(e):
                    sample_masks(pool)
            if d is not None:
                p_out(pool, d)

        def all_steps(engine, step):
            step(engine, 0, 1, None)
            step(engine, 1, 2, 0)
            with engine.Fori(1, (NCHUNK - 2) // 2) as j:
                for odd in range(2):
                    c, e, d = j * 2 + odd, j * 2 + (odd + 1), j * 2 + (odd - 1)
                    par_of.update({id(c): odd, id(e): 1 - odd, id(d): 1 - odd})
                    step(engine, c, e, d)
            for c in (NCHUNK - 2, NCHUNK - 1):
                step(engine, c, c + 1, c - 1)
            step(engine, SMP, None, SMP - 1)

        full = lambda b: b[tuple(slice(None) for _ in b.shape)]
        fills = ((ident, 0.0), (avg, 0.0), (ones, 0.0), (diag2, 0.0), (reset, 1.0), (eps, GN_EPS), (mask, 1.0),
                 (lr, 0.0), (lr_one, 1.0), (cmask, 0.0), (rmask, 1.0), (v_pad, 0.0), (ar[0], 0.0), (ar[1], 0.0),
                 (at, 0.0), (hsum, 0.0), (of_pair, 0.0), (to_head, 1.0),
                 *((x, 0.0) for x in pl), *((x, 1.0) for x in lmask))

        def constants(pool):
            for b, val in fills:
                pool.memset(full(b), val).then_inc(filled, 1)
            pool.wait_ge(filled, len(fills))
            steps = [0]

            def done(ins):
                ins.then_inc(masks_ready, 1)
                steps[0] += 1
                pool.wait_ge(masks_ready, steps[0])

            def select(ap, pattern, op, fill, base, cm):
                done(pool.affine_select(out=ap, in_=ap, pattern=pattern, compare_op=op, fill=fill, base=base,
                                        channel_multiplier=cm))

            select(ident[:, :], [[-1, P]], ALU.not_equal, 1.0, 0, 1)
            for h in range(2):
                done(pool.memset(avg[H2[h], H2[h]], 1.0 / HEAD))
                done(pool.memset(ones[H2[h], H2[h]], 1.0))
                for p in range(PAIRS):
                    done(pool.memset(hsum[H2[h], p, PAIRS * h + p:PAIRS * h + p + 1], 1.0))
                select(of_pair[:, :], [[-1, PAIRS]], ALU.not_equal, 1.0, -PAIRS * h, 1)
            th = to_head[:, :].rearrange("r (h c) -> r h c", h=2)
            select(th, [[-PAIRS, 2], [0, HEAD]], ALU.is_ge, 0.0, 0, 1)
            select(th, [[PAIRS, 2], [0, HEAD]], ALU.is_ge, 0.0, PAIRS - 1, -1)
            select(lr_one[:, :, :], [[-1, 2], [0, CH]], ALU.is_equal, 0.0, 0, 1)
            select(diag2[:, :], [[-1, P]], ALU.not_equal, 1.0, 1, 1)
            done(pool.memset(diag2[:, :].rearrange("p (n b) -> p n b", b=2)[:, :, 0], 0.0))
            select(diag2[:, :], [[-1, P]], ALU.not_equal, 1.0, 0, 1)
            done(pool.memset(reset[:, :].rearrange("p (n c) -> p n c", c=CH)[:, :, 0], 0.0))
            for rows in H2:
                select(mask[rows, 0, :], [[1, CH]], ALU.is_ge, 0.0, -1, -1)
                select(mask[rows, 1, :], [[1, CH]], ALU.is_ge, 0.0, 0, -1)
                select(rmask[rows, :], [[-STEPS, BATCH]], ALU.is_ge, 0.0, 0, 1)
                select(rmask[rows, :], [[STEPS, BATCH]], ALU.is_ge, 0.0, STEPS - 1, -1)
            for b in range(BATCH):
                done(pool.memset(cmask[:, b, b * STEPS:(b + 1) * STEPS], 1.0))
            for n, b in enumerate(LEVELS):
                select(lmask[n][:, :], [[0, 4], [-2 * b, CH // b], [0, b]], ALU.is_ge, 0.0, -b, 1)
                select(lmask[n][:, :], [[0, 4], [2 * b, CH // b], [0, b]], ALU.is_ge, 0.0, 2 * b - 1, -1)
            pool.memset(st[:, :, :], 0.0).then_inc(const_ready, 1)

        def sample_reset(pool):
            pool.wait_ge(cum_ready, NCHUNK)
            pool.memset(reset[:, :].rearrange("p (n c) -> p n c", c=STEPS)[:, :, 0], 0.0).then_inc(smasks_ready, 1)

        def sample_masks(pool):
            pool.wait_ge(m_ready, NCHUNK * 4)
            for n, (rows, j) in enumerate((rows, j) for rows in H2 for j in range(2)):
                pool.affine_select(out=mask[rows, j, :], in_=mask[rows, j, :], pattern=[[-STEPS, BATCH], [0, STEPS]],
                                   compare_op=ALU.is_ge, fill=0.0, base=0, channel_multiplier=1).then_inc(smasks_ready, 1)
                pool.wait_ge(smasks_ready, n + 2)

        with nc.Block() as block:
            @block.sync
            def _(sp):
                for dst, src in ((lrw[:, :], lowrank), (lrb[:, :], lr_bias), (mu_sb[:, :], mu), (par_sb[:, :, :], par)):
                    sp.dma_start(dst, src).then_inc(par_loaded, 16)
                sync_load(sp, 0)
                with sp.Fori(1, NCHUNK) as c:
                    sync_load(sp, c)
                sync_load(sp, SMP)
                sp.dma_start(sts[:, :, :, :], stateT).then_inc(sts_loaded, 16)
                sp.wait_ge(shift_ready, 3)
                sp.dma_start(shift_out, sh_out[:, :, :]).then_inc(state_stored, 16)
                sp.wait_ge(st_ready, NCHUNK * 4)
                sp.dma_start(pwkv_out, st[:, :, :]).then_inc(state_stored, 16)
                sp.wait_ge(st_ready, (NCHUNK + BATCH) * 4)
                sp.dma_start(swkv_out, sts[:, :, :, :]).then_inc(state_stored, 16)
                sp.wait_ge(state_stored, 48)
                sp.wait_ge(y_stored, (NCHUNK + 1) * 16)

            @block.gpsimd
            def _(pool):
                constants(pool)
                pool.wait_ge(const_ready, 1)
                pool.wait_ge(par_loaded, 64)
                p_scale(pool, 0)
                p_early(pool, 0)
                all_steps(pool, pool_step)
                p_sample(pool)
                p_out(pool, SMP)

            @block.scalar
            def _(act):
                act.wait_ge(const_ready, 1)
                scalar_early(act, 0)
                all_steps(act, scalar_step)
                a_rhs(act, SMP)
                a_u(act, SMP)
                a_y(act, SMP)
                a_sample(act)
                a_ysq(act, SMP)
                a_sd(act, SMP)
                a_store(act, SMP)

            @block.vector
            def _(dve):
                dve.wait_ge(par_loaded, 64)
                dve.wait_ge(const_ready, 1)
                v_diff(dve, 0)
                v_mix(dve, 0)
                v_scan(dve, 0)
                v_k(dve, 0)
                v_norm(dve, 0)
                v_kk(dve, 0)
                for h in range(2):
                    v_ar(dve, 0, h)
                v_b(dve, 0)
                all_steps(dve, vector_step)
                dve.wait_ge(sts_loaded, 16)
                v_decay(dve, SMP)
                v_state(dve, SMP)
                v_center(dve, SMP)
                v_rs(dve, SMP)
                v_scale(dve, SMP)

            @block.tensor
            def _(pe):
                pe.wait_ge(par_loaded, 64)
                pe.wait_ge(const_ready, 1)
                t_lowrank(pe, 0)
                t_sumsq(pe, 0)
                t_spread_norm(pe, 0)
                t_bonus(pe, 0)
                all_steps(pe, tensor_step)
                pe.wait_ge(ltt_ready, (SMP * NL + last_level(SMP) + 1) * 2)
                t_rhs(pe, SMP)
                t_u(pe, SMP)
                t_y(pe, SMP)
                t_state(pe, SMP)
                t_mean(pe, SMP)
                t_var(pe, SMP)
                t_spread_sd(pe, SMP)


def phase_sgu(nc, z, wT, bias, ln_par, sT, vn_out):
    with ExitStack() as stack:
        sc = Scope(nc, stack)
        sb, sem = sc.sb, sc.sem
        G = PAIRS
        vn = sb("vn", [P, G, TP])
        sqb = [sb(f"sgu_sq{n}", [P, TP]) for n in range(2)]
        rs = sb("sgu_rs", [P, TP])
        u, gg, sg = ([sb(f"sgu_{n}{j}", [P, TP]) for j in range(2)] for n in ("u", "g", "sg"))
        so = [sb(f"sgu_out{j}", [P, TP]) for j in range(2)]
        vt = [sb(f"sgu_vt{j}", [P, 4, Q]) for j in range(2)]
        wm, w8 = sb("sgu_wm", [P, G, Q]), sb("sgu_w8", [SAMPLE, G, SAMPLE])
        bb = sb("sgu_bb", [P, G, Q])
        lnp = sb("sgu_ln", [P, 2, G])
        ones, ident, eps = sb("sgu_ones", [P, P]), sb("sgu_ident", [P, P]), sb("sgu_eps", [P, 1])
        mean, var = sc.ps("sgu_mean", [P, 3, 512]), sc.ps("sgu_var", [P, 3, 512])
        mixed = [sc.ps(f"sgu_mixed{j}", [P, 512]) for j in range(2)]
        turned = [mean[:, j, :] for j in range(2)]

        vg_loaded = [sem(f"vg_loaded{n}") for n in range(G)]
        w_loaded, w8_loaded, w8_zero = sem("sgu_w_loaded"), sem("sgu_w8_loaded"), sem("sgu_w8_zero")
        const0, const_ready, w_ready = sem("sgu_const0"), sem("sgu_const_ready"), sem("sgu_w_ready")
        mean_done, vc_ready, sq_ready, sq_summed = sem("sgu_mean_done"), sem("vc_ready"), sem("sgu_sq_ready"), sem("sgu_sq_summed")
        rt_ready, rs_ready, vs_ready, vn_ready = sem("sgu_rt_ready"), sem("sgu_rs_ready"), sem("vs_ready"), sem("vn_ready")
        turn_done, vt_ready, mix_done, mix_read = sem("turn_done"), sem("vt_ready"), sem("sgu_mix_done"), sem("sgu_mix_read")
        ug_loaded = [sem(f"ug_loaded{j}") for j in range(2)]
        sig_ready, su_ready, gate_ready, out_ready = sem("sgu_sig_ready"), sem("su_ready"), sem("sgu_gate_ready"), sem("sgu_out_ready")
        stored, vn_stored = [sem(f"sgu_stored{j}") for j in range(2)], sem("vn_stored")
        cols = lambda j: slice(j * 512, (j + 1) * 512) if j < 2 else slice(PROMPT, TOK)

        with nc.Block() as block:
            @block.sync
            def _(sp):
                for n in range(G):
                    sp.dma_start(vn[:, n, :], z[T_VG + n, :, ZO:ZW]).then_inc(vg_loaded[n], 16)
                for n in range(G):
                    j = n % 2
                    if n >= 2:
                        sp.wait_ge(out_ready, n - 1)
                    sp.dma_start(u[j][:, :], z[T_U + n, :, ZO:ZW]).then_inc(ug_loaded[j], 16)
                    sp.dma_start(gg[j][:, :], z[T_GG + n, :, ZO:ZW]).then_inc(ug_loaded[j], 16)
                    if n >= 1:
                        sp.wait_ge(out_ready, n)
                        sp.dma_start(sT[n - 1, :, 0:TOK], so[1 - j][:, 0:TOK]).then_inc(stored[1 - j], 16)
                    if n == 1:
                        sp.wait_ge(vn_ready, G)
                        sp.dma_start(vn_out, vn[:, :, PROMPT:TOK]).then_inc(vn_stored, 16)
                sp.wait_ge(out_ready, G)
                sp.dma_start(sT[G - 1, :, 0:TOK], so[(G - 1) % 2][:, 0:TOK]).then_inc(stored[(G - 1) % 2], 16)
                for j in range(2):
                    sp.wait_ge(stored[j], G // 2 * 16)
                sp.wait_ge(vn_stored, 16)

            @block.gpsimd
            def _(pool):
                pool.dma_start(wm[:, :, :], wT.rearrange("g s t -> s g t")).then_inc(w_loaded, 16)
                pool.dma_start(bb[:, :, :], bias.unsqueeze(0).broadcast_to([P, G, Q])).then_inc(w_loaded, 16)
                pool.dma_start(lnp[:, :, :], ln_par).then_inc(w_loaded, 16)
                pool.memset(w8[:, :, :], 0.0).then_inc(w8_zero, 1)
                pool.memset(ones[:, :], 1.0 / D_G).then_inc(const_ready, 1)
                pool.memset(eps[:, :], LN_EPS).then_inc(const_ready, 1)
                pool.memset(ident[:, :], 0.0).then_inc(const0, 1)
                pool.wait_ge(const0, 1)
                pool.affine_select(out=ident[:, :], in_=ident[:, :], pattern=[[-1, P]], compare_op=ALU.not_equal,
                                   fill=1.0, base=0, channel_multiplier=1).then_inc(const_ready, 1)
                pool.wait_ge(w8_zero, 1)
                for b in range(BATCH):
                    e = slice(b * STEPS, (b + 1) * STEPS)
                    pool.dma_start(w8[e, :, e], wT[:, 0:STEPS, 0:STEPS].rearrange("g s t -> s g t")).then_inc(w8_loaded, 16)
                pool.wait_ge(w_loaded, 48)
                pool.wait_ge(const_ready, 3)
                pool.affine_select(out=wm[:, :, :], in_=wm[:, :, :], pattern=[[0, G], [1, Q]], compare_op=ALU.is_ge,
                                   fill=0.0, base=0, channel_multiplier=-1).then_inc(w_ready, 1)
                pool.wait_ge(w8_loaded, 16 * BATCH)
                pool.wait_ge(w_ready, 1)
                pool.affine_select(out=w8[:, :, :], in_=w8[:, :, :], pattern=[[0, G], [1, SAMPLE]], compare_op=ALU.is_ge,
                                   fill=0.0, base=0, channel_multiplier=-1).then_inc(w_ready, 1)
                for n in range(G):
                    j = n % 2
                    pool.wait_ge(sig_ready, n + 1)
                    pool.tensor_tensor(sg[j][:, 0:TOK], sg[j][:, 0:TOK], gg[j][:, 0:TOK], MUL).then_inc(gate_ready, 1)
                    pool.wait_ge(gate_ready, n + 1)
                    pool.wait_ge(su_ready, 3 * n + 3)
                    pool.tensor_tensor(so[j][:, 0:TOK], so[j][:, 0:TOK], sg[j][:, 0:TOK], MUL).then_inc(out_ready, 1)

            @block.scalar
            def _(act):
                for n in range(G):
                    act.wait_ge(vc_ready, n + 1)
                    if n >= 2:
                        act.wait_ge(sq_summed, n - 1)
                    nc.scalar.activation(sqb[n % 2][:, :], vn[:, n, :], ACT.Square).then_inc(sq_ready, 1)
                act.wait_ge(sq_summed, G)
                act.wait_ge(const_ready, 3)
                nc.scalar.activation(pieces(rs[:, :]), var[:, :, 0:NCH], ACT.Sqrt, bias=eps[:, 0:1]).then_inc(rt_ready, 1)
                act.wait_ge(w_loaded, 48)
                for n in range(G):
                    act.wait_ge(vs_ready, n + 1)
                    nc.scalar.activation(vn[:, n, :], vn[:, n, :], ACT.Identity, scale=lnp[:, 0, n:n + 1],
                                         bias=lnp[:, 1, n:n + 1]).then_inc(vn_ready, 1)
                for n in range(G):
                    act.wait_ge(ug_loaded[n % 2], 32 * (n // 2 + 1))
                    if n >= 2:
                        act.wait_ge(out_ready, n - 1)
                    nc.scalar.activation(sg[n % 2][:, 0:TOK], gg[n % 2][:, 0:TOK], ACT.Sigmoid).then_inc(sig_ready, 1)
                    for j in range(3):
                        e = 3 * n + j
                        act.wait_ge(turn_done, e + 1)
                        if e >= 2:
                            act.wait_ge(mix_done, e - 1)
                        if j < 2:
                            nc.scalar.activation(vt[e % 2][:, :, :].rearrange("p c t -> p (c t)"), turned[e % 2],
                                                 ACT.Copy).then_inc(vt_ready, 1)
                        else:
                            nc.scalar.activation(vt[e % 2][0:SAMPLE, 0, :], turned[e % 2][0:SAMPLE, 0:P],
                                                 ACT.Copy).then_inc(vt_ready, 1)

            @block.vector
            def _(dve):
                dve.wait_ge(mean_done, 1)
                for n in range(G):
                    dve.tensor_tensor(pieces(vn[:, n, :]), pieces(vn[:, n, :]), mean[:, :, 0:NCH], SUB).then_inc(vc_ready, 1)
                dve.wait_ge(rt_ready, 1)
                dve.reciprocal(rs[:, :], rs[:, :]).then_inc(rs_ready, 1)
                dve.wait_ge(rs_ready, 1)
                for n in range(G):
                    dve.tensor_tensor(vn[:, n, :], vn[:, n, :], rs[:, :], MUL).then_inc(vs_ready, 1)
                for n in range(G):
                    dve.wait_ge(ug_loaded[n % 2], 32 * (n // 2 + 1))
                    if n >= 2:
                        dve.wait_ge(stored[n % 2], n // 2 * 16)
                    for j in range(3):
                        e = 3 * n + j
                        dst, src = so[n % 2][:, cols(j)], mixed[e % 2][:, :]
                        dve.wait_ge(mix_done, e + 1)
                        if j < 2:
                            dst4 = dst.rearrange("p (c t) -> p c t", t=Q)
                            dve.tensor_tensor(dst4, src.rearrange("p (c t) -> p c t", t=Q),
                                              bb[:, n, :].unsqueeze(1).broadcast_to([P, 4, Q]), ADD).then_inc(mix_read, 1)
                        else:
                            dst4 = dst.rearrange("p (c t) -> p c t", t=STEPS)
                            dve.tensor_tensor(dst4, src[:, 0:SAMPLE].rearrange("p (c t) -> p c t", t=STEPS),
                                              bb[:, n, 0:STEPS].unsqueeze(1).broadcast_to([P, BATCH, STEPS]),
                                              ADD).then_inc(mix_read, 1)
                        dve.wait_ge(mix_read, e + 1)
                        dve.tensor_tensor(dst, dst, u[n % 2][:, cols(j)], MUL).then_inc(su_ready, 1)

            @block.tensor
            def _(pe):
                pe.wait_ge(const_ready, 3)
                for n in range(G):
                    pe.wait_ge(vg_loaded[n], 16)
                    for c in range(3):
                        mm = pe.matmul(mean[:, c, 0:NCH], ones[:, :], vn[:, n, c * NCH:(c + 1) * NCH],
                                       start=(n == 0), stop=(n == G - 1))
                mm.then_inc(mean_done, 1)
                for n in range(G):
                    pe.wait_ge(sq_ready, n + 1)
                    for c in range(3):
                        mm = pe.matmul(var[:, c, 0:NCH], ones[:, :], sqb[n % 2][:, c * NCH:(c + 1) * NCH],
                                       start=(n == 0), stop=(n == G - 1))
                    mm.then_inc(sq_summed, 1)
                pe.wait_ge(w_ready, 2)

                def turn(e):
                    n, j = e // 3, e % 3
                    pe.wait_ge(vn_ready, n + 1)
                    if e >= 2:
                        pe.wait_ge(vt_ready, e - 1)
                    if j < 2:
                        for c in range(4):
                            o = j * 512 + c * Q
                            mm = pe.transpose(turned[e % 2][:, c * Q:(c + 1) * Q], vn[:, n, o:o + Q], ident[:, :])
                    else:
                        mm = pe.transpose(turned[e % 2][0:SAMPLE, 0:P], vn[:, n, PROMPT:TOK], ident[:, :])
                    mm.then_inc(turn_done, 1)

                turn(0)
                for e in range(3 * G):
                    n, j = e // 3, e % 3
                    if e + 1 < 3 * G:
                        turn(e + 1)
                    pe.wait_ge(vt_ready, e + 1)
                    if e >= 2:
                        pe.wait_ge(mix_read, e - 1)
                    if j < 2:
                        for c in range(4):
                            mm = pe.matmul(mixed[e % 2][:, c * Q:(c + 1) * Q], vt[e % 2][:, c, :], wm[:, n, :],
                                           start=True, stop=True)
                    else:
                        mm = pe.matmul(mixed[e % 2][:, 0:SAMPLE], vt[e % 2][0:SAMPLE, 0, :], w8[:, n, :],
                                       start=True, stop=True)
                    mm.then_inc(mix_done, 1)


class Operand:

    RING = 4

    def __init__(self, sc, tag, tiles, xh, xl, gm, ring):
        self.tiles, self.xh, self.xl, self.gm = tiles, xh, xl, gm
        self.ring = [sc.sb(f"{tag}_xs{n}", [P, TP]) for n in range(ring)]
        self.loaded = [sc.sem(f"{tag}_x_loaded{n}") for n in range(ring)]
        self.xh_ready, self.pad_ready = sc.sem(f"{tag}_xh_ready"), sc.sem(f"{tag}_pad_ready")

    def load(self, engine):
        r = len(self.ring)
        for n, tile in enumerate(self.tiles):
            if n >= r:
                engine.wait_ge(self.gm.x_ready, n - r + 1)
            engine.dma_start(self.ring[n % r][:, 0:TOK], tile).then_inc(self.loaded[n % r], 16)

    def pad(self, engine):
        for b in self.ring:
            engine.memset(b[:, TOK:TP], 0.0).then_inc(self.pad_ready, 1)

    def split(self, dve):
        r = len(self.ring)
        dve.wait_ge(self.pad_ready, r)
        for n in range(len(self.tiles)):
            x = self.ring[n % r]
            dve.wait_ge(self.loaded[n % r], 16 * (n // r + 1))
            dve.tensor_copy(self.xh[:, n, :], x[:, :]).then_inc(self.xh_ready, 1)
            dve.wait_ge(self.xh_ready, n + 1)
            dve.tensor_tensor(self.xl[:, n, :], x[:, :], self.xh[:, n, :].bitcast(F32), SUB).then_inc(self.gm.x_ready, 1)


def phase_merge(nc, z, yT, sT, wt, mT):
    with ExitStack() as stack:
        sc = Scope(nc, stack)
        xh, xl = sc.sb("mg_xh", [P, KT, TP], F32R), sc.sb("mg_xl", [P, KT, TP], F32R)
        gm = Gemm(nc, sc, "mg", wt, KH, xh, xl, (0, KH))
        op = Operand(sc, "mg", [d[n, :, 0:TOK] for d in (yT, sT) for n in range(KH)], xh, xl, gm, 4)
        gate = [sc.sb(f"mg_gate{s}", [P, TP]) for s in range(2)]
        part = [sc.sb(f"mg_part{s}", [P, TP]) for s in range(2)]
        mo = sc.sb("mg_out", [P, TP])
        gate_loaded = [sc.sem(f"mg_gate_loaded{s}") for s in range(2)]
        sig_ready, part_ready = sc.sem("mg_sig_ready"), sc.sem("mg_part_ready")
        m_ready, stored = sc.sem("mg_m_ready"), sc.sem("mg_m_stored")

        with nc.Block() as block:
            @block.sync
            def _(sp):
                def load(g, i, s):
                    gm.load(sp, g, i, s)
                    sp.wait_ge(part_ready, i * 2)
                    sp.dma_start(gate[s][:, :], tile_of(z, i + (T_GA, T_GB)[s])[:, ZO:ZW]).then_inc(gate_loaded[s], 16)

                in_slots(sp, 2 * KT, load)

            @block.scalar
            def _(act):
                op.load(act)

                def step(g, i, s):
                    act.wait_ge(gate_loaded[s], i * 16 + 16)
                    nc.scalar.activation(gate[s][:, :], gate[s][:, :], ACT.Sigmoid).then_inc(sig_ready, 1)
                    act.wait_ge(gm.group_done[s], i + 1)
                    act.wait_ge(m_ready, i)
                    nc.scalar.activation(pieces(part[s][:, :]), gm.sums(s), ACT.Copy).then_inc(gm.evacuated[s], 1)
                    if s == 1:
                        act.wait_ge(m_ready, i + 1)
                        act.dma_start(tile_of(mT, i), mo[:, :]).then_inc(stored, 16)

                in_slots(act, 2 * KT, step)
                act.wait_ge(stored, KT * 16)

            @block.gpsimd
            def _(pool):
                op.pad(pool)

                def step(g, i, s):
                    pool.wait_ge(sig_ready, i * 2 + s + 1)
                    pool.wait_ge(gm.evacuated[s], i + 1)
                    pool.tensor_tensor(part[s][:, :], part[s][:, :], gate[s][:, :], MUL).then_inc(part_ready, 1)
                    if s == 1:
                        pool.wait_ge(part_ready, i * 2 + 2)
                        pool.wait_ge(stored, i * 16)
                        pool.tensor_tensor(mo[:, :], part[0][:, :], part[1][:, :], ADD).then_inc(m_ready, 1)

                in_slots(pool, 2 * KT, step)

            @block.vector
            def _(dve):
                for s in range(2):
                    gm.split(dve, 0, s)
                op.split(dve)
                with dve.Fori(1, KT) as i:
                    for s in range(2):
                        gm.split(dve, i, s)

            @block.tensor
            def _(pe):
                in_slots(pe, 2 * KT, lambda g, i, s: gm.products(pe, i, s))


def phase_out(nc, xT, mT, wt, hT, ssq_dram):
    with ExitStack() as stack:
        sc = Scope(nc, stack)
        xh, xl = sc.sb("out_xh", [P, KT, TP], F32R), sc.sb("out_xl", [P, KT, TP], F32R)
        gm = Gemm(nc, sc, "out", wt, KT, xh, xl, (0, 0))
        op = Operand(sc, "out", [mT[n, :, 0:TOK] for n in range(KT)], xh, xl, gm, 2)
        xr, h = op.ring
        sq, ssq = sc.sb("out_sq", [P, TP]), sc.sb("out_ssq", [P, TP])
        x_loaded, h_ready, sq_ready = sc.sem("out_xr_loaded"), sc.sem("h_ready"), sc.sem("out_sq_ready")
        ssq_ready, stored, ssq_stored = sc.sem("ssq_ready"), sc.sem("h_stored"), sc.sem("ssq_stored")

        with nc.Block() as block:
            @block.sync
            def _(sp):
                in_slots(sp, KT, lambda g, i, s: gm.load(sp, g, i, s))

            @block.scalar
            def _(act):
                op.load(act)
                act.wait_ge(gm.x_ready, KT)

                def step(g, i, s):
                    act.wait_ge(h_ready, g)
                    act.dma_start(xr[:, 0:TOK], tile_of(xT, g)).then_inc(x_loaded, 16)
                    act.wait_ge(gm.group_done[s], i + 1)
                    act.wait_ge(stored, g * 16)
                    act.wait_ge(sq_ready, g)
                    nc.scalar.activation(pieces(h[:, :]), gm.sums(s), ACT.Copy).then_inc(gm.evacuated[s], 1)
                    act.wait_ge(h_ready, g + 1)
                    act.dma_start(tile_of(hT, g), h[:, :]).then_inc(stored, 16)

                in_slots(act, KT, step)
                act.wait_ge(ssq_ready, KT + 1)
                act.dma_start(ssq_dram, ssq[:, :]).then_inc(ssq_stored, 16)
                act.wait_ge(stored, KT * 16)
                act.wait_ge(ssq_stored, 16)

            @block.gpsimd
            def _(pool):
                op.pad(pool)
                pool.memset(ssq[:, :], 0.0).then_inc(ssq_ready, 1)

                def step(g, i, s):
                    pool.wait_ge(x_loaded, g * 16 + 16)
                    pool.wait_ge(gm.evacuated[s], i + 1)
                    pool.tensor_tensor(h[:, :], h[:, :], xr[:, :], ADD).then_inc(h_ready, 1)
                    pool.wait_ge(h_ready, g + 1)
                    pool.wait_ge(ssq_ready, g + 1)
                    pool.tensor_tensor(sq[:, :], h[:, :], h[:, :], MUL).then_inc(sq_ready, 1)
                    pool.wait_ge(sq_ready, g + 1)
                    pool.tensor_tensor(ssq[:, :], ssq[:, :], sq[:, :], ADD).then_inc(ssq_ready, 1)

                in_slots(pool, KT, step)

            @block.vector
            def _(dve):
                for s in range(2):
                    gm.split(dve, 0, s)
                op.split(dve)
                with dve.Fori(1, KT // 2) as i:
                    for s in range(2):
                        gm.split(dve, i, s)

            @block.tensor
            def _(pe):
                in_slots(pe, KT, lambda g, i, s: gm.products(pe, i, s))


def phase_final(nc, hT, ssq_dram, final_g, outT):
    with ExitStack() as stack:
        sc = Scope(nc, stack)
        h = sc.sb("fin_h", [P, KT, TP])
        o = [sc.sb(f"fin_o{n}", [P, TP]) for n in range(4)]
        ssq, rs = sc.sb("fin_ssq", [P, TP]), sc.sb("fin_rs", [P, TP])
        g_sb, eps, ones = sc.sb("fin_g", [P, KT]), sc.sb("fin_eps", [P, 1]), sc.sb("fin_ones", [P, P])
        ms = sc.ps("fin_ms", [P, 3, 512])
        h_loaded = [sc.sem(f"fin_h_loaded{n}") for n in range(KT)]
        ssq_loaded, const_ready, ms_done = sc.sem("fin_ssq_loaded"), sc.sem("fin_const_ready"), sc.sem("fin_ms_done")
        rt_ready, rs_ready, o_ready = sc.sem("fin_rt_ready"), sc.sem("fin_rs_ready"), sc.sem("fin_o_ready")
        stored = [sc.sem(f"fin_stored{n}") for n in range(4)]

        with nc.Block() as block:
            @block.sync
            def _(sp):
                sp.dma_start(ssq[:, :], ssq_dram).then_inc(ssq_loaded, 16)
                sp.dma_start(g_sb[:, :], final_g).then_inc(ssq_loaded, 16)
                for n in range(KT):
                    sp.dma_start(h[:, n, :], hT[n]).then_inc(h_loaded[n], 16)

            @block.gpsimd
            def _(pool):
                pool.memset(ones[:, :], 1.0 / D_MODEL).then_inc(const_ready, 1)
                pool.memset(eps[:, :], RMS_EPS).then_inc(const_ready, 1)

            @block.tensor
            def _(pe):
                pe.wait_ge(const_ready, 2)
                pe.wait_ge(ssq_loaded, 32)
                for c in range(3):
                    mm = pe.matmul(ms[:, c, 0:NCH], ones[:, :], ssq[:, c * NCH:(c + 1) * NCH], start=True, stop=True)
                mm.then_inc(ms_done, 1)

            @block.scalar
            def _(act):
                act.wait_ge(const_ready, 2)
                act.wait_ge(ms_done, 1)
                nc.scalar.activation(pieces(rs[:, :]), ms[:, :, 0:NCH], ACT.Sqrt, bias=eps[:, 0:1]).then_inc(rt_ready, 1)
                for n in range(KT):
                    act.wait_ge(o_ready, n + 1)
                    act.dma_start(outT[n], o[n % 4][:, 0:TOK]).then_inc(stored[n % 4], 16)
                for s in stored:
                    act.wait_ge(s, KT // 4 * 16)

            @block.vector
            def _(dve):
                dve.wait_ge(rt_ready, 1)
                dve.reciprocal(rs[:, :], rs[:, :]).then_inc(rs_ready, 1)
                dve.wait_ge(rs_ready, 1)
                dve.wait_ge(ssq_loaded, 32)
                for n in range(KT):
                    dve.wait_ge(h_loaded[n], 16)
                    if n >= 4:
                        dve.wait_ge(stored[n % 4], n // 4 * 16)
                    dve.scalar_tensor_tensor(o[n % 4][:, :], h[:, n, :], g_sb[:, n:n + 1], rs[:, :], MUL,
                                             MUL).then_inc(o_ready, 1)


OUTPUTS = {
    "outT": (KT, P, TOK), "shift_out": (P, N_SHIFT, 1 + BATCH), "pwkv_out": (P, PAIRS, HEAD),
    "swkv_out": (P, BATCH, PAIRS, HEAD), "vn_out": (P, PAIRS, SAMPLE),
}


def program(nc, a):
    scratch = lambda name, shape: nc.dram_tensor(name, shape, F32, kind="Internal").ap()
    z = scratch("z", (NTILE, P, ZW))
    yT, sT = scratch("yT", (PAIRS, P, TP)), scratch("sT", (PAIRS, P, TP))
    mT, hT, ssq = scratch("mT", (KT, P, TP)), scratch("hT", (KT, P, TP)), scratch("ssq", (P, TP))
    phase_in(nc, a["xT"], a["norm_g"], a["w_in"], z)
    phase_rwkv(nc, z, a["lowrank"], a["lr_bias"], a["mu"], a["par"], a["shiftT"], a["stateT"], yT,
               a["shift_out"], a["swkv_out"], a["pwkv_out"])
    phase_sgu(nc, z, a["sgu_wT"], a["sgu_b"], a["ln_par"], sT, a["vn_out"])
    phase_merge(nc, z, yT, sT, a["w_proj"], mT)
    phase_out(nc, a["xT"], mT, a["w_out"], hT, ssq)
    phase_final(nc, hT, ssq, a["final_g"], a["outT"])


def layouts(inputs):
    import numpy as np
    x = {n: np.asarray(a) for n, a in inputs.items()}
    rows = lambda a: np.ascontiguousarray(a.reshape(-1, P).T)
    tok = np.concatenate([x["x_prompt"].reshape(PROMPT, D_MODEL), x["x_sample"].reshape(SAMPLE, D_MODEL)])
    tiles = lambda w: w.reshape(w.shape[0] // P, P, -1, P).transpose(2, 1, 0, 3).reshape(w.shape[1] // P, P, -1)
    out = {
        "xT": tok.T.reshape(KT, P, TOK),
        "norm_g": rows(x["norm_g"][0]),
        "w_in": tiles(x["w_in"][0]),
        "lowrank": np.concatenate([x["w2"][0], x["a2"][0]]),
        "lr_bias": np.stack([x["w0"][0], x["a0"][0]]),
        "mu": rows(x["shift_mu"][0]),
        "par": np.stack([rows(x[n].reshape(-1)) for n in ("k_k", "k_a", "r_k", "lnx_g", "lnx_b")], 1),
        "shiftT": x["state_shift"].reshape(BATCH, N_SHIFT, P).transpose(2, 1, 0),
        "stateT": x["state_wkv"].reshape(BATCH, PAIRS, 2, HEAD, HEAD).transpose(2, 4, 0, 1, 3).reshape(
            P, BATCH, PAIRS, HEAD),
        "sgu_wT": x["sgu_w"][0].transpose(0, 2, 1),
        "sgu_b": x["sgu_b"][0],
        "ln_par": np.stack([rows(x[n][0]) for n in ("sgu_ln_g", "sgu_ln_b")], 1),
        "w_proj": np.stack([tiles(x["w_proj_a"][0]), tiles(x["w_proj_b"][0])], 1).reshape(2 * KT, P, KH * P),
        "w_out": tiles(x["w_out"][0]),
        "final_g": rows(x["final_norm_g"]),
    }
    return {n: np.ascontiguousarray(a) for n, a in out.items()}


def kernel(**inputs):
    import numpy as np
    import concourse.bacc as bacc
    from concourse.bass_utils import run_bass_kernel_spmd

    nc = bacc.Bacc("TRN2", target_bir_lowering=False, num_devices=1)
    arrays = {f"in_{n}": a for n, a in layouts(inputs).items()}
    aps = {n[3:]: nc.dram_tensor(n, a.shape, mybir.dt.from_np(a.dtype), kind="ExternalInput").ap()
           for n, a in arrays.items()}
    for n, shape in OUTPUTS.items():
        aps[n] = nc.dram_tensor(n, shape, F32, kind="ExternalOutput").ap()
    program(nc, aps)
    got = run_bass_kernel_spmd(nc, [arrays], core_ids=[0]).results[0]

    tok = got["outT"].reshape(D_MODEL, TOK).T
    shift = got["shift_out"].transpose(2, 1, 0).reshape(1 + BATCH, N_SHIFT * P)
    pwkv = got["pwkv_out"].reshape(2, HEAD, PAIRS, HEAD).transpose(2, 0, 3, 1).reshape(1, 1, 2 * PAIRS, HEAD, HEAD)
    swkv = got["swkv_out"].reshape(2, HEAD, BATCH, PAIRS, HEAD).transpose(2, 3, 0, 4, 1).reshape(
        1, BATCH, 2 * PAIRS, HEAD, HEAD)
    vn = got["vn_out"].transpose(2, 1, 0).reshape(1, BATCH, STEPS, D_G)
    back = np.ascontiguousarray
    return (back(tok[:PROMPT]).reshape(1, PROMPT, D_MODEL), back(tok[PROMPT:]).reshape(BATCH, STEPS, D_MODEL),
            back(pwkv), back(shift[0:1]).reshape(1, 1, 1, -1), back(swkv), back(shift[1:]).reshape(1, BATCH, 1, -1),
            back(vn))
```

```python
from contextlib import ExitStack

import concourse.bass as bass
from concourse import mybir

P = 128
D_MODEL, D_R, D_G = 2048, 1024, 1024
KT = D_MODEL // P
KH = D_R // P
HEAD = 64
PAIRS = D_R // P
PROMPT, BATCH, STEPS = 1024, 8, 8
SAMPLE = BATCH * STEPS
TOK = PROMPT + SAMPLE
NCH = 364
TP = 3 * NCH
ZO = 4
ZW = ZO + TP
PAD = TP - TOK
CH = 64
NCHUNK = PROMPT // CH
Q = 128
T_R, T_K, T_V, T_LR, T_GR = 0, 8, 16, 24, 25
T_U, T_VG, T_GG, T_GA, T_GB, NTILE = 33, 41, 49, 57, 73, 89
N_SHIFT = 25
LEVELS = (2, 4, 8, 16, 32)
RMS_EPS, LN_EPS, GN_EPS = 1e-6, 1e-5, 64e-5
DECAY = 0.6065306597126334

F32, F32R = mybir.dt.float32, mybir.dt.float32r
ALU, ACT = mybir.AluOpType, mybir.ActivationFunctionType
MUL, ADD, SUB = ALU.mult, ALU.add, ALU.subtract


NH = 2 * PAIRS
TABLES = {"ident": P, "avg": P, "ones": P, "diag2": P, "mask": 2 * CH, "sample_mask": 2 * CH, "hsum": PAIRS * NH,
          "of_pair": PAIRS, "to_head": P, "reset": PAIRS * CH, "sample_reset": PAIRS * CH,
          "rmask": BATCH, **{f"lmask{b}": 4 * CH for b in LEVELS}}


def tables():
    import numpy as np
    row, col = np.arange(P)[:, None], np.arange(P)[None, :]
    tok, c = row % HEAD, np.arange(CH)[None, :]
    same_head = row // HEAD == col // HEAD
    same_seq = tok // STEPS == c // STEPS
    causal = np.stack([tok < c, tok <= c], 1)
    pair = np.arange(PAIRS)
    t = {
        "ident": row == col,
        "avg": same_head / HEAD,
        "ones": same_head,
        "diag2": (row == col) | ((col == row + 1) & (row % 2 == 0)),
        "mask": causal,
        "sample_mask": causal & same_seq[:, None, :],
        "hsum": np.arange(NH)[None, None, :] == PAIRS * (row // HEAD)[:, :, None] + pair[None, :, None],
        "of_pair": row % PAIRS == pair[None, :],
        "to_head": row // PAIRS == col // HEAD,
        "reset": np.broadcast_to(np.arange(PAIRS * CH) % CH != 0, (P, PAIRS * CH)),
        "sample_reset": np.broadcast_to(np.arange(PAIRS * CH) % STEPS != 0, (P, PAIRS * CH)),
        "rmask": tok // STEPS == np.arange(BATCH)[None, :],
    }
    for b in LEVELS:
        blk = np.arange(4 * CH)[None, :] // b % (CH // b)
        t[f"lmask{b}"] = (row >= 2 * b * blk + b) & (row < 2 * b * (blk + 1))
    return np.concatenate([t[n].astype(np.float32).reshape(P, w) for n, w in TABLES.items()], 1)


def tile_of(dram, i):
    if isinstance(i, int):
        return dram[i]
    return dram[bass.ds(i, 1)].rearrange("o p c -> (o p) c")


def after(engine, sem, n):
    if not isinstance(n, int) or n > 0:
        engine.wait_ge(sem, n)


class Scope:

    def __init__(self, nc, stack):
        self.nc, self.stack, self.sems = nc, stack, []
        stack.callback(self.clear)

    def sb(self, name, shape, dt=F32):
        return self.stack.enter_context(self.nc.sbuf_tensor(name, shape, dt))

    def ps(self, name, shape):
        return self.stack.enter_context(self.nc.psum_tensor(name, shape, F32))

    def sem(self, name):
        self.sems.append(self.nc.alloc_semaphore(name))
        return self.sems[-1]

    def clear(self):
        self.nc.clear_and_free_semaphores(self.sems)
        self.nc.all_engine_barrier()


def pieces(ap):
    return ap.rearrange("p (c n) -> p c n", c=3)


class Gemm:

    def __init__(self, nc, sc, tag, wt, kts, xh, xl, koff):
        self.nc, self.wt, self.kts, self.xh, self.xl, self.koff = nc, wt, kts, xh, xl, koff
        self.raw = [sc.sb(f"{tag}_raw{s}", [P, kts * P]) for s in range(2)]
        self.wh = [sc.sb(f"{tag}_wh{s}", [P, kts * P], F32R) for s in range(2)]
        self.wl = [sc.sb(f"{tag}_wl{s}", [P, kts * P], F32R) for s in range(2)]
        self.acc = [sc.ps(f"{tag}_acc{s}", [P, 3, 512]) for s in range(2)]
        self.w_loaded = [sc.sem(f"{tag}_w_loaded{s}") for s in range(2)]
        self.hi_ready = [sc.sem(f"{tag}_hi_ready{s}") for s in range(2)]
        self.lo_ready = [sc.sem(f"{tag}_lo_ready{s}") for s in range(2)]
        self.group_done = [sc.sem(f"{tag}_group_done{s}") for s in range(2)]
        self.evacuated = [sc.sem(f"{tag}_evacuated{s}") for s in range(2)]
        self.x_ready = sc.sem(f"{tag}_x_ready")

    def load(self, sp, g, i, s):
        sp.wait_ge(self.lo_ready[s], i)
        sp.dma_start(self.raw[s][:, :], tile_of(self.wt, g)).then_inc(self.w_loaded[s], 16)

    def split(self, dve, i, s):
        dve.wait_ge(self.w_loaded[s], i * 16 + 16)
        dve.wait_ge(self.group_done[s], i)
        dve.tensor_copy(self.wh[s][:, :], self.raw[s][:, :]).then_inc(self.hi_ready[s], 1)
        dve.wait_ge(self.hi_ready[s], i + 1)
        dve.tensor_tensor(self.wl[s][:, :], self.raw[s][:, :], self.wh[s][:, :].bitcast(F32),
                          SUB).then_inc(self.lo_ready[s], 1)

    def products(self, pe, i, s, before=lambda k: None):
        pe.wait_ge(self.lo_ready[s], i + 1)
        pe.wait_ge(self.evacuated[s], i)
        for k in range(self.kts):
            before(k)
            kx = k + self.koff[s]
            pe.wait_ge(self.x_ready, kx + 1)
            for w, x in ((self.wh, self.xh), (self.wh, self.xl), (self.wl, self.xh)):
                for c in range(3):
                    mm = pe.matmul(self.acc[s][:, c, 0:NCH], w[s][:, k * P:(k + 1) * P],
                                   x[:, kx, c * NCH:(c + 1) * NCH],
                                   start=(k == 0 and w is self.wh and x is self.xh),
                                   stop=(k == self.kts - 1 and w is self.wl))
        mm.then_inc(self.group_done[s], 1)

    def sums(self, s):
        return self.acc[s][:, :, 0:NCH]


def in_slots(engine, groups, body):
    for s in range(2):
        body(s, 0, s)
    with engine.Fori(1, groups // 2) as i:
        for s in range(2):
            body(i * 2 + s, i, s)
    if groups % 2:
        body(groups - 1, groups // 2, 0)


def evacuate_and_split(dve, gm, groups, evacuate):
    turns = groups // 2

    def turn(i):
        for s in range(2):
            evacuate(i * 2 + s, i, s)
            gm.split(dve, i + 1, s)

    turn(0)
    with dve.Fori(1, turns - 1) as i:
        turn(i)
    evacuate(2 * turns - 2, turns - 1, 0)
    if groups % 2:
        gm.split(dve, turns, 0)
    evacuate(2 * turns - 1, turns - 1, 1)
    if groups % 2:
        evacuate(2 * turns, turns, 0)


def phase_in(nc, xT, norm_g, wt, z):
    with ExitStack() as stack:
        sc = Scope(nc, stack)
        xh = sc.sb("in_xh", [P, KT, TP], F32R)
        xl = sc.sb("in_xl", [P, KT, TP], F32R)
        gm = Gemm(nc, sc, "in", wt, KT, xh, xl, (0, 0))
        stage = [sc.sb(f"in_stage{s}", [P, ZW]) for s in range(2)]
        sqb = [b[:, ZO:ZW] for b in stage]
        g_sb = sc.sb("in_g", [P, KT])
        eps = sc.sb("in_eps", [P, 1])
        ones = sc.sb("in_ones", [P, P])
        rstd = sc.sb("in_rstd", [P, TP])
        xr = [sc.sb(f"in_x{n}", [P, TP]) for n in range(2)]
        ring = [xr[0][:, :], xr[1][:, :], rstd[:, :], gm.raw[1][:, 0:TP]]
        x_loaded = [sc.sem(f"in_x_loaded{n}") for n in range(4)]
        g_loaded, const_ready = sc.sem("in_g_loaded"), sc.sem("in_const_ready")
        sq_ready, sq_summed = sc.sem("in_sq_ready"), sc.sem("in_sq_summed")
        rt_ready, rstd_ready, xh_ready = sc.sem("in_rt_ready"), sc.sem("in_rstd_ready"), sc.sem("in_xh_ready")
        stored = [sc.sem(f"in_stored{s}") for s in range(2)]
        turns = NTILE // 2
        x = lambda n: ring[n % 4]

        with nc.Block() as block:
            @block.sync
            def _(sp):
                sp.dma_start(g_sb[:, :], norm_g).then_inc(g_loaded, 16)
                gm.load(sp, 0, 0, 0)
                for n in range(KT):
                    if n >= 4:
                        sp.wait_ge(gm.x_ready, n - 3)
                        sp.wait_ge(sq_ready, n - 3)
                    sp.dma_start(x(n)[:, 0:TOK], xT[n]).then_inc(x_loaded[n % 4], 16)
                sp.wait_ge(gm.x_ready, KT)
                sp.wait_ge(sq_ready, KT)
                gm.load(sp, 1, 0, 1)
                with sp.Fori(1, turns) as i:
                    for s in range(2):
                        gm.load(sp, i * 2 + s, i, s)
                if NTILE % 2:
                    gm.load(sp, NTILE - 1, turns, 0)

            @block.gpsimd
            def _(pool):
                pool.memset(ones[:, :], 1.0 / D_MODEL).then_inc(const_ready, 1)
                pool.memset(eps[:, :], RMS_EPS).then_inc(const_ready, 1)
                pool.memset(stage[0][:, 0:ZO], 0.0).then_inc(const_ready, 1)
                pool.memset(stage[1][:, 0:ZO], 0.0).then_inc(const_ready, 1)
                for b in ring:
                    pool.memset(b[:, TOK:TP], 0.0).then_inc(const_ready, 1)

            @block.scalar
            def _(act):
                act.wait_ge(const_ready, 8)
                for n in range(KT):
                    act.wait_ge(x_loaded[n % 4], 16 * (n // 4 + 1))
                    if n >= 2:
                        act.wait_ge(sq_summed, n - 1)
                    nc.scalar.activation(sqb[n % 2], x(n), ACT.Square).then_inc(sq_ready, 1)
                act.wait_ge(sq_summed, KT)
                act.wait_ge(gm.x_ready, KT)
                nc.scalar.activation(pieces(rstd[:, :]), gm.sums(1), ACT.Sqrt, bias=eps[:, 0:1]).then_inc(rt_ready, 1)

                def store(g, i, s):
                    act.wait_ge(gm.evacuated[s], i + 1)
                    act.dma_start(tile_of(z, g), stage[s][:, :]).then_inc(stored[s], 16)

                in_slots(act, NTILE, store)
                act.wait_ge(stored[0], 16 * (NTILE - turns))
                act.wait_ge(stored[1], 16 * turns)

            @block.vector
            def _(dve):
                gm.split(dve, 0, 0)
                dve.wait_ge(const_ready, 8)
                dve.wait_ge(g_loaded, 16)
                for n in range(KT):
                    dve.wait_ge(x_loaded[n % 4], 16 * (n // 4 + 1))
                    dve.tensor_scalar(xh[:, n, :], x(n), g_sb[:, n:n + 1], None, MUL).then_inc(xh_ready, 1)
                    dve.wait_ge(xh_ready, n + 1)
                    dve.scalar_tensor_tensor(xl[:, n, :], x(n), g_sb[:, n:n + 1], xh[:, n, :].bitcast(F32), MUL,
                                             SUB).then_inc(gm.x_ready, 1)
                gm.split(dve, 0, 1)
                dve.wait_ge(rt_ready, 1)
                dve.reciprocal(rstd[:, :], rstd[:, :]).then_inc(rstd_ready, 1)
                dve.wait_ge(rstd_ready, 1)

                def evacuate(g, i, s):
                    dve.wait_ge(gm.group_done[s], i + 1)
                    dve.wait_ge(stored[s], i * 16)
                    dve.tensor_tensor(pieces(stage[s][:, ZO:ZW]), gm.sums(s), pieces(rstd[:, :]),
                                      MUL).then_inc(gm.evacuated[s], 1)

                evacuate_and_split(dve, gm, NTILE, evacuate)

            @block.tensor
            def _(pe):
                pe.wait_ge(const_ready, 1)

                def sum_squares(n):
                    pe.wait_ge(sq_ready, n + 1)
                    for c in range(3):
                        mm = pe.matmul(gm.acc[1][:, c, 0:NCH], ones[:, :], sqb[n % 2][:, c * NCH:(c + 1) * NCH],
                                       start=(n == 0), stop=(n == KT - 1))
                    mm.then_inc(sq_summed, 1)

                gm.products(pe, 0, 0, sum_squares)
                pe.wait_ge(rt_ready, 1)
                gm.products(pe, 0, 1)
                with pe.Fori(1, turns) as i:
                    for s in range(2):
                        gm.products(pe, i, s)
                if NTILE % 2:
                    gm.products(pe, turns, 0)


def phase_rwkv(nc, z, lowrank, lr_bias, mu, par, table, shiftT, stateT, yT, shift_out, swkv_out, pwkv_out):
    with ExitStack() as stack:
        sc = Scope(nc, stack)
        sb, sem = sc.sb, sc.sem
        H2 = slice(0, HEAD), slice(HEAD, P)
        FOUR = slice(0, 4), slice(4, 8)
        two = lambda name, shape: [sb(f"{name}{n}", shape) for n in range(2)]
        big = lambda name: sb(name, [P, PAIRS, CH])

        zin = sb("zin", [P, N_SHIFT, CH + 1])
        gin = sb("gin", [P, PAIRS, CH])
        mix = sb("mix", [P, N_SHIFT, CH])
        r, k = mix[:, T_R:T_K, :], mix[:, T_K:T_V, :]
        v_pad = sb("v_pad", [P, PAIRS, 2 * CH])
        v = v_pad[:, :, CH:2 * CH]
        lr = sb("lr", [P, 2, CH])
        swa, cum, cum1 = sb("swa", [P, 2, PAIRS, CH]), big("cum"), big("cum1")
        sw, sa = swa[:, 0, :, :], swa[:, 1, :, :]
        ep, en, em = big("ep"), big("en"), big("em")
        kk, sq = big("kk"), big("sq")
        nrm, rn, rnx = sb("nrm", [NH, CH]), sb("rn", [NH, CH]), sb("rnx", [NH, PAIRS, CH])
        k2, rk, bsa, bv, gs = big("k2"), big("rk"), big("bsa"), big("bv"), big("gs")
        bk = sb("bk", [P, PAIRS, 2, CH])
        bkw = sb("bkw", [P, PAIRS, 2, CH])
        ar = two("ar", [P, PAIRS, 2, 2, CH])
        m = two("m", [P, PAIRS, 2, 2, CH])
        at, t = sb("at", [P, PAIRS, P]), sb("t", [P, PAIRS, P])
        tt = two("tt", [P, PAIRS, P])
        pl = [sb(f"p{b}", [P, PAIRS, P]) for b in LEVELS]
        bkt = two("bkt", [P, PAIRS, P])
        zz = two("zz", [P, PAIRS, P])
        xst = sb("xst", [P, PAIRS, HEAD])
        st, stw = sb("st", [P, PAIRS, HEAD]), sb("stw", [P, PAIRS, HEAD])
        bonus, gate, wc = two("bonus", [P, PAIRS, CH]), two("gate", [P, PAIRS, CH]), two("wc", [P, PAIRS, BATCH])
        y, ysq, yo = big("y"), big("ysq"), big("yo")
        sd, rs, rsx = sb("sd", [NH, CH]), sb("rs", [NH, CH]), sb("rsx", [NH, PAIRS, CH])
        tab = sb("tab", [P, sum(TABLES.values())])
        col, at_col = {}, 0
        for name, width in TABLES.items():
            col[name] = tab[:, at_col:at_col + width]
            at_col += width
        ident, avg, diag2, rmask = col["ident"], col["avg"], col["diag2"], col["rmask"]
        ones = col["ones"]
        hsum = col["hsum"].rearrange("p (u r) -> p u r", u=PAIRS)
        of_pair, to_head = col["of_pair"][0:NH, :], col["to_head"][0:NH, :]
        masks, resets = (col["mask"], col["sample_mask"]), (col["reset"], col["sample_reset"])
        lmask = [col[f"lmask{b}"] for b in LEVELS]
        eps = sb("gn_eps", [P, 1])
        lrw, lrb = sb("lrw", [P, D_R]), sb("lrb", [P, 2, PAIRS])
        mu_sb, par_sb = sb("mu_sb", [P, N_SHIFT]), sb("par_sb", [P, 5, PAIRS])
        k_k, k_a, r_k, lnx_g, lnx_b = (
            par_sb[:, n, :].unsqueeze(2).broadcast_to([P, PAIRS, CH]) for n in range(5))
        sts = sb("sts", [P, BATCH, PAIRS, HEAD])
        zprev = sb("zprev", [P, N_SHIFT, BATCH])
        xr = pl[2][:, :, :].rearrange("p u (j c) -> p u j c", j=2)
        zmask = [pl[4], t]
        sh_out = sb("sh_out", [P, N_SHIFT, 1 + BATCH])

        bank = [sc.ps(f"bank{n}", [P, 512]) for n in range(8)]
        L0, L1, L2, L3, E0, E1, B0, B1 = range(8)
        by = lambda n, j: bank[n][:, :].rearrange("p (j c) -> p j c", j=j)
        MM, LL, LT, EE, BB = (L0, L1, L2, L3), (L0, L2), (L1, L3), (E0, E1), (B0, B1)

        zin_loaded, gin_loaded, par_loaded = sem("zin_loaded"), sem("gin_loaded"), sem("par_loaded")
        zprev_loaded, sts_loaded = sem("zprev_loaded"), sem("sts_loaded")
        filled, dve_filled = sem("filled"), sem("dve_filled")
        rnx_ready, wab_ready, mu_loaded = sem("rnx_ready"), sem("wab_ready"), sem("mu_loaded")
        diff_ready, lrs_ready, scaled_ready, mix_ready = sem("diff_ready"), sem("lrs_ready"), sem("scaled_ready"), sem("mix_ready")
        lrmix_ready, lr_ready, wa_done, sig_ready = sem("lrmix_ready"), sem("lr_ready"), sem("wa_done"), sem("sig_ready")
        cum_ready, cum1_ready, exp_ready = sem("cum_ready"), sem("cum1_ready"), sem("exp_ready")
        kkr_ready, sq_ready, ss_done, nrm_ready = sem("kkr_ready"), sem("sq_ready"), sem("ss_done"), sem("nrm_ready")
        clamp_ready, rn_ready, rnb_done, kk_ready = sem("clamp_ready"), sem("rn_ready"), sem("rnb_done"), sem("kk_ready")
        t1_ready, k2_ready, rk_ready, bsa_ready = sem("t1_ready"), sem("k2_ready"), sem("rk_ready"), sem("bsa_ready")
        rkp_ready, rsx_ready, yg_ready = sem("rkp_ready"), sem("rsx_ready"), sem("yg_ready")
        b_ready, k_ready, ar_ready = sem("b_ready"), sem("k_ready"), sem("ar_ready")
        vt_done, zv_ready, bonus_done, bv_ready, bonus_ready = (
            sem("vt_done"), sem("zv_ready"), sem("bonus_done"), sem("bv_ready"), sem("bonus_ready"))
        gs_ready, gate_ready, wc_ready = sem("gs_ready"), sem("gate_ready"), sem("wc_ready")
        m_done, m_ready, at_ready = sem("m_done"), sem("m_ready"), sem("at_ready")
        bkw_ready, bkt_done, bkt_ready = sem("bkw_ready"), sem("bkt_done"), sem("bkt_ready")
        tt_ready, t_done, t_ready = sem("tt_ready"), sem("t_done"), sem("t_ready")
        lp_done, lp_ready, lt_done, ltt_done = sem("lp_done"), sem("lp_ready"), sem("lt_done"), sem("ltt_done")
        lt_ready, ltt_ready = sem("lt_ready"), sem("ltt_ready")
        x_done, x_ready, u_done, u_ready = sem("x_done"), sem("x_ready"), sem("u_done"), sem("u_ready")
        s_done, stw_ready, st_ready, y_done = sem("s_done"), sem("stw_ready"), sem("st_ready"), sem("y_done")
        y_ready, mean_done, yc_ready, ysq_ready = sem("y_ready"), sem("mean_done"), sem("yc_ready"), sem("ysq_ready")
        var_done, sd_ready, rs_ready, rsb_done = sem("var_done"), sem("sd_ready"), sem("rs_ready"), sem("rsb_done")
        yn_ready, yv_ready, yo_ready, y_stored = sem("yn_ready"), sem("yv_ready"), sem("yo_ready"), sem("y_stored")
        xr_done, xr_ready, zmask_ready = sem("xr_done"), sem("xr_ready"), sem("zmask_ready")
        shift_ready, state_stored = sem("shift_ready"), sem("state_stored")

        NL = len(LEVELS)
        SMP = NCHUNK
        flat = lambda ap: ap.rearrange("p u c -> p (u c)")

        def last_level(c):
            return LEVELS.index(STEPS // 2) if is_sample(c) else NL - 1

        def is_sample(c):
            return isinstance(c, int) and c == SMP

        def halves_of(ap, b):
            w = ap.rearrange("p u (n h b) -> p (u n) h b", h=2, b=b)
            return w[:, :, 0, :], w[:, :, 1, :]

        def pb(buffers, c):
            return buffers[parity(c)]

        def parity(c):
            return c % 2 if isinstance(c, int) else par_of[id(c)]

        par_of = {}

        def sync_load(sp, c):
            if is_sample(c):
                z_at, g_at = ZO + PROMPT - 1, ZO + PROMPT
            elif isinstance(c, int):
                z_at, g_at = c * CH + (ZO - 1), c * CH + ZO
            else:
                z_at, g_at = sp.snap(c * CH + (ZO - 1)), sp.snap(c * CH + ZO)
            cols = (lambda at, n: slice(at, at + n)) if isinstance(c, int) else bass.ds
            after(sp, mix_ready, c * 2)
            sp.dma_start(zin[:, :, :], z[0:N_SHIFT, :, cols(z_at, CH + 1)].rearrange("n p c -> p n c")
                         ).then_inc(zin_loaded, 16)
            if is_sample(c):
                sp.dma_start(zprev[:, :, :], shiftT).then_inc(zprev_loaded, 16)
            after(sp, gate_ready, c)
            sp.dma_start(gin[:, :, :], z[T_GR:T_GR + PAIRS, :, cols(g_at, CH)].rearrange("n p c -> p n c")
                         ).then_inc(gin_loaded, 16)

        def v_diff(dve, c):
            cur = zin[:, :, 1:CH + 1]
            dve.wait_ge(zin_loaded, c * 16 + 16)
            if is_sample(c):
                c4 = cur.rearrange("p n (b t) -> p n b t", b=BATCH)
                m4 = mix[:, :, :].rearrange("p n (b t) -> p n b t", b=BATCH)
                dve.wait_ge(zprev_loaded, 16)
                dve.tensor_copy(sh_out[:, :, 0:1], zin[:, :, 0:1]).then_inc(shift_ready, 1)
                dve.tensor_copy(sh_out[:, :, 1:1 + BATCH], c4[:, :, :, STEPS - 1]).then_inc(shift_ready, 1)
                dve.tensor_tensor(m4[:, :, :, 0], zprev[:, :, :], c4[:, :, :, 0], SUB).then_inc(shift_ready, 1)
                dve.wait_ge(shift_ready, 3)
                dve.tensor_tensor(m4[:, :, :, 1:STEPS], c4[:, :, :, 0:STEPS - 1], c4[:, :, :, 1:STEPS],
                                  SUB).then_inc(diff_ready, 1)
            else:
                dve.tensor_tensor(mix[:, :, :], zin[:, :, 0:CH], cur, SUB).then_inc(diff_ready, 1)
            dve.wait_ge(diff_ready, c + 1)
            dve.tensor_scalar(mix[:, T_LR, :], mix[:, T_LR, :], mu_sb[:, T_LR:T_LR + 1], None, MUL).then_inc(lrs_ready, 1)
            dve.wait_ge(lrs_ready, c + 1)
            dve.tensor_tensor(mix[:, T_LR, :], mix[:, T_LR, :], cur[:, T_LR, :], ADD).then_inc(lrmix_ready, 1)

        def p_scale(pool, c):
            pool.wait_ge(diff_ready, c + 1)
            pool.tensor_tensor(mix[:, 0:T_LR, :], mix[:, 0:T_LR, :],
                               mu_sb[:, 0:T_LR].unsqueeze(2).broadcast_to([P, T_LR, CH]), MUL).then_inc(scaled_ready, 1)

        def v_mix(dve, c):
            cur = zin[:, :, 1:CH + 1]
            dve.wait_ge(scaled_ready, c + 1)
            dve.tensor_tensor(mix[:, T_R:T_V, :], mix[:, T_R:T_V, :], cur[:, T_R:T_V, :], ADD).then_inc(mix_ready, 1)
            dve.tensor_tensor(v, mix[:, T_V:T_LR, :], cur[:, T_V:T_LR, :], ADD).then_inc(mix_ready, 1)

        def a_lowrank(act, c):
            act.wait_ge(lrmix_ready, c + 1)
            nc.scalar.activation(lr[0:HEAD, 0, :], mix[0:HEAD, T_LR, :], ACT.Tanh).then_inc(lr_ready, 1)
            nc.scalar.activation(lr[HEAD:P, 1, :], mix[HEAD:P, T_LR, :], ACT.Copy).then_inc(lr_ready, 1)

        def t_lowrank(pe, c):
            pe.wait_ge(lr_ready, c * 2 + 2)
            after(pe, bkt_ready, c * 2)
            for f in range(2):
                for p in range(4 * f, 4 * f + 4):
                    mm = pe.matmul(by(EE[f], 4)[:, p % 4, :], lrw[:, p * P:(p + 1) * P],
                                   lr[:, :, :].rearrange("p j c -> p (j c)"), start=True, stop=True)
                mm.then_inc(wa_done, 1)

        def v_bias(dve, c):
            for f in range(2):
                dve.wait_ge(wa_done, c * 2 + f + 1)
                dve.tensor_tensor(swa[:, :, FOUR[f], :].rearrange("p j u c -> p u j c"),
                                  bank[EE[f]][:, :].rearrange("p (u j c) -> p u j c", u=4, j=2),
                                  lrb[:, :, FOUR[f]].rearrange("p j u -> p u j").unsqueeze(3).broadcast_to([P, 4, 2, CH]),
                                  ADD).then_inc(wab_ready, 1)

        def a_sigmoids(act, c):
            for f in range(2):
                act.wait_ge(wab_ready, c * 2 + f + 1)
                nc.scalar.activation(swa[:, :, FOUR[f], :], swa[:, :, FOUR[f], :], ACT.Sigmoid).then_inc(sig_ready, 1)

        def a_gate(act, c):
            act.wait_ge(gin_loaded, c * 16 + 16)
            nc.scalar.activation(gs[:, :, :], gin[:, :, :], ACT.Sigmoid).then_inc(gs_ready, 1)

        def v_scan(dve, c):
            dve.wait_ge(sig_ready, c * 2 + 2)
            dve.tensor_tensor_scan(flat(cum[:, :, :]), resets[is_sample(c)], flat(sw), 0.0, MUL, ADD).then_inc(cum_ready, 1)

        def v_k(dve, c):
            dve.scalar_tensor_tensor(k2[:, :, :], sa, -1.0, k_a, ADD, MUL).then_inc(t1_ready, 1)
            dve.wait_ge(t1_ready, c + 1)
            dve.scalar_tensor_tensor(k2[:, :, :], k2[:, :, :], 1.0, k, ADD, MUL).then_inc(k2_ready, 1)

        def p_early(pool, c):
            pool.wait_ge(mix_ready, c * 2 + 1)
            pool.tensor_tensor(kk[:, :, :], k, k_k, MUL).then_inc(kkr_ready, 1)
            pool.wait_ge(cum_ready, c + 1)
            pool.tensor_tensor(cum1[:, :, :], cum[:, :, :], sw, SUB).then_inc(cum1_ready, 1)
            pool.wait_ge(k2_ready, c + 1)
            pool.tensor_tensor(rk[:, :, :], r, k2[:, :, :], MUL).then_inc(rk_ready, 1)
            pool.wait_ge(rk_ready, c + 1)
            pool.tensor_tensor(rk[:, :, :], rk[:, :, :], r_k, MUL).then_inc(rkp_ready, 1)
            pool.wait_ge(exp_ready, c * 3 + 2)
            pool.tensor_tensor(bk[:, :, 1, :], k2[:, :, :], en[:, :, :], MUL).then_inc(k_ready, 1)

        def a_exps(act, c):
            act.wait_ge(cum_ready, c + 1)
            nc.scalar.activation(ep[:, :, :], cum[:, :, :], ACT.Exp, scale=-DECAY).then_inc(exp_ready, 1)
            nc.scalar.activation(en[:, :, :], cum[:, :, :], ACT.Exp, scale=DECAY).then_inc(exp_ready, 1)
            act.wait_ge(cum1_ready, c + 1)
            nc.scalar.activation(em[:, :, :], cum1[:, :, :], ACT.Exp, scale=-DECAY).then_inc(exp_ready, 1)

        def a_square(act, c):
            act.wait_ge(kkr_ready, c + 1)
            nc.scalar.activation(sq[:, :, :], kk[:, :, :], ACT.Square).then_inc(sq_ready, 1)

        def t_sumsq(pe, c):
            pe.wait_ge(sq_ready, c + 1)
            pe.wait_ge(sig_ready, c * 2 + 1)
            for p in range(PAIRS):
                mm = pe.matmul(bank[E0][0:NH, 0:CH], hsum[:, p, :], sq[:, p, :], start=(p == 0), stop=(p == PAIRS - 1))
            mm.then_inc(ss_done, 1)

        def a_norm(act, c):
            act.wait_ge(ss_done, c + 1)
            nc.scalar.activation(nrm[:, :], bank[E0][0:NH, 0:CH], ACT.Sqrt).then_inc(nrm_ready, 1)

        def v_norm(dve, c):
            dve.wait_ge(nrm_ready, c + 1)
            dve.tensor_scalar(nrm[:, :], nrm[:, :], 1e-12, None, ALU.max).then_inc(clamp_ready, 1)
            dve.wait_ge(clamp_ready, c + 1)
            dve.reciprocal(rn[:, :], nrm[:, :]).then_inc(rn_ready, 1)
            dve.wait_ge(rn_ready, c + 1)
            dve.tensor_tensor(rnx[:, :, :], rn[:, :].unsqueeze(1).broadcast_to([NH, PAIRS, CH]),
                              of_pair.unsqueeze(2).broadcast_to([NH, PAIRS, CH]), MUL).then_inc(rnx_ready, 1)

        def t_spread_norm(pe, c):
            pe.wait_ge(rnx_ready, c + 1)
            pe.wait_ge(sig_ready, c * 2 + 2)
            pe.matmul(bank[E1][:, :], to_head, flat(rnx[:, :, :]), start=True, stop=True).then_inc(rnb_done, 1)

        def t_bonus(pe, c):
            pe.wait_ge(rkp_ready, c + 1)
            pe.wait_ge(nrm_ready, c + 1)
            pe.matmul(bank[E0][:, :], ones[:, :], flat(rk[:, :, :]), start=True, stop=True).then_inc(bonus_done, 1)

        def v_kk(dve, c):
            dve.wait_ge(rnb_done, c + 1)
            dve.tensor_tensor(kk[:, :, :], kk[:, :, :], by(E1, PAIRS), MUL).then_inc(kk_ready, 1)
            dve.wait_ge(kk_ready, c + 1)
            dve.tensor_tensor(bsa[:, :, :], kk[:, :, :], sa, MUL).then_inc(bsa_ready, 1)

        def v_ar(dve, c, h):
            a = pb(ar, c)
            dve.wait_ge(exp_ready, c * 3 + 3)
            after(dve, y_done, c - 1)
            dve.scalar_tensor_tensor(a[H2[h], :, h, 0, :], kk[H2[h], :, :], -1.0, em[H2[h], :, :],
                                     MUL, MUL).then_inc(ar_ready, 1)
            dve.tensor_tensor(a[H2[h], :, h, 1, :], r[H2[h], :, :], ep[H2[h], :, :], MUL).then_inc(ar_ready, 1)

        def v_b(dve, c):
            dve.wait_ge(bonus_done, c + 1)
            after(dve, bonus_ready, c)
            dve.tensor_tensor(bv[:, :, :], by(E0, PAIRS), v, MUL).then_inc(bv_ready, 1)
            dve.wait_ge(bsa_ready, c + 1)
            after(dve, bkw_ready, c * 2)
            dve.tensor_tensor(bk[:, :, 0, :], bsa[:, :, :], en[:, :, :], MUL).then_inc(b_ready, 1)

        def t_values(pe, c):
            pe.wait_ge(mix_ready, c * 2 + 2)
            pe.wait_ge(bv_ready, c + 1)
            for f in range(2):
                for p in range(4 * f, 4 * f + 4):
                    mm = pe.transpose(by(EE[f], 4)[:, p % 4, :], v_pad[:, p, :], ident[:, :])
                mm.then_inc(vt_done, 1)

        def t_m(pe, c):
            a = pb(ar, c)
            pe.wait_ge(b_ready, c + 1)
            pe.wait_ge(k_ready, c + 1)
            pe.wait_ge(ar_ready, c * 4 + 4)
            after(pe, ltt_ready, c * 2 * NL)
            for q in range(4):
                for p in (2 * q, 2 * q + 1):
                    mm = pe.matmul(bank[MM[q]][:, (p % 2) * 256:(p % 2) * 256 + 256],
                                   bk[:, p, :, :].rearrange("p j c -> p (j c)"),
                                   a[:, p, :, :, :].rearrange("p h j c -> p (h j c)"), start=True, stop=True)
                mm.then_inc(m_done, 1)

        def a_values(act, c):
            for f in range(2):
                act.wait_ge(vt_done, c * 2 + f + 1)
                after(act, s_done, c * 2 - 2)
                nc.scalar.activation(pb(zz, c)[:, FOUR[f], :], by(EE[f], 4), ACT.Copy).then_inc(zv_ready, 1)

        def v_mask(dve, c):
            msk = masks[is_sample(c)].unsqueeze(1).broadcast_to([P, 4, P])
            after(dve, u_done, c * 2 - 2)
            for q in range(4):
                dve.wait_ge(m_done, c * 4 + q + 1)
                dve.tensor_tensor(pb(m, c)[:, 2 * q:2 * q + 2, :, :, :].rearrange("p u h j c -> p (u h) (j c)"),
                                  by(MM[q], 4), msk, MUL).then_inc(m_ready, 1)

        def v_at(dve, c):
            eye = ident[H2[0], H2[0]].unsqueeze(1).broadcast_to([HEAD, PAIRS, HEAD])
            dve.wait_ge(m_ready, c * 4 + 4)
            for h in range(2):
                dve.tensor_tensor(at[H2[h], :, H2[h]], pb(m, c)[H2[0], :, h, 0, :], eye, ADD).then_inc(at_ready, 1)

        def p_mid(pool, c):
            pool.wait_ge(b_ready, c + 1)
            pool.wait_ge(k_ready, c + 1)
            after(pool, bkt_done, c * 2)
            for j in range(2):
                if is_sample(c):
                    split = lambda ap: ap.rearrange("p u (b t) -> p u b t", t=STEPS)
                    pool.tensor_tensor(split(bkw[:, :, j, :]), split(bk[:, :, j, :]),
                                       split(ep[:, :, :])[:, :, :, STEPS - 1:STEPS].broadcast_to(
                                           [P, PAIRS, BATCH, STEPS]), MUL).then_inc(bkw_ready, 1)
                else:
                    pool.tensor_tensor(bkw[:, :, j, :], bk[:, :, j, :], ep[:, :, CH - 1:CH].broadcast_to([P, PAIRS, CH]),
                                       MUL).then_inc(bkw_ready, 1)
            pool.wait_ge(gs_ready, c + 1)
            after(pool, yo_ready, c - 1)
            pool.tensor_tensor(pb(gate, c)[:, :, :], gs[:, :, :], gin[:, :, :], MUL).then_inc(gate_ready, 1)
            pool.wait_ge(bv_ready, c + 1)
            after(pool, yv_ready, c - 1)
            pool.tensor_tensor(pb(bonus, c)[:, :, :], bv[:, :, :], lnx_b, ADD).then_inc(bonus_ready, 1)

        def v_wc(dve, c):
            after(dve, stw_ready, c - 1)
            src = ep[:, :, :].rearrange("p u (b t) -> p u b t", t=STEPS)[:, :, :, STEPS - 1]
            dve.tensor_copy(pb(wc, c)[:, :, :], src).then_inc(wc_ready, 1)

        def t_bkt(pe, c):
            pe.wait_ge(bkw_ready, c * 2 + 2)
            for f in range(2):
                pe.wait_ge(zv_ready, c * 2 + f + 1)
                for p in range(4 * f, 4 * f + 4):
                    mm = pe.transpose(by(EE[f], 4)[:, p % 4, :], bkw[:, p, :, :].rearrange("p j c -> p (j c)"), ident[:, :])
                mm.then_inc(bkt_done, 1)

        def a_bkt(act, c):
            for f in range(2):
                act.wait_ge(bkt_done, c * 2 + f + 1)
                nc.scalar.activation(pb(bkt, c)[:, FOUR[f], :], by(EE[f], 4), ACT.Copy).then_inc(bkt_ready, 1)

        def v_tt(dve, c):
            dve.wait_ge(at_ready, c * 2 + 2)
            dve.tensor_tensor(pb(tt, c)[:, :, :], at[:, :, :], diag2[:, :].unsqueeze(1).broadcast_to([P, PAIRS, P]),
                              MUL).then_inc(tt_ready, 1)

        def t_turn(pe, c):
            pe.wait_ge(tt_ready, c + 1)
            for f in range(2):
                for p in range(4 * f, 4 * f + 4):
                    mm = pe.transpose(by(LT[f], 4)[:, p % 4, :], pb(tt, c)[:, p, :], ident[:, :])
                mm.then_inc(t_done, 1)

        def a_turn(act, c):
            for f in range(2):
                act.wait_ge(t_done, c * 2 + f + 1)
                nc.scalar.activation(t[:, FOUR[f], :], by(LT[f], 4), ACT.Copy).then_inc(t_ready, 1)

        def t_level(pe, c, n):
            last = n == last_level(c)
            if n > last_level(c):
                return
            for f in range(2):
                if n == 0:
                    pe.wait_ge(t_ready, c * 2 + f + 1)
                else:
                    pe.wait_ge(lt_ready, (c * (NL - 1) + n) * 2 - 1 + f)
                for p in range(4 * f, 4 * f + 4):
                    mm = pe.matmul(by(LL[f], 4)[:, p % 4, :], at[:, p, :], t[:, p, :], start=True, stop=True)
                mm.then_inc(lp_done, 1)
            for f in range(2):
                pe.wait_ge(lp_ready, (c * NL + n) * 2 + f + 1)
                if n:
                    pe.wait_ge(ltt_ready, (c * NL + n) * 2 - 1 + f)
                if not last:
                    for p in range(4 * f, 4 * f + 4):
                        mm = pe.matmul(by(LL[f], 4)[:, p % 4, :], pb(tt, c)[:, p, :], pl[n][:, p, :], start=True, stop=True)
                    mm.then_inc(lt_done, 1)
                for p in range(4 * f, 4 * f + 4):
                    mm = pe.matmul(by(LT[f], 4)[:, p % 4, :], pl[n][:, p, :], pb(tt, c)[:, p, :], start=True, stop=True)
                mm.then_inc(ltt_done, 1)

        def v_mask_p(dve, c, n):
            b = LEVELS[n]
            if n > last_level(c):
                return
            for f in range(2):
                dve.wait_ge(lp_done, (c * NL + n) * 2 + f + 1)
                dve.tensor_tensor(halves_of(pl[n][:, FOUR[f], :], b)[0], halves_of(by(LL[f], 4), b)[0],
                                  lmask[n][:, :].rearrange("p (n b) -> p n b", b=b), MUL).then_inc(lp_ready, 1)

        def v_grow(dve, c, n):
            b, last = LEVELS[n], n == last_level(c)
            if n > last_level(c):
                return
            for f in range(2):
                if not last:
                    dst = halves_of(t[:, FOUR[f], :], b)[0]
                    dve.wait_ge(lt_done, (c * (NL - 1) + n) * 2 + f + 1)
                    dve.tensor_tensor(dst, dst, halves_of(by(LL[f], 4), b)[0], ADD).then_inc(lt_ready, 1)
                dst = halves_of(pb(tt, c)[:, FOUR[f], :], b)[1]
                dve.wait_ge(ltt_done, (c * NL + n) * 2 + f + 1)
                dve.tensor_tensor(dst, dst, halves_of(by(LT[f], 4), b)[1], ADD).then_inc(ltt_ready, 1)

        def t_rhs(pe, c):
            sample, a, mc, zc = is_sample(c), pb(ar, c), pb(m, c), pb(zz, c)
            after(pe, st_ready, c * 4)
            after(pe, yn_ready, c)
            for f in range(2):
                if sample:
                    pe.wait_ge(xr_ready, f + 1)
                for p in range(4 * f, 4 * f + 4):
                    for h in range(2):
                        out = by(BB[f], 4)[H2[0], p % 4, H2[h]]
                        if sample:
                            pe.matmul(out, xr[:, p, 0, :], ident[:, H2[h]], start=True, stop=False)
                        else:
                            pe.matmul(out, a[:, p, h, 0, :], st[:, p, :], start=True, stop=False)
                        mm = pe.matmul(out, mc[:, p, h, 0, :], zc[:, p, H2[h]], start=False, stop=True)
                mm.then_inc(x_done, 1)

        def a_rhs(act, c):
            for f in range(2):
                act.wait_ge(x_done, c * 2 + f + 1)
                for h in range(2):
                    nc.scalar.activation(xst[H2[h], FOUR[f], :], by(BB[f], 4)[H2[0], :, H2[h]],
                                         ACT.Copy).then_inc(x_ready, 1)

        def t_u(pe, c):
            for f in range(2):
                pe.wait_ge(x_ready, c * 4 + 2 * f + 2)
                for p in range(4 * f, 4 * f + 4):
                    for h in range(2):
                        mm = pe.matmul(by(BB[f], 4)[H2[0], p % 4, H2[h]], pb(tt, c)[:, p, H2[h]], xst[:, p, :],
                                       start=True, stop=True)
                mm.then_inc(u_done, 1)

        def a_u(act, c):
            for f in range(2):
                act.wait_ge(u_done, c * 2 + f + 1)
                nc.scalar.activation(pb(zz, c)[H2[0], FOUR[f], :], by(BB[f], 4)[H2[0], :, :],
                                     ACT.Copy).then_inc(u_ready, 1)

        def t_y(pe, c):
            a, mc, zc = pb(ar, c), pb(m, c), pb(zz, c)
            pe.wait_ge(u_ready, c * 2 + 2)
            for h in range(2):
                for p in range(PAIRS):
                    out = by(B1, PAIRS)[H2[h], p, :]
                    if not is_sample(c):
                        pe.matmul(out, st[:, p, :], a[:, p, h, 1, :], start=True, stop=False)
                    mm = pe.matmul(out, zc[:, p, H2[h]], mc[:, p, h, 1, :], start=is_sample(c), stop=True)
            mm.then_inc(y_done, 1)

        def t_state(pe, c):
            sample = is_sample(c)
            for b in range(BATCH if sample else 1):
                if sample:
                    pe.wait_ge(zmask_ready, b + 1)
                for f in range(2):
                    if f == 1 and b == 0:
                        pe.wait_ge(y_ready, c + 1)
                    if sample and b > 0:
                        pe.wait_ge(st_ready, (c + b) * 4 - 2 + 2 * f)
                    for p in range(4 * f, 4 * f + 4):
                        mm = pe.matmul(by(BB[f], 4)[:, p % 4, :], pb(bkt, c)[:, p, :],
                                       (zmask[b % 2] if sample else pb(zz, c))[:, p, :], start=True, stop=True)
                    mm.then_inc(s_done, 1)

        def v_decay(dve, c, b=0):
            src = sts[:, b, :, :] if is_sample(c) else st[:, :, :]
            after(dve, st_ready, (c + b) * 4)
            dve.wait_ge(wc_ready, c + 1)
            at_b = b if is_sample(c) else BATCH - 1
            dve.tensor_tensor(stw[:, :, :], src, pb(wc, c)[:, :, at_b:at_b + 1].broadcast_to([P, PAIRS, HEAD]),
                              MUL).then_inc(stw_ready, 1)

        def v_state(dve, c):
            for b in range(BATCH if is_sample(c) else 1):
                dst = sts[:, b, :, :] if is_sample(c) else st[:, :, :]
                if b > 0:
                    v_decay(dve, c, b)
                dve.wait_ge(stw_ready, c + b + 1)
                dve.wait_ge(y_done, c + 1)
                for f in range(2):
                    dve.wait_ge(s_done, (c + b) * 2 + f + 1)
                    for h in range(2):
                        dve.tensor_tensor(dst[H2[h], FOUR[f], :], stw[H2[h], FOUR[f], :],
                                          by(BB[f], 4)[H2[h], :, H2[h]], ADD).then_inc(st_ready, 1)

        def a_y(act, c):
            act.wait_ge(y_done, c + 1)
            after(act, yv_ready, c)
            nc.scalar.activation(y[:, :, :], by(B1, PAIRS), ACT.Copy).then_inc(y_ready, 1)

        def t_mean(pe, c):
            pe.wait_ge(y_ready, c + 1)
            if is_sample(c):
                pe.wait_ge(st_ready, (c + BATCH) * 4)
            else:
                pe.wait_ge(st_ready, c * 4 + 4)
            pe.matmul(bank[B0][:, :], avg[:, :], flat(y[:, :, :]), start=True, stop=True).then_inc(mean_done, 1)

        def v_center(dve, c):
            dve.wait_ge(mean_done, c + 1)
            dve.tensor_tensor(y[:, :, :], y[:, :, :], by(B0, PAIRS), SUB).then_inc(yc_ready, 1)

        def a_ysq(act, c):
            act.wait_ge(yc_ready, c + 1)
            nc.scalar.activation(ysq[:, :, :], y[:, :, :], ACT.Square).then_inc(ysq_ready, 1)

        def t_var(pe, c):
            pe.wait_ge(ysq_ready, c + 1)
            for p in range(PAIRS):
                mm = pe.matmul(bank[B0][0:NH, 0:CH], hsum[:, p, :], ysq[:, p, :], start=(p == 0), stop=(p == PAIRS - 1))
            mm.then_inc(var_done, 1)

        def a_sd(act, c):
            act.wait_ge(var_done, c + 1)
            nc.scalar.activation(sd[:, :], bank[B0][0:NH, 0:CH], ACT.Sqrt, scale=1.0 / HEAD,
                                 bias=eps[0:NH, 0:1]).then_inc(sd_ready, 1)

        def v_rs(dve, c):
            dve.wait_ge(sd_ready, c + 1)
            dve.reciprocal(rs[:, :], sd[:, :]).then_inc(rs_ready, 1)
            dve.wait_ge(rs_ready, c + 1)
            dve.tensor_tensor(rsx[:, :, :], rs[:, :].unsqueeze(1).broadcast_to([NH, PAIRS, CH]),
                              of_pair.unsqueeze(2).broadcast_to([NH, PAIRS, CH]), MUL).then_inc(rsx_ready, 1)

        def t_spread_sd(pe, c):
            pe.wait_ge(rsx_ready, c + 1)
            pe.matmul(bank[B0][:, :], to_head, flat(rsx[:, :, :]), start=True, stop=True).then_inc(rsb_done, 1)

        def v_scale(dve, c):
            dve.wait_ge(rsb_done, c + 1)
            dve.tensor_tensor(y[:, :, :], y[:, :, :], by(B0, PAIRS), MUL).then_inc(yn_ready, 1)

        def p_out(pool, c):
            pool.wait_ge(yn_ready, c + 1)
            pool.tensor_tensor(y[:, :, :], y[:, :, :], lnx_g, MUL).then_inc(yg_ready, 1)
            pool.wait_ge(yg_ready, c + 1)
            pool.wait_ge(bonus_ready, c + 1)
            pool.tensor_tensor(y[:, :, :], y[:, :, :], pb(bonus, c)[:, :, :], ADD).then_inc(yv_ready, 1)
            pool.wait_ge(yv_ready, c + 1)
            after(pool, y_stored, c * 16)
            pool.tensor_tensor(yo[:, :, :], y[:, :, :], pb(gate, c)[:, :, :], MUL).then_inc(yo_ready, 1)

        def a_store(act, c):
            dst = yT[:, :, PROMPT:TOK] if is_sample(c) else yT[:, :, c * CH:(c + 1) * CH] if isinstance(c, int) \
                else yT[:, :, bass.ds(c * CH, CH)]
            act.wait_ge(yo_ready, c + 1)
            act.dma_start(dst.rearrange("n p c -> p n c"), yo[:, :, :]).then_inc(y_stored, 16)

        def t_sample(pe):
            pe.wait_ge(sts_loaded, 16)
            pe.wait_ge(ar_ready, (SMP + 1) * 4)
            pe.wait_ge(bkt_ready, (SMP + 1) * 2)
            for f in range(2):
                for p in range(4 * f, 4 * f + 4):
                    for h in range(2):
                        for b in range(BATCH):
                            e = slice(b * STEPS, (b + 1) * STEPS)
                            out = by(EE[f], 4)[H2[h], p % 4, :].rearrange("p (j c) -> p j c", j=2)[:, :, e]
                            mm = pe.matmul(out, sts[:, b, p, :], pb(ar, SMP)[:, p, h, :, e],
                                           start=True, stop=True)
                mm.then_inc(xr_done, 1)

        def a_sample_x(act):
            for f in range(2):
                act.wait_ge(xr_done, f + 1)
                nc.scalar.activation(pl[2][:, FOUR[f], :], by(EE[f], 4), ACT.Copy).then_inc(xr_ready, 1)

        def v_sample_y(dve):
            dve.wait_ge(y_done, SMP + 1)
            dve.wait_ge(xr_ready, 2)
            dve.wait_ge(yo_ready, SMP)
            dve.tensor_tensor(y[:, :, :], by(B1, PAIRS), xr[:, :, 1, :], ADD).then_inc(y_ready, 1)

        def a_sample(act):
            for b in range(BATCH):
                act.wait_ge(u_ready, (SMP + 1) * 2)
                if b >= 2:
                    act.wait_ge(s_done, (SMP + b - 1) * 2)
                nc.scalar.activation(zmask[b % 2][:, :, :], pb(zz, SMP)[:, :, :], ACT.Copy,
                                     scale=rmask[:, b:b + 1]).then_inc(zmask_ready, 1)

        def scalar_step(act, c, e, d):
            a_values(act, c)
            if d is not None:
                a_rhs(act, d)
                a_u(act, d)
            a_bkt(act, c)
            if d is not None:
                a_y(act, d)
            a_turn(act, c)
            if e is not None:
                scalar_early(act, e)
            if d is not None:
                a_ysq(act, d)
                a_sd(act, d)
                a_store(act, d)

        def scalar_early(act, e):
            a_lowrank(act, e)
            a_sigmoids(act, e)
            a_square(act, e)
            a_gate(act, e)
            a_exps(act, e)
            a_norm(act, e)

        def vector_step(dve, c, e, d):
            v_mask(dve, c)
            v_at(dve, c)
            v_tt(dve, c)
            v_wc(dve, c)
            if d is not None:
                v_decay(dve, d)
            if e is not None:
                v_diff(dve, e)
            v_mask_p(dve, c, 0)
            v_grow(dve, c, 0)
            if e is not None:
                v_mix(dve, e)
                v_bias(dve, e)
            if d is not None:
                v_state(dve, d)
            v_mask_p(dve, c, 1)
            if e is not None:
                v_scan(dve, e)
                v_k(dve, e)
            v_grow(dve, c, 1)
            v_mask_p(dve, c, 2)
            if e is not None:
                v_norm(dve, e)
            if d is not None:
                v_center(dve, d)
            v_grow(dve, c, 2)
            if e is not None:
                v_kk(dve, e)
            v_mask_p(dve, c, 3)
            if e is not None:
                v_ar(dve, e, 0)
            v_grow(dve, c, 3)
            if d is not None:
                v_rs(dve, d)
            v_mask_p(dve, c, 4)
            if e is not None:
                v_ar(dve, e, 1)
            v_grow(dve, c, 4)
            if e is not None:
                v_b(dve, e)
            if d is not None:
                v_scale(dve, d)

        def tensor_step(pe, c, e, d):
            t_values(pe, c)
            if d is not None:
                t_rhs(pe, d)
            t_m(pe, c)
            if d is not None:
                t_u(pe, d)
            t_bkt(pe, c)
            if d is not None:
                t_y(pe, d)
            t_turn(pe, c)
            t_level(pe, c, 0)
            if e is not None:
                t_lowrank(pe, e)
            if d is not None:
                t_state(pe, d)
            t_level(pe, c, 1)
            if e is not None:
                t_sumsq(pe, e)
            if d is not None:
                t_mean(pe, d)
            t_level(pe, c, 2)
            if d is not None:
                t_var(pe, d)
            if e is not None:
                t_spread_norm(pe, e)
                t_bonus(pe, e)
            t_level(pe, c, 3)
            t_level(pe, c, 4)
            if d is not None:
                t_spread_sd(pe, d)

        def pool_step(pool, c, e, d):
            p_mid(pool, c)
            if e is not None:
                p_scale(pool, e)
                p_early(pool, e)
            if d is not None:
                p_out(pool, d)

        def all_steps(engine, step):
            step(engine, 0, 1, None)
            step(engine, 1, 2, 0)
            with engine.Fori(1, (NCHUNK - 2) // 2) as j:
                for odd in range(2):
                    c, e, d = j * 2 + odd, j * 2 + (odd + 1), j * 2 + (odd - 1)
                    par_of.update({id(c): odd, id(e): 1 - odd, id(d): 1 - odd})
                    step(engine, c, e, d)
            for c in (NCHUNK - 2, NCHUNK - 1):
                step(engine, c, c + 1, c - 1)
            step(engine, SMP, None, SMP - 1)

        full = lambda b: b[tuple(slice(None) for _ in b.shape)]
        pool_fills = (lr, v_pad, ar[0], ar[1], at)
        dve_fills = (*pl, st)

        with nc.Block() as block:
            @block.sync
            def _(sp):
                sp.dma_start(mu_sb[:, :], mu).then_inc(mu_loaded, 16)
                sync_load(sp, 0)
                for dst, src in ((par_sb[:, :, :], par), (tab[:, :], table), (lrw[:, :], lowrank),
                                 (lrb[:, :, :], lr_bias)):
                    sp.dma_start(dst, src).then_inc(par_loaded, 16)
                with sp.Fori(1, NCHUNK) as c:
                    sync_load(sp, c)
                sync_load(sp, SMP)
                sp.dma_start(sts[:, :, :, :], stateT).then_inc(sts_loaded, 16)
                sp.wait_ge(shift_ready, 3)
                sp.dma_start(shift_out, sh_out[:, :, :]).then_inc(state_stored, 16)
                sp.wait_ge(st_ready, NCHUNK * 4)
                sp.dma_start(pwkv_out, st[:, :, :]).then_inc(state_stored, 16)
                sp.wait_ge(st_ready, (NCHUNK + BATCH) * 4)
                sp.dma_start(swkv_out, sts[:, :, :, :]).then_inc(state_stored, 16)
                sp.wait_ge(state_stored, 48)
                sp.wait_ge(y_stored, (NCHUNK + 1) * 16)

            @block.gpsimd
            def _(pool):
                pool.memset(eps[:, :], GN_EPS).then_inc(filled, 1)
                for b in pool_fills:
                    pool.memset(full(b), 0.0).then_inc(filled, 1)
                pool.wait_ge(mu_loaded, 16)
                p_scale(pool, 0)
                pool.wait_ge(par_loaded, 64)
                p_early(pool, 0)
                all_steps(pool, pool_step)
                p_out(pool, SMP)

            @block.scalar
            def _(act):
                act.wait_ge(filled, 1 + len(pool_fills))
                scalar_early(act, 0)
                all_steps(act, scalar_step)
                a_sample_x(act)
                a_rhs(act, SMP)
                a_u(act, SMP)
                a_sample(act)
                a_ysq(act, SMP)
                a_sd(act, SMP)
                a_store(act, SMP)

            @block.vector
            def _(dve):
                for b in dve_fills:
                    dve.memset(full(b), 0.0).then_inc(dve_filled, 1)
                dve.wait_ge(dve_filled, len(dve_fills))
                dve.wait_ge(filled, 1 + len(pool_fills))
                dve.wait_ge(mu_loaded, 16)
                v_diff(dve, 0)
                dve.wait_ge(par_loaded, 64)
                v_mix(dve, 0)
                v_bias(dve, 0)
                v_scan(dve, 0)
                v_k(dve, 0)
                v_norm(dve, 0)
                v_kk(dve, 0)
                for h in range(2):
                    v_ar(dve, 0, h)
                v_b(dve, 0)
                all_steps(dve, vector_step)
                dve.wait_ge(sts_loaded, 16)
                v_decay(dve, SMP)
                v_sample_y(dve)
                v_state(dve, SMP)
                v_center(dve, SMP)
                v_rs(dve, SMP)
                v_scale(dve, SMP)

            @block.tensor
            def _(pe):
                pe.wait_ge(par_loaded, 64)
                pe.wait_ge(filled, 1 + len(pool_fills))
                pe.wait_ge(dve_filled, len(dve_fills))
                t_lowrank(pe, 0)
                t_sumsq(pe, 0)
                t_spread_norm(pe, 0)
                t_bonus(pe, 0)
                all_steps(pe, tensor_step)
                t_sample(pe)
                pe.wait_ge(ltt_ready, (SMP * NL + last_level(SMP) + 1) * 2)
                t_rhs(pe, SMP)
                t_u(pe, SMP)
                t_y(pe, SMP)
                t_state(pe, SMP)
                t_mean(pe, SMP)
                t_var(pe, SMP)
                t_spread_sd(pe, SMP)


def phase_sgu(nc, z, wT, bias, ln_par, sT, vn_out):
    with ExitStack() as stack:
        sc = Scope(nc, stack)
        sb, sem = sc.sb, sc.sem
        G = PAIRS
        vn = sb("vn", [P, G, TP])
        sqb = [sb(f"sgu_sq{n}", [P, TP]) for n in range(2)]
        rs = sb("sgu_rs", [P, TP])
        ug, gg = sb("sgu_ug", [P, G, TP]), sb("sgu_gg", [P, G, TP])
        sg = [sb(f"sgu_sg{j}", [P, TP]) for j in range(4)]
        so = [sb(f"sgu_out{j}", [P, TP]) for j in range(2)]
        vt = [sb(f"sgu_vt{j}", [P, 4, Q]) for j in range(2)]
        wm, w8 = sb("sgu_wm", [P, G, Q]), sb("sgu_w8", [SAMPLE, G, SAMPLE])
        bb = sb("sgu_bb", [P, G, Q])
        lnp = sb("sgu_ln", [P, 2, G])
        ones, ident, eps = sb("sgu_ones", [P, P]), sb("sgu_ident", [P, P]), sb("sgu_eps", [P, 1])
        mean, var = sc.ps("sgu_mean", [P, 3, 512]), sc.ps("sgu_var", [P, 3, 512])
        mixed = [sc.ps(f"sgu_mixed{j}", [P, 512]) for j in range(2)]
        turned = [mean[:, j, :] for j in range(2)]

        vg_loaded = [sem(f"vg_loaded{n}") for n in range(G)]
        w_loaded, w8_loaded, w8_zero = sem("sgu_w_loaded"), sem("sgu_w8_loaded"), sem("sgu_w8_zero")
        const0, const_ready, w_ready = sem("sgu_const0"), sem("sgu_const_ready"), sem("sgu_w_ready")
        mean_done, vc_ready, sq_ready, sq_summed = sem("sgu_mean_done"), sem("vc_ready"), sem("sgu_sq_ready"), sem("sgu_sq_summed")
        rt_ready, rs_ready, vs_ready, vn_ready = sem("sgu_rt_ready"), sem("sgu_rs_ready"), sem("vs_ready"), sem("vn_ready")
        turn_done, vt_ready, mix_done, mix_read = sem("turn_done"), sem("vt_ready"), sem("sgu_mix_done"), sem("sgu_mix_read")
        ug_loaded = [sem(f"ug_loaded{j}") for j in range(G)]
        sig_ready, gate_ready, ug_ready = sem("sgu_sig_ready"), sem("sgu_gate_ready"), sem("ug_ready")
        out_ready = sem("sgu_out_ready")
        stored, vn_stored = [sem(f"sgu_stored{j}") for j in range(2)], sem("vn_stored")
        cols = lambda j: slice(j * 512, (j + 1) * 512) if j < 2 else slice(PROMPT, TOK)

        with nc.Block() as block:
            @block.sync
            def _(sp):
                for n in range(G):
                    sp.dma_start(vn[:, n, :], z[T_VG + n, :, ZO:ZW]).then_inc(vg_loaded[n], 16)
                for n in range(G):
                    sp.dma_start(gg[:, n, :], z[T_GG + n, :, ZO:ZW]).then_inc(ug_loaded[n], 16)
                    sp.dma_start(ug[:, n, :], z[T_U + n, :, ZO:ZW]).then_inc(ug_loaded[n], 16)
                for n in range(G):
                    sp.wait_ge(out_ready, 3 * n + 3)
                    sp.dma_start(sT[n, :, 0:TOK], so[n % 2][:, 0:TOK]).then_inc(stored[n % 2], 16)
                sp.wait_ge(vn_ready, G)
                sp.dma_start(vn_out, vn[:, :, PROMPT:TOK]).then_inc(vn_stored, 16)
                for j in range(2):
                    sp.wait_ge(stored[j], G // 2 * 16)
                sp.wait_ge(vn_stored, 16)

            @block.gpsimd
            def _(pool):
                pool.dma_start(wm[:, :, :], wT.rearrange("g s t -> s g t")).then_inc(w_loaded, 16)
                pool.dma_start(bb[:, :, :], bias.unsqueeze(0).broadcast_to([P, G, Q])).then_inc(w_loaded, 16)
                pool.dma_start(lnp[:, :, :], ln_par).then_inc(w_loaded, 16)
                pool.memset(w8[:, :, :], 0.0).then_inc(w8_zero, 1)
                pool.memset(ones[:, :], 1.0 / D_G).then_inc(const_ready, 1)
                pool.memset(eps[:, :], LN_EPS).then_inc(const_ready, 1)
                pool.memset(ident[:, :], 0.0).then_inc(const0, 1)
                pool.wait_ge(const0, 1)
                pool.affine_select(out=ident[:, :], in_=ident[:, :], pattern=[[-1, P]], compare_op=ALU.not_equal,
                                   fill=1.0, base=0, channel_multiplier=1).then_inc(const_ready, 1)
                pool.wait_ge(w8_zero, 1)
                for b in range(BATCH):
                    e = slice(b * STEPS, (b + 1) * STEPS)
                    pool.dma_start(w8[e, :, e], wT[:, 0:STEPS, 0:STEPS].rearrange("g s t -> s g t")).then_inc(w8_loaded, 16)

                def gates(first, end):
                    for n in range(first, end):
                        pool.wait_ge(sig_ready, n + 1)
                        pool.tensor_tensor(gg[:, n, :], gg[:, n, :], sg[n % 4][:, :], MUL).then_inc(gate_ready, 1)
                        pool.wait_ge(gate_ready, n + 1)
                        pool.tensor_tensor(ug[:, n, :], ug[:, n, :], gg[:, n, :], MUL).then_inc(ug_ready, 1)

                gates(0, G // 2)
                pool.wait_ge(w_loaded, 48)
                pool.wait_ge(const_ready, 3)
                pool.affine_select(out=wm[:, :, :], in_=wm[:, :, :], pattern=[[0, G], [1, Q]], compare_op=ALU.is_ge,
                                   fill=0.0, base=0, channel_multiplier=-1).then_inc(w_ready, 1)
                pool.wait_ge(w8_loaded, 16 * BATCH)
                pool.wait_ge(w_ready, 1)
                pool.affine_select(out=w8[:, :, :], in_=w8[:, :, :], pattern=[[0, G], [1, SAMPLE]], compare_op=ALU.is_ge,
                                   fill=0.0, base=0, channel_multiplier=-1).then_inc(w_ready, 1)
                gates(G // 2, G)

            @block.scalar
            def _(act):
                def sigmoid(n):
                    act.wait_ge(ug_loaded[n], 32)
                    if n >= 4:
                        act.wait_ge(gate_ready, n - 3)
                    nc.scalar.activation(sg[n % 4][:, :], gg[:, n, :], ACT.Sigmoid).then_inc(sig_ready, 1)

                for n in range(4):
                    sigmoid(n)
                for n in range(G):
                    act.wait_ge(vc_ready, n + 1)
                    if n >= 2:
                        act.wait_ge(sq_summed, n - 1)
                    nc.scalar.activation(sqb[n % 2][:, :], vn[:, n, :], ACT.Square).then_inc(sq_ready, 1)
                    if n % 2:
                        sigmoid(4 + n // 2)
                act.wait_ge(sq_summed, G)
                act.wait_ge(const_ready, 3)
                nc.scalar.activation(pieces(rs[:, :]), var[:, :, 0:NCH], ACT.Sqrt, bias=eps[:, 0:1]).then_inc(rt_ready, 1)
                act.wait_ge(w_loaded, 48)

                def scale(n):
                    act.wait_ge(vs_ready, n + 1)
                    nc.scalar.activation(vn[:, n, :], vn[:, n, :], ACT.Identity, scale=lnp[:, 0, n:n + 1],
                                         bias=lnp[:, 1, n:n + 1]).then_inc(vn_ready, 1)

                scale(0)
                for n in range(G):
                    if n + 1 < G:
                        scale(n + 1)
                    for j in range(3):
                        e = 3 * n + j
                        act.wait_ge(turn_done, e + 1)
                        if e >= 2:
                            act.wait_ge(mix_done, e - 1)
                        if j < 2:
                            nc.scalar.activation(vt[e % 2][:, :, :].rearrange("p c t -> p (c t)"), turned[e % 2],
                                                 ACT.Copy).then_inc(vt_ready, 1)
                        else:
                            nc.scalar.activation(vt[e % 2][0:SAMPLE, 0, :], turned[e % 2][0:SAMPLE, 0:P],
                                                 ACT.Copy).then_inc(vt_ready, 1)

            @block.vector
            def _(dve):
                dve.wait_ge(mean_done, 1)
                for n in range(G):
                    dve.tensor_tensor(pieces(vn[:, n, :]), pieces(vn[:, n, :]), mean[:, :, 0:NCH], SUB).then_inc(vc_ready, 1)
                dve.wait_ge(rt_ready, 1)
                dve.reciprocal(rs[:, :], rs[:, :]).then_inc(rs_ready, 1)
                dve.wait_ge(rs_ready, 1)
                for n in range(G):
                    dve.tensor_tensor(vn[:, n, :], vn[:, n, :], rs[:, :], MUL).then_inc(vs_ready, 1)
                for n in range(G):
                    dve.wait_ge(ug_ready, n + 1)
                    if n >= 2:
                        dve.wait_ge(stored[n % 2], n // 2 * 16)
                    for j in range(3):
                        e = 3 * n + j
                        dst, src = so[n % 2][:, cols(j)], mixed[e % 2][:, :]
                        dve.wait_ge(mix_done, e + 1)
                        if j < 2:
                            dst4 = dst.rearrange("p (c t) -> p c t", t=Q)
                            dve.tensor_tensor(dst4, src.rearrange("p (c t) -> p c t", t=Q),
                                              bb[:, n, :].unsqueeze(1).broadcast_to([P, 4, Q]), ADD).then_inc(mix_read, 1)
                        else:
                            dst4 = dst.rearrange("p (c t) -> p c t", t=STEPS)
                            dve.tensor_tensor(dst4, src[:, 0:SAMPLE].rearrange("p (c t) -> p c t", t=STEPS),
                                              bb[:, n, 0:STEPS].unsqueeze(1).broadcast_to([P, BATCH, STEPS]),
                                              ADD).then_inc(mix_read, 1)
                        dve.wait_ge(mix_read, e + 1)
                        dve.tensor_tensor(dst, dst, ug[:, n, cols(j)], MUL).then_inc(out_ready, 1)

            @block.tensor
            def _(pe):
                pe.wait_ge(const_ready, 3)
                for n in range(G):
                    pe.wait_ge(vg_loaded[n], 16)
                    for c in range(3):
                        mm = pe.matmul(mean[:, c, 0:NCH], ones[:, :], vn[:, n, c * NCH:(c + 1) * NCH],
                                       start=(n == 0), stop=(n == G - 1))
                mm.then_inc(mean_done, 1)
                for n in range(G):
                    pe.wait_ge(sq_ready, n + 1)
                    for c in range(3):
                        mm = pe.matmul(var[:, c, 0:NCH], ones[:, :], sqb[n % 2][:, c * NCH:(c + 1) * NCH],
                                       start=(n == 0), stop=(n == G - 1))
                    mm.then_inc(sq_summed, 1)
                pe.wait_ge(w_ready, 2)

                def turn(e):
                    n, j = e // 3, e % 3
                    pe.wait_ge(vn_ready, n + 1)
                    if e >= 2:
                        pe.wait_ge(vt_ready, e - 1)
                    if j < 2:
                        for c in range(4):
                            o = j * 512 + c * Q
                            mm = pe.transpose(turned[e % 2][:, c * Q:(c + 1) * Q], vn[:, n, o:o + Q], ident[:, :])
                    else:
                        mm = pe.transpose(turned[e % 2][0:SAMPLE, 0:P], vn[:, n, PROMPT:TOK], ident[:, :])
                    mm.then_inc(turn_done, 1)

                turn(0)
                for e in range(3 * G):
                    n, j = e // 3, e % 3
                    if e + 1 < 3 * G:
                        turn(e + 1)
                    pe.wait_ge(vt_ready, e + 1)
                    if e >= 2:
                        pe.wait_ge(mix_read, e - 1)
                    if j < 2:
                        for c in range(4):
                            mm = pe.matmul(mixed[e % 2][:, c * Q:(c + 1) * Q], vt[e % 2][:, c, :], wm[:, n, :],
                                           start=True, stop=True)
                    else:
                        mm = pe.matmul(mixed[e % 2][:, 0:SAMPLE], vt[e % 2][0:SAMPLE, 0, :], w8[:, n, :],
                                       start=True, stop=True)
                    mm.then_inc(mix_done, 1)


class Operand:

    def __init__(self, nc, sc, tag, tiles, xh, xl, gm, ring):
        self.nc, self.tiles, self.xh, self.xl, self.gm = nc, tiles, xh, xl, gm
        self.ring = [sc.sb(f"{tag}_xs{n}", [P, TP]) for n in range(ring)]
        self.loaded = [sc.sem(f"{tag}_x_loaded{n}") for n in range(ring)]
        self.xh_ready, self.pad_ready = sc.sem(f"{tag}_xh_ready"), sc.sem(f"{tag}_pad_ready")

    def feed(self, act):
        r, tiles = len(self.ring), self.tiles

        def load(n):
            act.dma_start(self.ring[n % r][:, 0:TOK], tiles[n]).then_inc(self.loaded[n % r], 16)

        for n in range(r):
            load(n)
        act.wait_ge(self.pad_ready, r)
        for n in range(len(tiles)):
            act.wait_ge(self.loaded[n % r], 16 * (n // r + 1))
            self.nc.scalar.activation(self.xh[:, n, :], self.ring[n % r][:, :], ACT.Copy).then_inc(self.xh_ready, 1)
            if 1 <= n <= len(tiles) - r:
                act.wait_ge(self.gm.x_ready, n)
                load(n - 1 + r)

    def pad(self, engine):
        for b in self.ring:
            engine.memset(b[:, TOK:TP], 0.0).then_inc(self.pad_ready, 1)

    def split(self, dve, first, end):
        for n in range(first, end):
            dve.wait_ge(self.xh_ready, n + 1)
            dve.tensor_tensor(self.xl[:, n, :], self.ring[n % len(self.ring)][:, :], self.xh[:, n, :].bitcast(F32),
                              SUB).then_inc(self.gm.x_ready, 1)


def phase_merge(nc, z, yT, sT, wt, mT):
    with ExitStack() as stack:
        sc = Scope(nc, stack)
        xh, xl = sc.sb("mg_xh", [P, KT, TP], F32R), sc.sb("mg_xl", [P, KT, TP], F32R)
        gm = Gemm(nc, sc, "mg", wt, KH, xh, xl, (0, KH))
        op = Operand(nc, sc, "mg", [d[n, :, 0:TOK] for d in (yT, sT) for n in range(KH)], xh, xl, gm, 4)
        gate = [sc.sb(f"mg_gate{s}", [P, TP]) for s in range(2)]
        part = [sc.sb(f"mg_part{s}", [P, TP]) for s in range(2)]
        mo = sc.sb("mg_out", [P, TP])
        gate_loaded = [sc.sem(f"mg_gate_loaded{s}") for s in range(2)]
        sig_ready, m_ready, stored = sc.sem("mg_sig_ready"), sc.sem("mg_m_ready"), sc.sem("mg_m_stored")

        with nc.Block() as block:
            @block.sync
            def _(sp):
                def load(g, i, s):
                    gm.load(sp, g, i, s)
                    sp.wait_ge(gm.evacuated[s], i)
                    sp.dma_start(gate[s][:, :], tile_of(z, i + (T_GA, T_GB)[s])[:, ZO:ZW]).then_inc(gate_loaded[s], 16)

                in_slots(sp, 2 * KT, load)

            @block.scalar
            def _(act):
                op.feed(act)

                def step(g, i, s):
                    act.wait_ge(gate_loaded[s], i * 16 + 16)
                    nc.scalar.activation(gate[s][:, :], gate[s][:, :], ACT.Sigmoid).then_inc(sig_ready, 1)
                    if s == 1:
                        act.wait_ge(m_ready, i + 1)
                        act.dma_start(tile_of(mT, i), mo[:, :]).then_inc(stored, 16)

                in_slots(act, 2 * KT, step)
                act.wait_ge(stored, KT * 16)

            @block.gpsimd
            def _(pool):
                op.pad(pool)

            @block.vector
            def _(dve):
                for s in range(2):
                    gm.split(dve, 0, s)
                    op.split(dve, s * KH, s * KH + KH)

                def evacuate(g, i, s):
                    dve.wait_ge(gm.group_done[s], i + 1)
                    dve.wait_ge(sig_ready, g + 1)
                    dve.wait_ge(m_ready, i)
                    dve.tensor_tensor(pieces(part[s][:, :]), gm.sums(s), pieces(gate[s][:, :]),
                                      MUL).then_inc(gm.evacuated[s], 1)
                    if s == 1:
                        for n in range(2):
                            dve.wait_ge(gm.evacuated[n], i + 1)
                        dve.wait_ge(stored, i * 16)
                        dve.tensor_tensor(mo[:, :], part[0][:, :], part[1][:, :], ADD).then_inc(m_ready, 1)

                evacuate_and_split(dve, gm, 2 * KT, evacuate)

            @block.tensor
            def _(pe):
                in_slots(pe, 2 * KT, lambda g, i, s: gm.products(pe, i, s))


def phase_out(nc, xT, mT, wt, hT, ssq_dram):
    with ExitStack() as stack:
        sc = Scope(nc, stack)
        xh, xl = sc.sb("out_xh", [P, KT, TP], F32R), sc.sb("out_xl", [P, KT, TP], F32R)
        gm = Gemm(nc, sc, "out", wt, KT, xh, xl, (0, 0))
        op = Operand(nc, sc, "out", [mT[n, :, 0:TOK] for n in range(KT)], xh, xl, gm, 4)
        xr, h, sq = op.ring[0:3]
        ssq = sc.sb("out_ssq", [P, TP])
        x_loaded, sq_ready = sc.sem("out_xr_loaded"), sc.sem("out_sq_ready")
        ssq_ready, stored, ssq_stored = sc.sem("ssq_ready"), sc.sem("h_stored"), sc.sem("ssq_stored")

        with nc.Block() as block:
            @block.sync
            def _(sp):
                in_slots(sp, KT, lambda g, i, s: gm.load(sp, g, i, s))

            @block.scalar
            def _(act):
                op.feed(act)
                act.wait_ge(gm.x_ready, KT)

                def step(g, i, s):
                    after(act, gm.evacuated[1 - s], i + s)
                    act.dma_start(xr[:, 0:TOK], tile_of(xT, g)).then_inc(x_loaded, 16)
                    act.wait_ge(gm.evacuated[s], i + 1)
                    act.wait_ge(ssq_ready, g + 1)
                    nc.scalar.activation(sq[:, :], h[:, :], ACT.Square).then_inc(sq_ready, 1)
                    act.dma_start(tile_of(hT, g), h[:, :]).then_inc(stored, 16)

                in_slots(act, KT, step)
                act.wait_ge(ssq_ready, KT + 1)
                act.dma_start(ssq_dram, ssq[:, :]).then_inc(ssq_stored, 16)
                act.wait_ge(stored, KT * 16)
                act.wait_ge(ssq_stored, 16)

            @block.gpsimd
            def _(pool):
                op.pad(pool)
                pool.memset(ssq[:, :], 0.0).then_inc(ssq_ready, 1)

                def step(g, i, s):
                    pool.wait_ge(sq_ready, g + 1)
                    pool.wait_ge(ssq_ready, g + 1)
                    pool.tensor_tensor(ssq[:, :], ssq[:, :], sq[:, :], ADD).then_inc(ssq_ready, 1)

                in_slots(pool, KT, step)

            @block.vector
            def _(dve):
                gm.split(dve, 0, 0)
                op.split(dve, 0, KT)
                gm.split(dve, 0, 1)

                def evacuate(g, i, s):
                    dve.wait_ge(gm.group_done[s], i + 1)
                    dve.wait_ge(x_loaded, g * 16 + 16)
                    dve.wait_ge(stored, g * 16)
                    dve.wait_ge(sq_ready, g)
                    dve.tensor_tensor(pieces(h[:, :]), gm.sums(s), pieces(xr[:, :]), ADD).then_inc(gm.evacuated[s], 1)

                evacuate_and_split(dve, gm, KT, evacuate)

            @block.tensor
            def _(pe):
                in_slots(pe, KT, lambda g, i, s: gm.products(pe, i, s))


def phase_final(nc, hT, ssq_dram, final_g, outT):
    with ExitStack() as stack:
        sc = Scope(nc, stack)
        h = sc.sb("fin_h", [P, KT, TP])
        o = [sc.sb(f"fin_o{n}", [P, TP]) for n in range(4)]
        ssq, rs = sc.sb("fin_ssq", [P, TP]), sc.sb("fin_rs", [P, TP])
        g_sb, eps, ones = sc.sb("fin_g", [P, KT]), sc.sb("fin_eps", [P, 1]), sc.sb("fin_ones", [P, P])
        ms = sc.ps("fin_ms", [P, 3, 512])
        h_loaded = [sc.sem(f"fin_h_loaded{n}") for n in range(KT)]
        ssq_loaded, const_ready, ms_done = sc.sem("fin_ssq_loaded"), sc.sem("fin_const_ready"), sc.sem("fin_ms_done")
        rt_ready, rs_ready, o_ready = sc.sem("fin_rt_ready"), sc.sem("fin_rs_ready"), sc.sem("fin_o_ready")
        stored = [sc.sem(f"fin_stored{n}") for n in range(4)]

        with nc.Block() as block:
            @block.sync
            def _(sp):
                sp.dma_start(ssq[:, :], ssq_dram).then_inc(ssq_loaded, 16)
                sp.dma_start(g_sb[:, :], final_g).then_inc(ssq_loaded, 16)
                for n in range(KT):
                    sp.dma_start(h[:, n, :], hT[n]).then_inc(h_loaded[n], 16)

            @block.gpsimd
            def _(pool):
                pool.memset(ones[:, :], 1.0 / D_MODEL).then_inc(const_ready, 1)
                pool.memset(eps[:, :], RMS_EPS).then_inc(const_ready, 1)

            @block.tensor
            def _(pe):
                pe.wait_ge(const_ready, 2)
                pe.wait_ge(ssq_loaded, 32)
                for c in range(3):
                    mm = pe.matmul(ms[:, c, 0:NCH], ones[:, :], ssq[:, c * NCH:(c + 1) * NCH], start=True, stop=True)
                mm.then_inc(ms_done, 1)

            @block.scalar
            def _(act):
                act.wait_ge(const_ready, 2)
                act.wait_ge(ms_done, 1)
                nc.scalar.activation(pieces(rs[:, :]), ms[:, :, 0:NCH], ACT.Sqrt, bias=eps[:, 0:1]).then_inc(rt_ready, 1)
                for n in range(KT):
                    act.wait_ge(o_ready, n + 1)
                    act.dma_start(outT[n], o[n % 4][:, 0:TOK]).then_inc(stored[n % 4], 16)
                for s in stored:
                    act.wait_ge(s, KT // 4 * 16)

            @block.vector
            def _(dve):
                dve.wait_ge(rt_ready, 1)
                dve.reciprocal(rs[:, :], rs[:, :]).then_inc(rs_ready, 1)
                dve.wait_ge(rs_ready, 1)
                dve.wait_ge(ssq_loaded, 32)
                for n in range(KT):
                    dve.wait_ge(h_loaded[n], 16)
                    if n >= 4:
                        dve.wait_ge(stored[n % 4], n // 4 * 16)
                    dve.scalar_tensor_tensor(o[n % 4][:, :], h[:, n, :], g_sb[:, n:n + 1], rs[:, :], MUL,
                                             MUL).then_inc(o_ready, 1)


OUTPUTS = {
    "outT": (KT, P, TOK), "shift_out": (P, N_SHIFT, 1 + BATCH), "pwkv_out": (P, PAIRS, HEAD),
    "swkv_out": (P, BATCH, PAIRS, HEAD), "vn_out": (P, PAIRS, SAMPLE),
}


def program(nc, a):
    scratch = lambda name, shape: nc.dram_tensor(name, shape, F32, kind="Internal").ap()
    z = scratch("z", (NTILE, P, ZW))
    yT, sT = scratch("yT", (PAIRS, P, TP)), scratch("sT", (PAIRS, P, TP))
    mT, hT, ssq = scratch("mT", (KT, P, TP)), scratch("hT", (KT, P, TP)), scratch("ssq", (P, TP))
    phase_in(nc, a["xT"], a["norm_g"], a["w_in"], z)
    phase_rwkv(nc, z, a["lowrank"], a["lr_bias"], a["mu"], a["par"], a["tables"], a["shiftT"],
               a["stateT"], yT, a["shift_out"], a["swkv_out"], a["pwkv_out"])
    phase_sgu(nc, z, a["sgu_wT"], a["sgu_b"], a["ln_par"], sT, a["vn_out"])
    phase_merge(nc, z, yT, sT, a["w_proj"], mT)
    phase_out(nc, a["xT"], mT, a["w_out"], hT, ssq)
    phase_final(nc, hT, ssq, a["final_g"], a["outT"])


def layouts(inputs):
    import numpy as np
    x = {n: np.asarray(a) for n, a in inputs.items()}
    rows = lambda a: np.ascontiguousarray(a.reshape(-1, P).T)
    tok = np.concatenate([x["x_prompt"].reshape(PROMPT, D_MODEL), x["x_sample"].reshape(SAMPLE, D_MODEL)])
    tiles = lambda w: w.reshape(w.shape[0] // P, P, -1, P).transpose(2, 1, 0, 3).reshape(w.shape[1] // P, P, -1)
    out = {
        "xT": tok.T.reshape(KT, P, TOK),
        "norm_g": rows(x["norm_g"][0]),
        "w_in": tiles(x["w_in"][0]),
        "lowrank": np.concatenate([x["w2"][0], x["a2"][0]]),
        "lr_bias": np.stack([rows(x["w0"][0]), rows(x["a0"][0])], 1),
        "mu": rows(x["shift_mu"][0]),
        "par": np.stack([rows(x[n].reshape(-1)) for n in ("k_k", "k_a", "r_k", "lnx_g", "lnx_b")], 1),
        "tables": tables(),
        "shiftT": x["state_shift"].reshape(BATCH, N_SHIFT, P).transpose(2, 1, 0),
        "stateT": x["state_wkv"].reshape(BATCH, PAIRS, 2, HEAD, HEAD).transpose(2, 4, 0, 1, 3).reshape(
            P, BATCH, PAIRS, HEAD),
        "sgu_wT": x["sgu_w"][0].transpose(0, 2, 1),
        "sgu_b": x["sgu_b"][0],
        "ln_par": np.stack([rows(x[n][0]) for n in ("sgu_ln_g", "sgu_ln_b")], 1),
        "w_proj": np.stack([tiles(x["w_proj_a"][0]), tiles(x["w_proj_b"][0])], 1).reshape(2 * KT, P, KH * P),
        "w_out": tiles(x["w_out"][0]),
        "final_g": rows(x["final_norm_g"]),
    }
    return {n: np.ascontiguousarray(a) for n, a in out.items()}


def kernel(**inputs):
    import numpy as np
    import concourse.bacc as bacc
    from concourse.bass_utils import run_bass_kernel_spmd

    nc = bacc.Bacc("TRN2", target_bir_lowering=False, num_devices=1)
    arrays = {f"in_{n}": a for n, a in layouts(inputs).items()}
    aps = {n[3:]: nc.dram_tensor(n, a.shape, mybir.dt.from_np(a.dtype), kind="ExternalInput").ap()
           for n, a in arrays.items()}
    for n, shape in OUTPUTS.items():
        aps[n] = nc.dram_tensor(n, shape, F32, kind="ExternalOutput").ap()
    program(nc, aps)
    got = run_bass_kernel_spmd(nc, [arrays], core_ids=[0]).results[0]

    tok = got["outT"].reshape(D_MODEL, TOK).T
    shift = got["shift_out"].transpose(2, 1, 0).reshape(1 + BATCH, N_SHIFT * P)
    pwkv = got["pwkv_out"].reshape(2, HEAD, PAIRS, HEAD).transpose(2, 0, 3, 1).reshape(1, 1, 2 * PAIRS, HEAD, HEAD)
    swkv = got["swkv_out"].reshape(2, HEAD, BATCH, PAIRS, HEAD).transpose(2, 3, 0, 4, 1).reshape(
        1, BATCH, 2 * PAIRS, HEAD, HEAD)
    vn = got["vn_out"].transpose(2, 1, 0).reshape(1, BATCH, STEPS, D_G)
    back = np.ascontiguousarray
    return (back(tok[:PROMPT]).reshape(1, PROMPT, D_MODEL), back(tok[PROMPT:]).reshape(BATCH, STEPS, D_MODEL),
            back(pwkv), back(shift[0:1]).reshape(1, 1, 1, -1), back(swkv), back(shift[1:]).reshape(1, BATCH, 1, -1),
            back(vn))
```
